# Optimizing a Trainium2 kernel written in Bass

```python
import math
import jax, jax.numpy as jnp
from jax import lax
import numpy as np

D_MODEL = 1024
BATCH = 1
SEQ = 512
DEPTH = 2

N_EVEN = (DEPTH + 1) // 2
N_ODD = DEPTH // 2

M_WIDTH = D_MODEL // 2
M_HEADS = 4
M_HEAD_DIM = M_WIDTH // M_HEADS
M_CONV = 4
QKV_BLOCK = 4
M_CHUNK = 64
S_WIDTH = D_MODEL // 2
S_GROUP = 16
S_GROUPS = S_WIDTH // S_GROUP
S_STATE = 64
DT_MIN = 1e-3
DT_MAX = 1e-1
IN_EVEN = 2 * M_WIDTH + S_WIDTH
MIX_EVEN = M_WIDTH + S_WIDTH
H_EXPAND = 128
H_HEADS = D_MODEL // H_EXPAND
H_WIDTH = H_HEADS * H_EXPAND
H_CHUNK = 64
IN_ODD = 4 * H_WIDTH
D_FF = -(-8 * D_MODEL // (3 * 256)) * 256
EPS = 1e-6


def rmsnorm(x, g):
    xf = x.astype(jnp.float32)
    return xf * lax.rsqrt(jnp.mean(xf * xf, axis=-1, keepdims=True) + EPS) * g

def causal_dwconv(x, w, b):
    K, Cc = w.shape
    y = lax.conv_general_dilated(x, w[:, None, :].astype(x.dtype), window_strides=(1,), padding=[(K - 1, 0)],
                                 dimension_numbers=('NWC', 'WIO', 'NWC'), feature_group_count=Cc)
    return y + b

def swiglu(x, w1, w3, w2):
    return (jax.nn.silu(x @ w1) * (x @ w3)) @ w2

def mlstm_chunkwise(q, k, v, i_pre, f_pre):
    f32 = jnp.float32
    Bsz, H, L, Dh = q.shape
    C = M_CHUNK
    NC = L // C
    q, k, v = (t.astype(f32).reshape(Bsz, H, NC, C, Dh) for t in (q, k, v))
    log_f = jax.nn.log_sigmoid(f_pre.astype(f32)).reshape(Bsz, H, NC, C)
    log_i = i_pre.astype(f32).reshape(Bsz, H, NC, C)
    b = jnp.cumsum(log_f, axis=-1)
    b_last = b[..., -1]
    causal = jnp.tril(jnp.ones((C, C), dtype=bool))
    d_log = jnp.where(causal, b[..., :, None] - b[..., None, :] + log_i[..., None, :], -jnp.inf)
    m_intra = jnp.max(d_log, axis=-1)
    a = b_last[..., None] - b + log_i
    a_max = jnp.max(a, axis=-1)
    kw = k * jnp.exp(a - a_max[..., None])[..., None]
    U = jnp.einsum('bhcsk,bhcsv->bhckv', kw, v)
    un = jnp.sum(kw, axis=-2)

    def step(carry, inp):
        c_st, n_st, m_st = carry
        u_c, un_c, am_c, bl_c = inp
        m_new = jnp.maximum(bl_c + m_st, am_c)
        s_old = jnp.exp(bl_c + m_st - m_new)
        s_new = jnp.exp(am_c - m_new)
        c_new = s_old[..., None, None] * c_st + s_new[..., None, None] * u_c
        n_new = s_old[..., None] * n_st + s_new[..., None] * un_c
        return (c_new, n_new, m_new), (c_st, n_st, m_st)

    init = (jnp.zeros((Bsz, H, Dh, Dh), f32), jnp.zeros((Bsz, H, Dh), f32), jnp.zeros((Bsz, H), f32))
    xs = (jnp.moveaxis(U, 2, 0), jnp.moveaxis(un, 2, 0), jnp.moveaxis(a_max, 2, 0), jnp.moveaxis(b_last, 2, 0))
    _, (c_prev, n_prev, m_prev) = lax.scan(step, init, xs)
    c_prev = jnp.moveaxis(c_prev, 0, 2)
    n_prev = jnp.moveaxis(n_prev, 0, 2)
    m_prev = jnp.moveaxis(m_prev, 0, 2)
    inter_log = b + m_prev[..., None]
    m_t = jnp.maximum(inter_log, m_intra)
    s_inter = jnp.exp(inter_log - m_t)
    scores = jnp.einsum('bhctd,bhcsd->bhcts', q, k) * jnp.exp(d_log - m_t[..., None])
    num = jnp.einsum('bhcts,bhcsv->bhctv', scores, v) + s_inter[..., None] * jnp.einsum('bhctk,bhckv->bhctv', q, c_prev)
    den = jnp.sum(scores, axis=-1) + s_inter * jnp.einsum('bhctk,bhck->bhct', q, n_prev)
    h = num / jnp.maximum(jnp.abs(den), jnp.exp(-m_t))[..., None]
    return h.reshape(Bsz, H, L, Dh)

def _complex_affine_combine(e1, e2):
    a1r, a1i, b1r, b1i = e1
    a2r, a2i, b2r, b2i = e2
    return (a2r * a1r - a2i * a1i, a2r * a1i + a2i * a1r,
            a2r * b1r - a2i * b1i + b2r, a2r * b1i + a2i * b1r + b2i)

def s5_ssm(u, a_re, a_im, log_dt, b_re, b_im, c_re, c_im, d_skip):
    f32 = jnp.float32
    Bsz, L, _ = u.shape
    ug = u.astype(f32).reshape(Bsz, L, S_GROUPS, S_GROUP)
    a_re, a_im, b_re, b_im, c_re, c_im = (t.astype(f32) for t in (a_re, a_im, b_re, b_im, c_re, c_im))
    dt = jnp.exp(log_dt.astype(f32))[:, None]
    mag = jnp.exp(a_re * dt)
    ab_re = mag * jnp.cos(a_im * dt)
    ab_im = mag * jnp.sin(a_im * dt)
    inv = 1.0 / (a_re * a_re + a_im * a_im)
    g_re = ((ab_re - 1.0) * a_re + ab_im * a_im) * inv
    g_im = (ab_im * a_re - (ab_re - 1.0) * a_im) * inv
    bb_re = g_re[..., None] * b_re - g_im[..., None] * b_im
    bb_im = g_re[..., None] * b_im + g_im[..., None] * b_re
    bu_re = jnp.einsum('blgp,gnp->blgn', ug, bb_re)
    bu_im = jnp.einsum('blgp,gnp->blgn', ug, bb_im)
    shp = (1, L, S_GROUPS, S_STATE)
    a_seq_re = jnp.broadcast_to(ab_re, shp)
    a_seq_im = jnp.broadcast_to(ab_im, shp)
    _, _, x_re, x_im = lax.associative_scan(_complex_affine_combine, (a_seq_re, a_seq_im, bu_re, bu_im), axis=1)
    y = jnp.einsum('blgn,gpn->blgp', x_re, c_re) - jnp.einsum('blgn,gpn->blgp', x_im, c_im)
    y = y + d_skip.astype(f32).reshape(S_GROUPS, S_GROUP) * ug
    return y.reshape(Bsz, L, S_WIDTH)

def mixer_ab(x, w_in, conv_w, conv_b, wq, wk, wv, w_if, b_if, mh_gain, skip,
             a_re, a_im, log_dt, b_re, b_im, c_re, c_im, d_skip, w_glu, b_glu, w_out):
    Bsz, L, _ = x.shape
    proj = x @ w_in
    xm = proj[..., :M_WIDTH]
    zm = proj[..., M_WIDTH:2 * M_WIDTH]
    us = proj[..., 2 * M_WIDTH:]
    xc = jax.nn.silu(causal_dwconv(xm, conv_w, conv_b))
    nb = M_WIDTH // QKV_BLOCK
    xc_b = xc.reshape(Bsz, L, nb, QKV_BLOCK)
    xm_b = xm.reshape(Bsz, L, nb, QKV_BLOCK)
    q = jnp.einsum('blnd,nde->blne', xc_b, wq).reshape(Bsz, L, M_WIDTH)
    k = jnp.einsum('blnd,nde->blne', xc_b, wk).reshape(Bsz, L, M_WIDTH) * (M_HEAD_DIM ** -0.5)
    v = jnp.einsum('blnd,nde->blne', xm_b, wv).reshape(Bsz, L, M_WIDTH)
    gates = jnp.concatenate([q, k, v], axis=-1) @ w_if + b_if
    to_h = lambda t: t.reshape(Bsz, L, M_HEADS, M_HEAD_DIM).transpose(0, 2, 1, 3)
    h = mlstm_chunkwise(to_h(q), to_h(k), to_h(v),
                        gates[..., :M_HEADS].transpose(0, 2, 1), gates[..., M_HEADS:].transpose(0, 2, 1))
    mu = jnp.mean(h, axis=-1, keepdims=True)
    var = jnp.mean(jnp.square(h - mu), axis=-1, keepdims=True)
    hn = ((h - mu) * lax.rsqrt(var + EPS)).transpose(0, 2, 1, 3).reshape(Bsz, L, M_WIDTH) * mh_gain
    out_m = (hn + skip * xc) * jax.nn.silu(zm)
    y = jax.nn.gelu(s5_ssm(us, a_re, a_im, log_dt, b_re, b_im, c_re, c_im, d_skip))
    out_s = y * jax.nn.sigmoid(y @ w_glu + b_glu)
    return jnp.concatenate([out_m, out_s], axis=-1) @ w_out

def hgrn2_chunkwise(q, k, v, log_f):
    f32 = jnp.float32
    Bsz, H, L, E = q.shape
    C = H_CHUNK
    NC = L // C
    q, k, v, log_f = (t.astype(f32).reshape(Bsz, H, NC, C, E) for t in (q, k, v, log_f))
    b = jnp.cumsum(log_f, axis=3)
    b_last = b[:, :, :, -1:, :]
    q_inter = q * jnp.exp(b)
    k_state = k * jnp.exp(b_last - b)
    q_intra = q * jnp.exp(b - b_last)
    causal = jnp.tril(jnp.ones((C, C), dtype=bool))
    scores = jnp.where(causal, jnp.einsum('bhctk,bhcsk->bhcts', q_intra, k_state), 0.0)
    intra = jnp.einsum('bhcts,bhcsv->bhctv', scores, v)
    U = jnp.einsum('bhcsk,bhcsv->bhckv', k_state, v)
    decay = jnp.exp(b_last[:, :, :, 0, :])

    def step(s, inp):
        u_c, d_c = inp
        return d_c[..., None] * s + u_c, s

    _, s_prev = lax.scan(step, jnp.zeros((Bsz, H, E, E), f32), (jnp.moveaxis(U, 2, 0), jnp.moveaxis(decay, 2, 0)))
    s_prev = jnp.moveaxis(s_prev, 0, 2)
    inter = jnp.einsum('bhctk,bhckv->bhctv', q_inter, s_prev)
    return (intra + inter).reshape(Bsz, H, L, E)

def mixer_c(x, layer_idx, w_in, lb_raw, g_gain, w_out):
    Bsz, L, _ = x.shape
    proj = x @ w_in
    q = jax.nn.silu(proj[..., :H_WIDTH])
    f = proj[..., H_WIDTH:2 * H_WIDTH].astype(jnp.float32)
    i = proj[..., 2 * H_WIDTH:3 * H_WIDTH]
    g = proj[..., 3 * H_WIDTH:]
    lbs = jnp.cumsum(jax.nn.softmax(lb_raw.astype(jnp.float32), axis=0), axis=0)
    lb = lbs[layer_idx] - lbs[0]
    fg = lb + (1.0 - lb) * jax.nn.sigmoid(f)
    to_h = lambda t: t.reshape(Bsz, L, H_HEADS, H_EXPAND).transpose(0, 2, 1, 3)
    o = hgrn2_chunkwise(to_h(q), to_h(1.0 - fg), to_h(i), to_h(jnp.log(fg)))
    o = o * lax.rsqrt(jnp.mean(o * o, axis=-1, keepdims=True) + EPS)
    o = o.transpose(0, 2, 1, 3).reshape(Bsz, L, H_WIDTH) * g_gain * jax.nn.silu(g)
    return o @ w_out

def first_inputs(seed: int = 0) -> dict:
    key = jax.random.key(seed)
    ks = iter(jax.random.split(key, 48))
    f32 = jnp.float32
    nrm = lambda shape, scale: scale * jax.random.normal(next(ks), shape, f32)
    NE, NO = N_EVEN, N_ODD
    nb = M_WIDTH // QKV_BLOCK
    b_if = jnp.concatenate([nrm((NE, M_HEADS), 0.1),
                            jnp.broadcast_to(jnp.linspace(3.0, 6.0, M_HEADS, dtype=f32), (NE, M_HEADS)) + nrm((NE, M_HEADS), 0.01)], axis=-1)
    return {
        'x': nrm((BATCH, SEQ, D_MODEL), 1.0),
        'norm_g': 1.0 + nrm((DEPTH, 4, D_MODEL), 0.05),
        'ab_w_in': nrm((NE, D_MODEL, IN_EVEN), D_MODEL ** -0.5),
        'ab_conv_w': nrm((NE, M_CONV, M_WIDTH), M_CONV ** -0.5),
        'ab_conv_b': nrm((NE, M_WIDTH), 0.01),
        'ab_wq': nrm((NE, nb, QKV_BLOCK, QKV_BLOCK), QKV_BLOCK ** -0.5),
        'ab_wk': nrm((NE, nb, QKV_BLOCK, QKV_BLOCK), QKV_BLOCK ** -0.5),
        'ab_wv': nrm((NE, nb, QKV_BLOCK, QKV_BLOCK), QKV_BLOCK ** -0.5),
        'ab_w_if': nrm((NE, 3 * M_WIDTH, 2 * M_HEADS), 0.1 * (3 * M_WIDTH) ** -0.5),
        'ab_b_if': b_if,
        'ab_mh_gain': 1.0 + nrm((NE, M_WIDTH), 0.05),
        'ab_skip': 1.0 + nrm((NE, M_WIDTH), 0.05),
        'ab_a_re': -0.5 + nrm((NE, S_GROUPS, S_STATE), 0.01),
        'ab_a_im': jnp.pi * jnp.arange(S_STATE, dtype=f32) + nrm((NE, S_GROUPS, S_STATE), 0.01),
        'ab_log_dt': jax.random.uniform(next(ks), (NE, S_GROUPS), f32, math.log(DT_MIN), math.log(DT_MAX)),
        'ab_b_re': nrm((NE, S_GROUPS, S_STATE, S_GROUP), (2 * S_GROUP) ** -0.5),
        'ab_b_im': nrm((NE, S_GROUPS, S_STATE, S_GROUP), (2 * S_GROUP) ** -0.5),
        'ab_c_re': nrm((NE, S_GROUPS, S_GROUP, S_STATE), S_STATE ** -0.5),
        'ab_c_im': nrm((NE, S_GROUPS, S_GROUP, S_STATE), S_STATE ** -0.5),
        'ab_d': nrm((NE, S_WIDTH), 1.0),
        'ab_w_glu': nrm((NE, S_WIDTH, S_WIDTH), S_WIDTH ** -0.5),
        'ab_b_glu': nrm((NE, S_WIDTH), 0.01),
        'ab_w_out': nrm((NE, MIX_EVEN, D_MODEL), MIX_EVEN ** -0.5),
        'c_w_in': nrm((NO, D_MODEL, IN_ODD), D_MODEL ** -0.5),
        'c_lb_raw': nrm((DEPTH, H_WIDTH), 0.1),
        'c_g_gain': 1.0 + nrm((NO, H_WIDTH), 0.05),
        'c_w_out': nrm((NO, H_WIDTH, D_MODEL), H_WIDTH ** -0.5),
        'ffn_w1': nrm((DEPTH, D_MODEL, D_FF), D_MODEL ** -0.5),
        'ffn_w3': nrm((DEPTH, D_MODEL, D_FF), D_MODEL ** -0.5),
        'ffn_w2': nrm((DEPTH, D_FF, D_MODEL), D_FF ** -0.5),
    }

def first_block(x, norm_g, ab_w_in, ab_conv_w, ab_conv_b, ab_wq, ab_wk, ab_wv, ab_w_if, ab_b_if, ab_mh_gain, ab_skip,
              ab_a_re, ab_a_im, ab_log_dt, ab_b_re, ab_b_im, ab_c_re, ab_c_im, ab_d, ab_w_glu, ab_b_glu, ab_w_out,
              c_w_in, c_lb_raw, c_g_gain, c_w_out, ffn_w1, ffn_w3, ffn_w2):
    for layer in range(DEPTH):
        j = layer // 2
        h = rmsnorm(x, norm_g[layer, 0])
        if layer % 2 == 0:
            mix = mixer_ab(h, ab_w_in[j], ab_conv_w[j], ab_conv_b[j], ab_wq[j], ab_wk[j], ab_wv[j], ab_w_if[j],
                           ab_b_if[j], ab_mh_gain[j], ab_skip[j], ab_a_re[j], ab_a_im[j], ab_log_dt[j], ab_b_re[j],
                           ab_b_im[j], ab_c_re[j], ab_c_im[j], ab_d[j], ab_w_glu[j], ab_b_glu[j], ab_w_out[j])
        else:
            mix = mixer_c(h, layer, c_w_in[j], c_lb_raw, c_g_gain[j], c_w_out[j])
        x = x + rmsnorm(mix, norm_g[layer, 1])
        h = rmsnorm(x, norm_g[layer, 2])
        x = x + rmsnorm(swiglu(h, ffn_w1[layer], ffn_w3[layer], ffn_w2[layer]), norm_g[layer, 3])
    return x


GRID_W = 64
CHUNK = 128
Q_BLOCK = 128
N_HEADS = 8
N_KV_HEADS = 2
HEAD_DIM = 64
GQA_GROUP = N_HEADS // N_KV_HEADS
ATTN_WIDTH = N_HEADS * HEAD_DIM
KV_WIDTH = N_KV_HEADS * HEAD_DIM
SG_HEADS = 8
SG_HEAD_DIM = 64
SG_WIDTH = SG_HEADS * SG_HEAD_DIM
MIX_WIDTH = ATTN_WIDTH + SG_WIDTH
IN_WIDTH = ATTN_WIDTH + 2 * KV_WIDTH + 2 * SG_WIDTH
D_FF_2 = 2816
CONV_W = 3
ROPE_THETA = 10000.0


def rms_norm(x, g):
    xf = x.astype(jnp.float32)
    y = xf * lax.rsqrt(jnp.mean(xf * xf, axis=-1, keepdims=True) + EPS)
    return (y * g.astype(jnp.float32)).astype(x.dtype)

def axial_rope_tables(seq_len):
    rows = seq_len // GRID_W
    row = jnp.repeat(jnp.arange(rows, dtype=jnp.float32), GRID_W)
    col = jnp.tile(jnp.arange(GRID_W, dtype=jnp.float32), rows)
    axis_dim = HEAD_DIM // 2
    inv_freq = 1.0 / (ROPE_THETA ** (jnp.arange(0, axis_dim, 2, dtype=jnp.float32) / axis_dim))
    ang_r = row[:, None] * inv_freq[None, :]
    ang_c = col[:, None] * inv_freq[None, :]
    return jnp.cos(ang_r), jnp.sin(ang_r), jnp.cos(ang_c), jnp.sin(ang_c)

def rotate(x, cos, sin):
    n = x.shape[-1] // 2
    x1, x2 = x[..., :n], x[..., n:]
    c = cos[None, :, None, :].astype(x.dtype)
    s = sin[None, :, None, :].astype(x.dtype)
    return jnp.concatenate([x1 * c - x2 * s, x2 * c + x1 * s], axis=-1)

def axial_rope(x, tables):
    cr, sr, cc, sc = tables
    half = HEAD_DIM // 2
    return jnp.concatenate([rotate(x[..., :half], cr, sr), rotate(x[..., half:], cc, sc)], axis=-1)

def gqa_attention(q, k, v):
    b, s, _, dh = q.shape
    nblk = s // Q_BLOCK
    qb = q.reshape(b, nblk, Q_BLOCK, N_KV_HEADS, GQA_GROUP, dh)
    qb = jnp.moveaxis(qb, 1, 0)
    scale = HEAD_DIM ** -0.5

    def one_block(qblk):
        sc = jnp.einsum('bqkgd,bskd->bkgqs', qblk, k).astype(jnp.float32) * scale
        p = jax.nn.softmax(sc, axis=-1).astype(v.dtype)
        return jnp.einsum('bkgqs,bskd->bqkgd', p, v)

    o = lax.map(one_block, qb)
    return jnp.moveaxis(o, 0, 1).reshape(b, s, ATTN_WIDTH)

def spatial_gating(u, vv, sg_norm_g, sg_w, sg_b):
    b, s, _ = u.shape
    nc = s // CHUNK
    vv = rms_norm(vv.reshape(b, s, SG_HEADS, SG_HEAD_DIM), sg_norm_g)
    vv = vv.reshape(b, nc, CHUNK, SG_HEADS, SG_HEAD_DIM)
    mixed = jnp.einsum('hpq,bnqhd->bnphd', sg_w, vv) + sg_b.T[:, :, None]
    out = u.reshape(b, nc, CHUNK, SG_HEADS, SG_HEAD_DIM) * mixed
    return out.reshape(b, s, SG_WIDTH)

def depthwise_conv(h, w, bias):
    c = h.shape[-1]
    y = lax.conv_general_dilated(h, w[:, None, :].astype(h.dtype), window_strides=(1,),
                                 padding=[(CONV_W // 2, CONV_W // 2)],
                                 dimension_numbers=('NWC', 'WIO', 'NWC'),
                                 feature_group_count=c)
    return y + bias

def second_inputs(seed: int = 0) -> dict:
    key = jax.random.key(seed)
    ks = jax.random.split(key, 17)
    f32 = jnp.float32
    nrm = lambda k, shape, scale: jax.random.normal(k, shape, f32) * scale
    gain = lambda k, shape: 1.0 + 0.05 * jax.random.normal(k, shape, f32)
    return {
        "x": jax.random.normal(ks[0], (BATCH, SEQ, D_MODEL), f32),
        "attn_norm_g": gain(ks[1], (DEPTH, D_MODEL)),
        "w_in": nrm(ks[2], (DEPTH, D_MODEL, IN_WIDTH), D_MODEL ** -0.5),
        "q_norm_g": gain(ks[3], (DEPTH, HEAD_DIM)),
        "k_norm_g": gain(ks[4], (DEPTH, HEAD_DIM)),
        "sg_norm_g": gain(ks[5], (DEPTH, SG_HEADS, SG_HEAD_DIM)),
        "sg_w": nrm(ks[6], (DEPTH, SG_HEADS, CHUNK, CHUNK), 0.5 * CHUNK ** -0.5),
        "sg_b": gain(ks[7], (DEPTH, SG_HEADS, CHUNK)),
        "attn_out_g": gain(ks[8], (DEPTH, ATTN_WIDTH)),
        "sg_out_g": gain(ks[9], (DEPTH, SG_WIDTH)),
        "w_o": nrm(ks[10], (DEPTH, MIX_WIDTH, D_MODEL), MIX_WIDTH ** -0.5),
        "ffn_norm_g": gain(ks[11], (DEPTH, D_MODEL)),
        "w_up": nrm(ks[12], (DEPTH, D_MODEL, 2 * D_FF_2), D_MODEL ** -0.5),
        "conv_w": nrm(ks[13], (DEPTH, CONV_W, 2 * D_FF_2), CONV_W ** -0.5),
        "conv_b": nrm(ks[14], (DEPTH, 2 * D_FF_2), 0.02),
        "w_down": nrm(ks[15], (DEPTH, D_FF_2, D_MODEL), D_FF_2 ** -0.5),
    }

def second_block(x, attn_norm_g, w_in, q_norm_g, k_norm_g, sg_norm_g, sg_w, sg_b,
              attn_out_g, sg_out_g, w_o, ffn_norm_g, w_up, conv_w, conv_b, w_down):
    b, s, _ = x.shape
    tables = axial_rope_tables(s)
    split_at = [ATTN_WIDTH, ATTN_WIDTH + KV_WIDTH, ATTN_WIDTH + 2 * KV_WIDTH,
                ATTN_WIDTH + 2 * KV_WIDTH + SG_WIDTH]
    for i in range(DEPTH):
        h = rms_norm(x, attn_norm_g[i])
        proj = h @ w_in[i]
        q, k, v, u, vv = jnp.split(proj, split_at, axis=-1)
        q = rms_norm(q.reshape(b, s, N_HEADS, HEAD_DIM), q_norm_g[i])
        k = rms_norm(k.reshape(b, s, N_KV_HEADS, HEAD_DIM), k_norm_g[i])
        v = v.reshape(b, s, N_KV_HEADS, HEAD_DIM)
        q = axial_rope(q, tables)
        k = axial_rope(k, tables)
        attn_o = gqa_attention(q, k, v)
        sg_o = spatial_gating(jax.nn.gelu(u), jax.nn.gelu(vv),
                              sg_norm_g[i], sg_w[i], sg_b[i])
        merged = jnp.concatenate([rms_norm(attn_o, attn_out_g[i]),
                                  rms_norm(sg_o, sg_out_g[i])], axis=-1)
        x = x + merged @ w_o[i]
        h = rms_norm(x, ffn_norm_g[i]) @ w_up[i]
        h = depthwise_conv(h, conv_w[i], conv_b[i])
        gate, up = jnp.split(h, 2, axis=-1)
        x = x + (jax.nn.silu(gate) * up) @ w_down[i]
    return x


def setup_inputs(seed=0):
    out = dict(first_inputs(seed))
    for name, value in second_inputs(seed + 1).items():
        if name != "x":
            out[name + "_2"] = value
    return out


def reference(
    x, norm_g, ab_w_in, ab_conv_w, ab_conv_b, ab_wq, ab_wk, ab_wv, ab_w_if, ab_b_if, ab_mh_gain,
    ab_skip, ab_a_re, ab_a_im, ab_log_dt, ab_b_re, ab_b_im, ab_c_re, ab_c_im, ab_d, ab_w_glu,
    ab_b_glu, ab_w_out, c_w_in, c_lb_raw, c_g_gain, c_w_out, ffn_w1, ffn_w3, ffn_w2,
    attn_norm_g_2, w_in_2, q_norm_g_2, k_norm_g_2, sg_norm_g_2, sg_w_2, sg_b_2, attn_out_g_2,
    sg_out_g_2, w_o_2, ffn_norm_g_2, w_up_2, conv_w_2, conv_b_2, w_down_2,
):
    x = first_block(
        x, norm_g, ab_w_in, ab_conv_w, ab_conv_b, ab_wq, ab_wk, ab_wv, ab_w_if, ab_b_if,
        ab_mh_gain, ab_skip, ab_a_re, ab_a_im, ab_log_dt, ab_b_re, ab_b_im, ab_c_re, ab_c_im,
        ab_d, ab_w_glu, ab_b_glu, ab_w_out, c_w_in, c_lb_raw, c_g_gain, c_w_out, ffn_w1, ffn_w3,
        ffn_w2,
    )
    return second_block(
        x, attn_norm_g_2, w_in_2, q_norm_g_2, k_norm_g_2, sg_norm_g_2, sg_w_2, sg_b_2,
        attn_out_g_2, sg_out_g_2, w_o_2, ffn_norm_g_2, w_up_2, conv_w_2, conv_b_2, w_down_2,
    )


_drawn_inputs = setup_inputs


def setup_inputs(seed=0):
    import zlib

    import numpy as np

    out = dict(_drawn_inputs(seed))
    spreads = {}
    factors = {'ab_conv_b': 3.871,
     'ab_a_re': 8.0,
     'ab_b_glu': 8.0,
     'c_lb_raw': 7.497,
     'q_norm_g_2': 7.096,
     'k_norm_g_2': 7.112,
     'sg_norm_g_2': 6.507,
     'sg_b_2': 3.343,
     'conv_b_2': 5.971}
    for name, (base, spread) in spreads.items():
        noise = np.random.default_rng([zlib.crc32(name.encode()), seed]).standard_normal(out[name].shape)
        drawn = base * np.exp(spread * noise) if base else spread * noise
        out[name] = __import__('jax').numpy.asarray(drawn.astype(out[name].dtype))
    for name, factor in factors.items():
        out[name] = (out[name] * factor).astype(out[name].dtype)
    return out
```

```python
from contextlib import ExitStack, contextmanager

import numpy as np

import concourse.bass as bass
from concourse import mybir

F32 = mybir.dt.float32
F32R = mybir.dt.float32r
ALU = mybir.AluOpType
ACT = mybir.ActivationFunctionType
AX = mybir.AxisListType

P = 128
SEQ = 512
D = 1024
KD = D // P
TT = SEQ // P
D_FF = 2816
KF = D_FF // P
EPS = 1e-6
RING = 4
AHEAD = 3
SLAB_K = 8
DOWN = [8, 8, KF - 16]
M_HEADS = 4
GROUPS, GW, STATE = 32, 16, 64
STEP = 8
CH = SEQ // STEP
C_HEADS = 8
C_CHUNK = 64
HEAD = 64
IN2 = 1792
TWO_PI = float(2 * np.pi)
PI_HIGH = 6.28125
PI_MID = float(np.float32(2 * np.pi - 6.28125))
PI_LOW = float(2 * np.pi - 6.28125 - np.float64(np.float32(2 * np.pi - 6.28125)))
ROUND = 1.5 * 2.0 ** 23
PI_IN = 3.1415925

ROWS = {}


def plan_rows():
    at = 0
    for name, count in (("norm", 64), ("attn_norm", 16), ("ffn_norm", 16), ("conv_w", 16), ("conv_b", 4),
                        ("mh_gain", 4), ("skip", 4), ("s5_d", 4),
                        ("b_glu", 4), ("lb_raw", 16), ("c_gain", 8), ("attn_gain", 8), ("sg_gain", 8),
                        ("q_norm", 2), ("k_norm", 2), ("a_re", 32), ("a_im", 32),
                        ("pad", 16), ("up_conv", 2 * 4 * 2 * KF)):
        ROWS[name] = at
        at += count
    return at


N_ROWS = plan_rows()
ROW_BLOCKS = -(-N_ROWS // P)


def constants():
    k = np.arange(P)
    zid = np.zeros((P, 2 * P), np.float32)
    zid[k, P + k] = 1
    lead = np.concatenate([zid, np.ones((P, P), np.float32)], 1)
    quad = (k[:, None] // 4 == np.arange(32)[None, :]).astype(np.float32)
    pick = np.zeros((P, M_HEADS, P), np.float32)
    for h in range(M_HEADS):
        pick[h, h] = 1
    causal = (k[:, None] <= k[None, :]).astype(np.float32)
    causal_c = causal * (k[:, None] // C_CHUNK == k[None, :] // C_CHUNK)
    restart = np.broadcast_to((np.arange(SEQ) % C_CHUNK != 0).astype(np.float32), (P, SEQ))
    swap = (k[:, None] == (k[None, :] + HEAD) % P).astype(np.float32)
    sign = np.where(k < HEAD, -1.0, 1.0).astype(np.float32)[:, None]
    early = np.concatenate([quad, pick.reshape(P, -1), causal, causal_c, restart, swap, sign], 1)
    inv = (1.0 / (np.float32(10000.0) ** (np.arange(0, 32, 2, dtype=np.float32) / np.float32(32)))).astype(np.float32)
    t = np.arange(SEQ)
    within = k % HEAD
    pos = np.where((within < 32)[:, None], (t // 64)[None, :], (t % 64)[None, :]).astype(np.float32)
    ang = pos * inv[within % 16][:, None]
    upper = (within % 32) >= 16
    cos = np.cos(ang).astype(np.float32)
    sin = (np.sin(ang) * np.where(upper, 1, -1)[:, None]).astype(np.float32)
    partner = np.where(upper, k - 16, k + 16)
    turn = (k[:, None] == partner[None, :]).astype(np.float32)
    block = (k[:, None] // HEAD == k[None, :] // HEAD).astype(np.float32)
    late = np.concatenate([cos, sin, turn, block], 1)
    return {"lead": lead, "early": np.ascontiguousarray(early), "late": late}


class Count:

    def __init__(self):
        self.seen, self.shift = {}, {}

    def __call__(self, sem, by=1):
        self.seen[sem.name] = self.seen.get(sem.name, 0) + by
        return self.now(sem)

    def now(self, sem):
        value = self.seen.get(sem.name, 0)
        return value if sem.name not in self.shift else self.shift[sem.name] + value

    @contextmanager
    def loop(self, eng, times, per):
        before = dict(self.seen)
        with eng.Fori(0, times) as i:
            self.shift = {sem.name: i * by for sem, by in per}
            yield i
        self.shift = {}
        turn = {k: v - before.get(k, 0) for k, v in self.seen.items() if v != before.get(k, 0)}
        want = {sem.name: by for sem, by in per}
        assert turn == want, f"per turn {turn}, not {want}"
        for k, v in want.items():
            self.seen[k] += (times - 1) * v


def program(nc, a, upto):
    ctx = ExitStack()
    with ctx:
        top = [-(-nc.sbuf_base // 64) * 64]

        def place(name, shape, dt=F32, at=None):
            size = 4 * int(np.prod(shape[1:]))
            if at is None:
                at = top[0]
                top[0] += -(-size // 32) * 32
                assert top[0] <= nc.sbuf_usable_end, (name, top[0])
            return nc.alloc_sbuf_tensor_at(name, list(shape), dt, offset=at)

        def sem(name):
            return ctx.enter_context(nc.semaphore(name))

        w_raw = place("w_raw", [P, RING, SLAB_K, P])
        w_hi = place("w_hi", [P, RING, SLAB_K, P], F32R)
        w_lo = place("w_lo", [P, RING, SLAB_K, P], F32R)
        x = place("x", [P, KD, SEQ])
        H0 = top[0]
        h_hi = place("h_hi", [P, KD, SEQ], F32R)
        h_lo = place("h_lo", [P, KD, SEQ], F32R)
        M0 = top[0]
        hid_hi = place("hid_hi", [P, KF, SEQ], F32R)
        hid_lo = place("hid_lo", [P, KF, SEQ], F32R)
        M1 = top[0]
        par = place("par", [P, ROW_BLOCKS * P])
        lead = place("lead", [P, 3 * P])
        shifted, ident, ones = lead[:, 0:2 * P], lead[:, P:2 * P], lead[:, 2 * P:3 * P]
        early = place("early", [P, 32 + 4 * P + 2 * P + SEQ + P + 1])
        quad = early[:, 0:32]
        pick = early[0:M_HEADS, 32:32 + 4 * P].rearrange("k (h m) -> k h m", h=M_HEADS)
        causal = early[:, 544:672]
        causal_c = early[:, 672:800]
        restart = early[:, 800:1312]
        swap = early[:, 1312:1440]
        sign = early[:, 1440:1441]
        eps = place("eps", [P, 1])
        rstd = place("rstd", [P, SEQ])
        rinv = place("rinv", [P, SEQ])
        tmp = place("tmp", [P, 4, SEQ])
        small = place("small", [P, 256])
        lstm_w4 = place("lstm_w4", [P, 3, 4, 4])
        lstm_wif = place("lstm_wif", [P, 12, 8])
        lstm_bif = place("lstm_bif", [M_HEADS, 2])
        lb = place("lb", [P, 8, 8])

        def m(name, shape, kb, dt=F32):
            assert M0 + 1024 * kb + 4 * int(np.prod(shape[1:])) <= M1, name
            return place(name, shape, dt, at=M0 + int(1024 * kb))

        def hm(name, shape, kb):
            assert H0 + 1024 * kb + 4 * int(np.prod(shape[1:])) <= M0, name
            return place(name, shape, F32, at=H0 + int(1024 * kb))

        x_tok = m("x_tok", [P, TT, D], 0)
        rows = m("rows", [P, ROW_BLOCKS, P], 16)
        out_tok = m("out_tok", [P, TT, D], 0)
        sq_ab = m("sq_ab", [P, KD, SEQ], 0)
        sq_in = m("sq_in", [P, KD, SEQ], 64)
        y_mix = m("y_mix", [P, KD, SEQ], 64)
        sq_mix = m("sq_mix", [P, KD, SEQ], 0)
        y_ffn = hm("y_ffn", [P, KD, SEQ], 0)
        sq_ffn = hm("sq_ffn", [P, KD, SEQ], 16)
        xm = m("xm", [P, 4, SEQ], 0)
        zs = m("zs", [P, 4, SEQ], 8)
        us = m("us", [P, 4, STEP, CH], 16)
        s5_in = m("s5_in", [P, GROUPS, P], 24)
        s5_out = m("s5_out", [P, GROUPS, STEP, GW], 40)
        s5_conv = m("s5_conv", [P, GROUPS, STEP, GW], 56)
        s5_cos = m("s5_cos", [P, GROUPS, CH], 72)
        s5_sin = m("s5_sin", [P, GROUPS, CH], 80)
        s5_q = m("s5_q", [P, GROUPS, STEP, GW], 56)
        s5_b = hm("s5_b", [P, 2, GROUPS, GW], 0)
        s5_bb = hm("s5_bb", [P, 2, GROUPS, GW], 4)
        s5_crow = hm("s5_crow", [P, 2, 4, P], 8)
        s5_c = hm("s5_c", [P, 2, GROUPS, GW], 12)
        s5_cx = hm("s5_cx", [P, GROUPS, GW], 16)
        s5_k = hm("s5_k", [P, GROUPS, GW], 18)
        s5_pow = hm("s5_pow", [P, 2, STEP + 1, GROUPS], 20)
        s5_ldt = hm("s5_ldt", [P, GROUPS], 23)
        s5_v = hm("s5_v", [P, 24, GROUPS], 24)
        s5_r8 = place("s5_r8", [P, GROUPS])
        s5_big = m("s5_big", [P, GROUPS, STEP, GW], 0)
        s5_t = hm("s5_t", [P, GROUPS, CH // 2], 28)
        u_step = hm("u_step", [P, GROUPS, CH], 0)
        s5_state = hm("s5_state", [P, GROUPS, CH], 8)
        s5_w = hm("s5_w", [P, GROUPS, CH], 16)
        s5_z = hm("s5_z", [P, GROUPS, CH], 24)
        ys_step = hm("ys_step", [P, GROUPS, CH], 16)
        ys = m("ys", [P, 4, SEQ], 24)
        yg = m("yg", [P, 4, SEQ], 32)
        gate = m("gate", [P, 4, SEQ], 40)
        xc = m("xc", [P, 4, SEQ], 16)
        qm = m("qm", [P, 4, SEQ], 24)
        km = m("km", [P, 4, SEQ], 32)
        vf = m("vf", [P, 4, SEQ], 40)
        vt = m("vt", [P, 4, TT, P], 48)
        sc_m = m("sc_m", [P, TT, SEQ], 56)
        lstm_bd = m("lstm_bd", [P, 3, 4, P], 64)
        rowv = m("rowv", [M_HEADS, 8, SEQ], 70)
        e_m = m("e_m", [P, 2, SEQ], 64)
        g_col = small[:, 0:16].rearrange("p (s h) -> p s h", s=TT)
        lstm_t = m("lstm_t", [P, 4, SEQ], 40)
        qc = m("qc", [P, 8, SEQ], 0)
        fc = m("fc", [P, 8, SEQ], 16)
        ic = m("ic", [P, 8, SEQ], 32)
        gc = m("gc", [P, 8, SEQ], 48)
        c_k = m("c_k", [P, SEQ], 64)
        c_f = m("c_f", [P, SEQ], 66)
        c_b = m("c_b", [P, SEQ], 68)
        c_d = m("c_d", [P, SEQ], 70)
        c_e = m("c_e", [P, SEQ], 72)
        c_kt = m("c_kt", [P, TT, P], 74)
        c_it = m("c_it", [P, TT, P], 76)
        c_s = m("c_s", [P, TT, P], 78)
        c_state = m("c_state", [P, 8, P], 80)
        c_i = m("c_i", [P, SEQ], 84)
        c_o = m("c_o", [P, SEQ], 86)
        late = m("late", [P, 2 * SEQ + 2 * P], 0)
        cos, sin = late[:, 0:SEQ], late[:, SEQ:2 * SEQ]
        turn, halves = late[:, 2 * SEQ:2 * SEQ + P], late[:, 2 * SEQ + P:2 * SEQ + 2 * P]
        qa = m("qa", [P, 5, SEQ], 6)
        k_swap = m("k_swap", [P, SEQ], 84)
        va = m("va", [P, SEQ], 16)
        ua = m("ua", [P, 4, SEQ], 18)
        vva = m("vva", [P, 4, SEQ], 26)
        v_tok = m("v_tok", [P, TT, P], 34)
        vv_tok = m("vv_tok", [P, TT, SEQ], 36)
        sgw = m("sgw", [P, 8, P], 44)
        sgw_t = m("sgw_t", [P, 8, P], 48)
        sgb = m("sgb", [P, 4, P], 52)
        sgn = m("sgn", [P, SEQ], 54)
        prob = m("prob", [P, 2, SEQ], 56)
        prob_t = m("prob_t", [P, TT, SEQ], 60)
        oa = m("oa", [P, 4, SEQ], 68)
        g_t = m("g_t", [P, 4, SEQ], 76)
        g_small = small[:, 64:128]

        bank = [ctx.enter_context(nc.psum_tensor(f"bank{b}", [P, 512], F32)) for b in range(8)]

        us_dram = nc.dram_tensor("us_dram", [4 * P, STEP, CH], F32, kind="Internal").ap()
        ys_dram = nc.dram_tensor("ys_dram", [4 * P, STEP, CH], F32, kind="Internal").ap()

        bank_free = [sem(f"bank{b}_free") for b in range(8)]
        raw_full = [sem(f"raw{s}_full") for s in range(RING)]
        hi_done = sem("hi_done")
        lo_done = sem("lo_done")
        slab_done = sem("slab_done")
        lead_in, x_in, early_in, rows_in = sem("lead_in"), sem("x_in"), sem("early_in"), sem("rows_in")
        s5_in_sem, lstm_in = sem("s5_in"), sem("lstm_in")
        x_turned, x_ready = sem("x_turned"), sem("x_ready")
        par_turned, par_ready = sem("par_turned"), sem("par_ready")
        eps_ready = sem("eps_ready")
        sq_ready, stat_ready, std_ready = sem("sq_ready"), sem("stat_ready"), sem("std_ready")
        h_ready, hid_ready, evac_ready = sem("h_ready"), sem("hid_ready"), sem("evac_ready")
        act_for_dve, dve_for_act = sem("ffn_scalar_to_vector"), sem("ffn_vector_to_scalar")
        vector_step = sem("vector_step")
        scalar_step = sem("scalar_step")

        def five(name):
            return {k: sem(f"{name}_{k}") for k in ("pe_to_vector", "pe_to_scalar", "vector_to_pe",
                                                     "scalar_to_pe", "vector_to_scalar", "scalar_to_vector")}

        prep, s5, lstm, hgrn, att = five("prep"), five("s5"), five("lstm"), five("hgrn"), five("att")
        us_stored, us_loaded, ys_stored, ys_loaded = (sem(k) for k in ("us_stored", "us_loaded", "ys_stored", "ys_loaded"))
        late_in, us_ready, ys_ready = sem("late_in"), sem("us_ready"), sem("ys_ready")
        out_turned, out_ready, out_stored = sem("out_turned"), sem("out_ready"), sem("out_stored")

        def cols(w):
            return w.rearrange("(k p) n -> p k n", p=P)

        SIZE = {"ab_in": 12, "ab_glu": 4, "ab_out": 8, "ffn1": 44, "ffn2": 24, "c_in": 32, "c_out": 8,
                "s_in": 14, "s_out": 8, "up": 44, "down": 24}
        parts = [["ab_in", "ab_glu", "ab_out"], ["ffn1", "ffn2"], ["c_in", "c_out"], ["ffn1", "ffn2"],
                 ["s_in", "s_out"], ["up", "down"], ["s_in", "s_out"], ["up", "down"]][:upto]
        row_dmas = [0]

        def block_rows(b):
            return ROWS["pad"] - P if b == 1 else min(P, N_ROWS - b * P)

        N_SLABS = sum(SIZE[s] for part in parts for s in part)

        def col(name, i=0):
            c = ROWS[name] + i
            return par[:, c:c + 1]

        def col_at(name, i):
            return par[:, bass.ds(i + ROWS[name], 1)]

        block = ctx.enter_context(nc.Block())

        @block.sync
        def _(sp):
            n = Count()
            sp.dma_start(lead[:], a["lead"]).then_inc(lead_in, 16)
            sp.dma_start(x_tok[:], a["x"][0].rearrange("(t p) d -> p t d", p=P)).then_inc(x_in, 16)
            slab = [0]

            def load(src):
                s = slab[0] % RING
                if slab[0] >= RING:
                    sp.wait_ge(lo_done, n(lo_done))
                sp.dma_start(w_raw[:, s, 0:src.shape[1]], src).then_inc(raw_full[s], 16)
                slab[0] += 1

            def stream(times, slabs, turn):
                if times > 1:
                    with n.loop(sp, times, [(lo_done, slabs)]) as i:
                        turn(i)
                    slab[0] += (times - 1) * slabs
                else:
                    turn(0)

            def plain(w, tiles):
                w = cols(w)

                def turn(i):
                    for t in range(RING):
                        load(w[:, :, bass.ds(i * (RING * P) + t * P, P)])
                stream(tiles // RING, RING, turn)

            def pairs(w, v, at):
                w, v = cols(w), cols(v)

                def turn(i):
                    for t in range(RING // 2):
                        load(w[:, :, bass.ds(i * (RING // 2 * P) + t * P, P)])
                        load(v[:, :, bass.ds(i * (RING // 2 * P) + (t * P + at), P)])
                stream(KF // 2, RING, turn)

            def deep(w):
                w = cols(w)

                def turn(i):
                    for t in range(RING):
                        for k, c in ((0, 8), (8, 8), (16, KF - 16)):
                            load(w[:, k:k + c, bass.ds(i * (RING * P) + t * P, P)])
                stream(2, RING * len(DOWN), turn)

            def ab():
                w = cols(a["ab_w_in"][0])
                for t in range(12):
                    load(w[:, :, t * P:(t + 1) * P])
                w = cols(a["ab_w_glu"][0])
                for t in range(4):
                    load(w[:, :, t * P:(t + 1) * P])
                plain(a["ab_w_out"][0], 8)

            def c():
                plain(a["c_w_in"][0], 32)
                plain(a["c_w_out"][0], 8)

            def ffn(i):
                pairs(a["ffn_w1"][i], a["ffn_w3"][i], 0)
                deep(a["ffn_w2"][i])

            def gated(i):
                w = cols(a["w_in_2"][i])
                for t in range(14):
                    load(w[:, :, t * P:(t + 1) * P])
                plain(a["w_o_2"][i], 8)

            def conv_ffn(i):
                pairs(a["w_up_2"][i], a["w_up_2"][i], D_FF)
                deep(a["w_down_2"][i])

            for part in [ab, lambda: ffn(0), c, lambda: ffn(1), lambda: gated(0), lambda: conv_ffn(0),
                         lambda: gated(1), lambda: conv_ffn(1)][:upto]:
                part()
            out = a["out"][0].rearrange("(t p) d -> p t d", p=P)
            for t in range(TT):
                sp.wait_ge(out_ready, 2 * t + 2)
                sp.dma_start(out[:, t], out_tok[:, t]).then_inc(out_stored, 16)
            sp.wait_ge(out_stored, 16 * TT)

        @block.gpsimd
        def _(pool):
            n = Count()

            def load_rows(src, first):
                at = 0
                while at < src.shape[0]:
                    r = (first + at) % P
                    k = min(P - r, src.shape[0] - at)
                    pool.dma_start(rows[r:r + k, (first + at) // P, 0:src.shape[1]] if src.shape[1] == P else None,
                                   src[at:at + k]).then_inc(rows_in, 16)
                    row_dmas[0] += 1
                    at += k

            def twice(src, first):
                r, b = first % P, first // P
                for h in range(2):
                    pool.dma_start(rows[r:r + src.shape[0], b, HEAD * h:HEAD * h + HEAD], src).then_inc(rows_in, 16)
                    row_dmas[0] += 1

            load_rows(a["norm_g"].rearrange("l j (k p) -> (l j k) p", p=P), ROWS["norm"])
            for key, name in (("attn_norm_g_2", "attn_norm"), ("ffn_norm_g_2", "ffn_norm"), ("ab_conv_b", "conv_b"),
                              ("ab_mh_gain", "mh_gain"), ("ab_skip", "skip"), ("ab_d", "s5_d"), ("ab_b_glu", "b_glu"),
                              ("c_lb_raw", "lb_raw"), ("c_g_gain", "c_gain"), ("attn_out_g_2", "attn_gain"),
                              ("sg_out_g_2", "sg_gain")):
                load_rows(a[key].rearrange("l (k p) -> (l k) p", p=P), ROWS[name])
            load_rows(a["ab_conv_w"][0].rearrange("t (k p) -> (t k) p", p=P), ROWS["conv_w"])
            twice(a["q_norm_g_2"], ROWS["q_norm"])
            twice(a["k_norm_g_2"], ROWS["k_norm"])
            twice(a["ab_a_re"][0], ROWS["a_re"])
            twice(a["ab_a_im"][0], ROWS["a_im"])
            for i in range(2):
                first = ROWS["up_conv"] + i * 4 * 2 * KF
                load_rows(a["conv_w_2"][i].rearrange("t (k p) -> (t k) p", p=P), first)
                load_rows(a["conv_b_2"][i].rearrange("(k p) -> k p", p=P), first + 3 * 2 * KF)
            b_re, b_im = (a[k][0].rearrange("g n p -> n g p") for k in ("ab_b_re", "ab_b_im"))
            c_re, c_im = (a[k][0].rearrange("g p n -> (g p) n").rearrange("(b q) n -> q b n", q=P)
                          for k in ("ab_c_re", "ab_c_im"))
            for v, (first, second) in enumerate(((b_re, b_im), (b_im, b_re))):
                pool.dma_start(s5_b[0:STATE, v], first).then_inc(s5_in_sem, 16)
                pool.dma_start(s5_b[STATE:P, v], second).then_inc(s5_in_sem, 16)
            for v, (first, second) in enumerate(((c_re, c_im), (c_im, c_re))):
                pool.dma_start(s5_crow[:, v, :, 0:STATE], first).then_inc(s5_in_sem, 16)
                pool.dma_start(s5_crow[:, v, :, STATE:P], second).then_inc(s5_in_sem, 16)
            pool.dma_start(s5_ldt[:], a["ab_log_dt"][0].partition_broadcast(P)).then_inc(s5_in_sem, 16)
            pool.dma_start(early[:], a["early"]).then_inc(early_in, 16)
            for v, key in enumerate(("ab_wq", "ab_wk", "ab_wv")):
                pool.dma_start(lstm_w4[:, v], a[key][0].rearrange("n d e -> (n d) e").rearrange("(t p) e -> p t e", p=P))\
                    .then_inc(lstm_in, 16)
            pool.dma_start(lstm_wif[:], a["ab_w_if"][0].rearrange("(k p) g -> p k g", p=P)).then_inc(lstm_in, 16)
            for v in range(2):
                pool.dma_start(lstm_bif[:, v:v + 1], a["ab_b_if"][0, M_HEADS * v:M_HEADS * v + M_HEADS].unsqueeze(1))\
                    .then_inc(lstm_in, 16)

            pool.wait_ge(us_ready, 1)
            pool.dma_start(us_dram.rearrange("(k p) i c -> p k i c", p=P), us[:]).then_inc(us_stored, 16)
            pool.wait_ge(us_stored, 16)
            by_step = us_dram.rearrange("(g p) i c -> i p g c", p=GW)
            for i in range(STEP):
                k = STEP - 1 - i
                pool.dma_start(u_step[GW * k:GW * k + GW], by_step[i]).then_inc(us_loaded, 16)
            pool.wait_ge(ys_ready, 1)
            by_step = ys_dram.rearrange("(g p) j c -> j p g c", p=GW)
            for j in range(STEP):
                pool.dma_start(by_step[j], ys_step[GW * j:GW * j + GW]).then_inc(ys_stored, 16)
            pool.wait_ge(ys_stored, 16 * STEP)
            pool.dma_start(ys[:], ys_dram.rearrange("(k p) j c -> p k (j c)", p=P)).then_inc(ys_loaded, 16)

            for i in range(2):
                if upto <= 4 + 2 * i:
                    break
                pool.wait_ge(x_ready, 8 * (5 + 2 * i))
                pool.dma_start(late[:], a["late"]).then_inc(late_in, 16)
                pool.dma_start(sgw[:], a["sg_w_2"][i].rearrange("h p q -> p h q")).then_inc(late_in, 16)
                for h in range(8):
                    pool.dma_start(sgb[HEAD * (h % 2):HEAD * (h % 2) + HEAD, h // 2],
                                   a["sg_b_2"][i, h].partition_broadcast(HEAD)).then_inc(late_in, 16)
                pool.dma_start(sgn[:], a["sg_norm_g_2"][i].rearrange("h d -> (h d)").partition_broadcast(P))\
                    .then_inc(late_in, 16)

        @block.tensor
        def _(pe):
            n = Count()
            at = {"slab": 0, "bank": 0}

            def take(b):
                pe.wait_ge(bank_free[b], n(bank_free[b]))
                return bank[b]

            def product(hi, lo, slabs, tiles):
                for _ in range(tiles):
                    out = take(at["bank"] % RING)
                    kt = 0
                    for many in slabs:
                        s = at["slab"] % RING
                        pe.wait_ge(lo_done, n(lo_done))
                        for k in range(many):
                            for w, v in ((w_hi, hi), (w_lo, hi), (w_hi, lo)):
                                mm = nc.tensor.matmul(out[:], w[:, s, k], v[:, kt],
                                                      start=(kt == 0 and w is w_hi and v is hi),
                                                      stop=(kt == sum(slabs) - 1 and v is lo))
                            kt += 1
                        mm.then_inc(slab_done, 1)
                        at["slab"] += 1
                    at["bank"] += 1

            def products(hi, lo, slabs, tiles):
                times = tiles // RING
                per = [(lo_done, RING * len(slabs))] + [(bank_free[b], 1) for b in range(RING)]
                if times == 1:
                    product(hi, lo, slabs, RING)
                    return
                with n.loop(pe, times, per):
                    product(hi, lo, slabs, RING)
                at["slab"] += (times - 1) * RING * len(slabs)
                at["bank"] += (times - 1) * RING

            def sums(squares, tiles, ready=None):
                out = take(4)
                for k in range(tiles):
                    pe.wait_ge(sq_ready, n(sq_ready))
                    mm = nc.tensor.matmul(out[:], ones, squares[:, k], start=(k == 0), stop=(k == tiles - 1))
                mm.then_inc(stat_ready, 1)

            pe.wait_ge(lead_in, 16)
            pe.wait_ge(x_in, 16)
            for k in range(KD):
                out = take(k % RING)
                for t in range(TT):
                    mm = nc.tensor.transpose(out[:, t * P:(t + 1) * P], x_tok[:, t, k * P:(k + 1) * P], ident)
                mm.then_inc(x_turned, 1)
            pe.wait_ge(rows_in, 16 * row_dmas[0])
            for b in range(ROW_BLOCKS):
                out = take(4 + b % 4)
                r = block_rows(b)
                nc.tensor.transpose(out[:, 0:r], rows[0:r, b], ident[0:r, 0:r]).then_inc(par_turned, 1)

            def s5_prepare():
                pe.wait_ge(s5_in_sem, 16 * 9)
                for v in range(2):
                    out = take(5 + v)
                    for b in range(4):
                        mm = nc.tensor.transpose(out[:, b * P:(b + 1) * P], s5_crow[:, v, b], ident)
                    mm.then_inc(prep["pe_to_vector"], 1)
                pe.wait_ge(prep["vector_to_pe"], n(prep["vector_to_pe"]))
                for i in range(GROUPS // 4):
                    out = take(4 + i % 4)
                    for g in range(4):
                        mm = nc.tensor.transpose(out[:, g * P:(g + 1) * P],
                                                 s5_q[:, 4 * i + g].rearrange("p k w -> p (k w)"), ident)
                    mm.then_inc(prep["pe_to_scalar"], 1)
                pe.wait_ge(prep["vector_to_pe"], n(prep["vector_to_pe"]))
                out = take(4)
                for g in range(GROUPS):
                    mm = nc.tensor.matmul(out[:, g * GW:(g + 1) * GW], s5_q[:, g].rearrange("p k w -> p (k w)"),
                                          s5_cx[:, g], start=True, stop=True)
                mm.then_inc(prep["pe_to_scalar"], 1)
                pe.wait_ge(prep["scalar_to_pe"], n(prep["scalar_to_pe"]))
                for j in range(STEP):
                    out = take(5 + j % 3)
                    off = P - GW * (STEP - 1 - j)
                    nc.tensor.matmul(out[:], shifted[:, off:off + P], s5_k[:].rearrange("p g w -> p (g w)"),
                                     start=True, stop=True).then_inc(prep["pe_to_scalar"], 1)

            def s5_run():
                pe.wait_ge(us_loaded, 16 * STEP)
                for i in range(4):
                    out = take(4 + i)
                    for g in range(8):
                        mm = nc.tensor.matmul(out[:, g * CH:(g + 1) * CH], s5_in[:, 8 * i + g], u_step[:, 8 * i + g],
                                              start=True, stop=True)
                    mm.then_inc(s5["pe_to_scalar"], 1)
                for i in range(4):
                    out = take(i)
                    pe.wait_ge(s5["scalar_to_pe"], n(s5["scalar_to_pe"]))
                    nc.tensor.matmul(out[:], swap, s5_state[:, 8 * i:8 * i + 8].rearrange("p g c -> p (g c)"),
                                     start=True, stop=True).then_inc(s5["pe_to_vector"], 1)
                pe.wait_ge(s5["vector_to_pe"], n(s5["vector_to_pe"]))
                for i in range(4):
                    out = take(4 + i)
                    nc.tensor.matmul(out[:], swap, s5_z[:, 8 * i:8 * i + 8].rearrange("p g c -> p (g c)"),
                                     start=True, stop=True).then_inc(s5["pe_to_vector"], 1)
                for i in range(4):
                    out = take(i)
                    pe.wait_ge(s5["vector_to_pe"], n(s5["vector_to_pe"]))
                    for g in range(8):
                        c = g * CH
                        nc.tensor.matmul(out[:, c:c + CH], s5_conv[:, 8 * i + g].rearrange("p j w -> p (j w)"),
                                         u_step[:, 8 * i + g], start=True, stop=False)
                        mm = nc.tensor.matmul(out[:, c + 1:c + CH], s5_out[:, 8 * i + g].rearrange("p j w -> p (j w)"),
                                              s5_state[:, 8 * i + g, 0:CH - 1], start=False, stop=True)
                    mm.then_inc(s5["pe_to_scalar"], 1)

            def lstm_run():
                for k in range(4):
                    pe.wait_ge(lstm["scalar_to_pe"], n(lstm["scalar_to_pe"]))
                    for v, src in ((0, xc), (1, xc), (2, xm)):
                        out = take(4 + v)
                        nc.tensor.matmul(out[:], lstm_bd[:, v, k], src[:, k], start=True, stop=True)\
                            .then_inc(lstm["pe_to_scalar"], 1)
                    out = take(7)
                    for t in range(TT):
                        mm = nc.tensor.matmul(out[:, t * P:(t + 1) * P], xm[:, k, t * P:(t + 1) * P], lstm_bd[:, 2, k],
                                              start=True, stop=True)
                    mm.then_inc(lstm["pe_to_scalar"], 1)
                pe.wait_ge(lstm["scalar_to_pe"], n(lstm["scalar_to_pe"]))
                for v in range(2):
                    out = take(4 + v)
                    for j in range(12):
                        mm = nc.tensor.matmul(out[0:M_HEADS, :], lstm_wif[:, j, 4 * v:4 * v + 4], (qm, km, vf)[j // 4][:, j % 4],
                                              start=(j == 0), stop=(j == 11))
                    mm.then_inc(lstm["pe_to_scalar"], 1)
                pe.wait_ge(lstm["vector_to_pe"], n(lstm["vector_to_pe"]))
                out = take(6)
                for t in range(TT):
                    mm = nc.tensor.transpose(out[:, 4 * t:4 * t + 4], rowv[:, 7, t * P:(t + 1) * P], ident[0:4, 0:4])
                mm.then_inc(lstm["pe_to_vector"], 1)
                pe.wait_ge(lstm["scalar_to_pe"], n(lstm["scalar_to_pe"]))
                for h in range(M_HEADS):
                    for v, row in ((0, 3), (1, 5)):
                        out = take(4 + v)
                        nc.tensor.matmul(out[:], pick[:, h], rowv[:, row], start=True, stop=True)\
                            .then_inc(lstm["pe_to_scalar"], 1)
                    for t in range(TT):
                        out = take(6 + t % 2)
                        nc.tensor.matmul(out[:, 0:SEQ - t * P], km[:, h, t * P:(t + 1) * P], qm[:, h, t * P:SEQ],
                                         start=True, stop=True).then_inc(lstm["pe_to_vector"], 1)
                    num, den = take(0), take(1)
                    for t in range(TT):
                        pe.wait_ge(lstm["vector_to_pe"], n(lstm["vector_to_pe"]))
                        nc.tensor.matmul(num[:, t * P:SEQ], vt[:, h, t], sc_m[:, t, t * P:SEQ], start=(t == 0), stop=(t == 3))
                        mm = nc.tensor.matmul(den[:, t * P:SEQ], ones, sc_m[:, t, t * P:SEQ], start=(t == 0), stop=(t == 3))
                    mm.then_inc(lstm["pe_to_vector"], 1)
                    out = take(2)
                    pe.wait_ge(lstm["vector_to_pe"], n(lstm["vector_to_pe"]))
                    nc.tensor.matmul(out[:], ones, lstm_t[:, 2], start=True, stop=True).then_inc(lstm["pe_to_vector"], 1)
                    out = take(3)
                    pe.wait_ge(lstm["scalar_to_pe"], n(lstm["scalar_to_pe"]))
                    nc.tensor.matmul(out[:], ones, lstm_t[:, 0], start=True, stop=True).then_inc(lstm["pe_to_scalar"], 1)

            def ab():
                s5_prepare()
                sums(sq_ab, KD)
                pe.wait_ge(h_ready, n(h_ready, KD))
                products(h_hi, h_lo, [8], 12)
                s5_run()
                pe.wait_ge(h_ready, n(h_ready, 4))
                product(h_hi, h_lo, [4], 4)
                lstm_run()
                pe.wait_ge(h_ready, n(h_ready, 8))
                products(h_hi, h_lo, [8], 8)
                sums(sq_mix, KD)

            def ffn(i):
                sums(sq_in, KD)
                pe.wait_ge(h_ready, n(h_ready, KD))
                products(h_hi, h_lo, [8], 2 * KF)
                pe.wait_ge(hid_ready, n(hid_ready, KF))
                products(hid_hi, hid_lo, DOWN, 8)
                sums(sq_ffn, KD)

            def c():
                sums(sq_in, KD)
                pe.wait_ge(h_ready, n(h_ready, KD))
                products(h_hi, h_lo, [8], 32)
                per = [(hgrn["scalar_to_pe"], 3), (hgrn["vector_to_pe"], 3)] + [(bank_free[b], 1) for b in range(7)]
                with n.loop(pe, C_HEADS, per):
                    out = take(4)
                    pe.wait_ge(hgrn["scalar_to_pe"], n(hgrn["scalar_to_pe"]))
                    for t in range(TT):
                        mm = nc.tensor.transpose(out[:, t * P:(t + 1) * P], c_i[:, t * P:(t + 1) * P], ident)
                    mm.then_inc(hgrn["pe_to_scalar"], 1)
                    out = take(5)
                    pe.wait_ge(hgrn["vector_to_pe"], n(hgrn["vector_to_pe"]))
                    for t in range(TT):
                        mm = nc.tensor.transpose(out[:, t * P:(t + 1) * P], c_k[:, t * P:(t + 1) * P], ident)
                    mm.then_inc(hgrn["pe_to_scalar"], 1)
                    out = take(6)
                    for t in range(TT):
                        mm = nc.tensor.matmul(out[:, t * P:(t + 1) * P], c_k[:, t * P:(t + 1) * P], c_d[:, t * P:(t + 1) * P],
                                              start=True, stop=True)
                    mm.then_inc(hgrn["pe_to_vector"], 1)
                    u = take(0), take(1)
                    pe.wait_ge(hgrn["scalar_to_pe"], n(hgrn["scalar_to_pe"]))
                    for j in range(7):
                        r = C_CHUNK * (j % 2)
                        mm = nc.tensor.matmul(u[j % 2][:, (j // 2) * P:(j // 2 + 1) * P], c_kt[r:r + C_CHUNK, j // 2],
                                              c_it[r:r + C_CHUNK, j // 2], start=True, stop=True)
                    mm.then_inc(hgrn["pe_to_vector"], 1)
                    out = take(2)
                    pe.wait_ge(hgrn["vector_to_pe"], n(hgrn["vector_to_pe"], 2))
                    for t in range(TT):
                        nc.tensor.matmul(out[:, t * P:(t + 1) * P], c_it[:, t], c_s[:, t], start=True, stop=False)
                        for j in (2 * t, 2 * t + 1):
                            if j:
                                mm = nc.tensor.matmul(out[:, j * C_CHUNK:(j + 1) * C_CHUNK], c_state[:, j],
                                                      c_e[:, j * C_CHUNK:(j + 1) * C_CHUNK], start=False, stop=(j % 2 == 1))
                    mm.then_inc(hgrn["pe_to_scalar"], 1)
                    out = take(3)
                    pe.wait_ge(hgrn["scalar_to_pe"], n(hgrn["scalar_to_pe"]))
                    nc.tensor.matmul(out[:], ones, c_o[:], start=True, stop=True).then_inc(hgrn["pe_to_scalar"], 1)
                pe.wait_ge(h_ready, n(h_ready, C_HEADS))
                products(h_hi, h_lo, [8], 8)
                sums(sq_mix, KD)

            def gated(i):
                sums(sq_in, KD)
                pe.wait_ge(h_ready, n(h_ready, KD))
                product(h_hi, h_lo, [8], 14)
                pe.wait_ge(late_in, n(late_in, 16 * 11))
                for v in range(2):
                    out = take(4 + v)
                    for h in range(4):
                        mm = nc.tensor.transpose(out[:, h * P:(h + 1) * P], sgw[:, 4 * v + h], ident)
                    mm.then_inc(att["pe_to_scalar"], 1)
                pe.wait_ge(att["scalar_to_pe"], n(att["scalar_to_pe"]))
                out = take(6)
                for t in range(TT):
                    mm = nc.tensor.transpose(out[:, t * P:(t + 1) * P], va[:, t * P:(t + 1) * P], ident)
                mm.then_inc(att["pe_to_scalar"], 1)
                for t in range(TT):
                    out = take((7, 4, 5, 6)[t])
                    for f in range(4):
                        mm = nc.tensor.transpose(out[:, f * P:(f + 1) * P], vva[:, f, t * P:(t + 1) * P], ident)
                    mm.then_inc(att["pe_to_scalar"], 1)
                for t in range(5):
                    out = take(4 + 2 * (t % 2))
                    pe.wait_ge(att["scalar_to_pe"], n(att["scalar_to_pe"]))
                    nc.tensor.matmul(out[:], halves, g_t[:, t % 2], start=True, stop=True).then_inc(att["pe_to_scalar"], 1)
                    out = take(5 + 2 * (t % 2))
                    pe.wait_ge(att["vector_to_pe"], n(att["vector_to_pe"]))
                    nc.tensor.matmul(out[:], turn, qa[:, t], start=True, stop=True).then_inc(att["pe_to_vector"], 1)
                pe.wait_ge(att["vector_to_pe"], n(att["vector_to_pe"]))
                out = take(6)
                nc.tensor.matmul(out[:], swap, qa[:, 4], start=True, stop=True).then_inc(att["pe_to_vector"], 1)
                for j in range(4):
                    out = take(j)
                    if j == 0:
                        pe.wait_ge(att["vector_to_pe"], n(att["vector_to_pe"]))
                    for t in range(TT):
                        for hh in range(2):
                            mm = nc.tensor.matmul(out[HEAD * hh:HEAD * hh + HEAD, t * P:(t + 1) * P],
                                                  vv_tok[:, t, (2 * j + hh) * HEAD:(2 * j + hh + 1) * HEAD],
                                                  sgw_t[:, 2 * j + hh], start=True, stop=True)
                    mm.then_inc(att["pe_to_vector"], 1)

                def scores(u):
                    h, t = u // TT, u % TT
                    r = HEAD * (h % 2)
                    keys = qa[r:r + HEAD, 4] if h // 4 == h % 2 else k_swap[r:r + HEAD]
                    out = take(4 + u % 2)
                    nc.tensor.matmul(out[:], qa[r:r + HEAD, h // 2, t * P:(t + 1) * P], keys, start=True, stop=True)\
                        .then_inc(att["pe_to_vector"], 1)

                scores(0)
                for u in range(8 * TT):
                    h, t = u // TT, u % TT
                    if u + 1 < 8 * TT:
                        scores(u + 1)
                    out = take(6 + u % 2)
                    pe.wait_ge(att["vector_to_pe"], n(att["vector_to_pe"]))
                    for s in range(TT):
                        mm = nc.tensor.transpose(out[:, s * P:(s + 1) * P], prob[:, u % 2, s * P:(s + 1) * P], ident)
                    mm.then_inc(att["pe_to_scalar"], 1)
                    if t == TT - 1:
                        if h % 2 == 0:
                            o = take(h // 2)
                        r = HEAD * (h % 2)
                        pe.wait_ge(att["scalar_to_pe"], n(att["scalar_to_pe"]))
                        for s in range(TT):
                            mm = nc.tensor.matmul(o[r:r + HEAD, :], v_tok[:, s, HEAD * (h // 4):HEAD * (h // 4) + HEAD],
                                                  prob_t[:, s], start=(s == 0), stop=(s == TT - 1))
                        mm.then_inc(att["pe_to_scalar"], 1)
                for v in range(2):
                    sums(g_t, 4)
                pe.wait_ge(h_ready, n(h_ready, KD))
                products(h_hi, h_lo, [8], 8)

            def conv_ffn(i):
                sums(sq_in, KD)
                pe.wait_ge(h_ready, n(h_ready, KD))
                products(h_hi, h_lo, [8], 2 * KF)
                pe.wait_ge(hid_ready, n(hid_ready, KF))
                products(hid_hi, hid_lo, DOWN, 8)

            for part in [ab, lambda: ffn(0), c, lambda: ffn(1), lambda: gated(0), lambda: conv_ffn(0),
                         lambda: gated(1), lambda: conv_ffn(1)][:upto]:
                part()
            pe.wait_ge(x_ready, KD * (1 + upto))
            for t in range(TT):
                for v in range(2):
                    out = take(4 + (2 * t + v) % 4)
                    for k in range(4):
                        mm = nc.tensor.transpose(out[:, k * P:(k + 1) * P], x[:, 4 * v + k, t * P:(t + 1) * P], ident)
                    mm.then_inc(out_turned, 1)

        @block.scalar
        def _(act):
            n = Count()
            at = {"split": 0, "bank": 0}

            def split():
                if at["split"] < N_SLABS:
                    s = at["split"] % RING
                    act.wait_ge(raw_full[s], n(raw_full[s], 16))
                    nc.scalar.activation(w_hi[:, s], w_raw[:, s], ACT.Copy).then_inc(hi_done, 1)
                    at["split"] += 1

            def slab():
                act.wait_ge(slab_done, n(slab_done))
                split()

            def turns(times, slabs, body, extra=()):
                dry = at["split"] + times * slabs > N_SLABS
                k = times - dry
                if k > 1:
                    per = [(slab_done, slabs)] + [(raw_full[s], 16 * slabs // RING) for s in range(RING)] + list(extra)
                    with n.loop(act, k, per) as i:
                        body(i)
                    at["split"] += (k - 1) * slabs
                elif k:
                    body(0)
                if dry:
                    body(times - 1)

            def turned_bank():
                at["bank"] += 1
                return (at["bank"] - 1) % RING

            def squares(src, dst, wait=None):
                for k in range(src.shape[1]):
                    if wait is not None:
                        act.wait_ge(wait, n(wait))
                    nc.scalar.activation(dst[:, k], src[:, k], ACT.Square).then_inc(sq_ready, 1)

            def deviation(width):
                act.wait_ge(stat_ready, n(stat_ready))
                nc.scalar.activation(rstd[:], bank[4][:], ACT.Sqrt, bias=eps[:, 0:1], scale=1.0 / width)\
                    .then_inc(std_ready, 1)

            def leave(y, sq, slabs):
                first = at["bank"]

                def body(i):
                    for t in range(RING):
                        for _ in range(slabs):
                            slab()
                        b = (first + t) % RING
                        k = bass.ds(i * RING + t, 1)
                        nc.scalar.activation(sq[:, k], bank[b][:].unsqueeze(1), ACT.Square).then_inc(sq_ready, 1)
                        nc.scalar.activation(y[:, k], bank[b][:].unsqueeze(1), ACT.Copy).then_inc(bank_free[b], 1)
                turns(2, RING * slabs, body)
                at["bank"] += KD
                deviation(D)

            def s5_prepare():
                v = [s5_v[:, i] for i in range(24)]
                act.wait_ge(s5_in_sem, 16 * 9)
                nc.scalar.activation(v[0], s5_ldt[:], ACT.Exp).then_inc(prep["scalar_to_vector"], 1)
                act.wait_ge(prep["vector_to_scalar"], n(prep["vector_to_scalar"]))
                nc.scalar.activation(v[7], v[1], ACT.Exp)
                nc.scalar.activation(s5_r8[:], v[1], ACT.Exp, scale=float(STEP))
                nc.scalar.activation(v[8], v[4], ACT.Sin)
                nc.scalar.activation(v[9], v[5], ACT.Sin).then_inc(prep["scalar_to_vector"], 1)
                for i in range(GROUPS // 4):
                    act.wait_ge(prep["pe_to_scalar"], n(prep["pe_to_scalar"]))
                    nc.scalar.activation(s5_in[:, 4 * i:4 * i + 4], bank[4 + i % 4][:].rearrange("p (g w) -> p g w", g=4),
                                         ACT.Copy).then_inc(bank_free[4 + i % 4], 1)
                act.wait_ge(prep["pe_to_scalar"], n(prep["pe_to_scalar"]))
                nc.scalar.activation(s5_k[:], bank[4][:].rearrange("p (g w) -> p g w", g=GROUPS), ACT.Copy)\
                    .then_inc(prep["scalar_to_pe"], 1)
                act.drain().then_inc(bank_free[4], 1)
                for j in range(STEP):
                    act.wait_ge(prep["pe_to_scalar"], n(prep["pe_to_scalar"]))
                    nc.scalar.activation(s5_conv[:, :, j], bank[5 + j % 3][:].rearrange("p (g w) -> p g w", g=GROUPS),
                                         ACT.Copy).then_inc(bank_free[5 + j % 3], 1)
                act.drain().then_inc(prep["scalar_to_vector"], 1)

            def s5_run():
                for i in range(4):
                    act.wait_ge(s5["pe_to_scalar"], n(s5["pe_to_scalar"]))
                    nc.scalar.activation(s5_state[:, 8 * i:8 * i + 8], bank[4 + i][:].rearrange("p (g c) -> p g c", g=8),
                                         ACT.Copy).then_inc(s5["scalar_to_pe"], 1)
                for i in range(4):
                    act.wait_ge(s5["pe_to_scalar"], n(s5["pe_to_scalar"]))
                    nc.scalar.activation(ys_step[:, 8 * i:8 * i + 8], bank[i][:].rearrange("p (g c) -> p g c", g=8),
                                         ACT.Copy).then_inc(bank_free[i], 1)
                act.drain().then_inc(ys_ready, 1)
                act.wait_ge(s5["vector_to_scalar"], n(s5["vector_to_scalar"]))
                nc.scalar.activation(yg[:], ys[:], ACT.Gelu_apprx_tanh).then_inc(s5["scalar_to_vector"], 1)
                for t in range(4):
                    slab()
                    nc.scalar.activation(gate[:, t], bank[turned_bank()][:], ACT.Sigmoid, bias=col("b_glu", t))\
                        .then_inc(s5["scalar_to_vector"], 1)

            def lstm_run():
                for k in range(4):
                    act.wait_ge(lstm["vector_to_scalar"], n(lstm["vector_to_scalar"]))
                    nc.scalar.activation(xc[:, k], xc[:, k], ACT.Silu).then_inc(lstm["scalar_to_pe"], 1)
                for k in range(4):
                    for v, (dst, scale) in enumerate(((qm, 1.0), (km, float(P) ** -0.5), (vf, 1.0), (vt, 1.0))):
                        act.wait_ge(lstm["pe_to_scalar"], n(lstm["pe_to_scalar"]))
                        to = dst[:, k] if v < 3 else dst[:, k].rearrange("p t w -> p (t w)")
                        nc.scalar.activation(to, bank[4 + v][:], ACT.Copy, scale=scale).then_inc(bank_free[4 + v], 1)
                act.drain().then_inc(lstm["scalar_to_pe"], 1)
                act.wait_ge(lstm["pe_to_scalar"], n(lstm["pe_to_scalar"], 2))
                i_b, f_b = lstm_bif[:, 0:1], lstm_bif[:, 1:2]
                r = [rowv[:, j] for j in range(8)]
                nc.scalar.activation(r[2], bank[5][0:M_HEADS, :], ACT.Abs, bias=f_b).then_inc(scalar_step, 1)
                nc.scalar.activation(r[1], bank[5][0:M_HEADS, :], ACT.Identity, bias=f_b).then_inc(bank_free[5], 1)
                nc.scalar.activation(r[0], bank[4][0:M_HEADS, :], ACT.Identity, bias=i_b).then_inc(bank_free[4], 1)
                act.wait_ge(scalar_step, n(scalar_step))
                nc.scalar.activation(r[3], r[2], ACT.Exp, scale=-1.0).then_inc(scalar_step, 1)
                act.wait_ge(scalar_step, n(scalar_step))
                nc.scalar.activation(r[4], r[3], ACT.Ln, bias=1.0).then_inc(lstm["scalar_to_vector"], 1)
                act.wait_ge(lstm["vector_to_scalar"], n(lstm["vector_to_scalar"]))
                nc.scalar.activation(r[5], r[4], ACT.Exp, scale=-1.0).then_inc(lstm["scalar_to_pe"], 1)
                for h in range(M_HEADS):
                    for v in range(2):
                        act.wait_ge(lstm["pe_to_scalar"], n(lstm["pe_to_scalar"]))
                        nc.scalar.activation(e_m[:, v], bank[4 + v][:], ACT.Copy).then_inc(lstm["scalar_to_vector"], 1)
                    for t in range(TT):
                        act.wait_ge(lstm["vector_to_scalar"], n(lstm["vector_to_scalar"]))
                        nc.scalar.activation(lstm_t[:, t, t * P:SEQ], lstm_t[:, t, t * P:SEQ], ACT.Exp)\
                            .then_inc(lstm["scalar_to_vector"], 1)
                    act.wait_ge(lstm["vector_to_scalar"], n(lstm["vector_to_scalar"]))
                    nc.scalar.activation(lstm_t[:, 0], lstm_t[:, 3], ACT.Square).then_inc(lstm["scalar_to_pe"], 1)
                    act.wait_ge(lstm["pe_to_scalar"], n(lstm["pe_to_scalar"]))
                    nc.scalar.activation(lstm_t[:, 1], bank[3][:], ACT.Sqrt, bias=eps[:, 0:1], scale=1.0 / P)\
                        .then_inc(lstm["scalar_to_vector"], 1)

            def ab():
                s5_prepare()
                act.wait_ge(prep["vector_to_scalar"], n(prep["vector_to_scalar"]))
                squares(x, sq_ab, x_ready)
                deviation(D)
                for t in range(12):
                    slab()
                    b = turned_bank()
                    if t < 4:
                        ins = nc.scalar.activation(xm[:, t], bank[b][:], ACT.Copy)
                    elif t < 8:
                        ins = nc.scalar.activation(zs[:, t - 4], bank[b][:], ACT.Silu)
                    else:
                        ins = nc.scalar.activation(us[:, t - 8], bank[b][:].rearrange("p (c i) -> p i c", i=STEP), ACT.Copy)
                    ins.then_inc(bank_free[b], 1)
                act.drain().then_inc(us_ready, 1)
                s5_run()
                lstm_run()
                leave(y_mix, sq_mix, 1)

            def ffn(i):
                squares(x, sq_in, x_ready)
                deviation(D)
                first = at["bank"]

                def body(i):
                    for p in range(2):
                        slab()
                        nc.scalar.activation(tmp[:, p], bank[(first + 2 * p) % RING][:], ACT.Silu).then_inc(act_for_dve, 1)
                        slab()
                turns(KF // 2, RING, body)
                at["bank"] += 2 * KF
                leave(y_ffn, sq_ffn, 3)

            def c():
                e = small[:, 0:16]
                act.wait_ge(hgrn["vector_to_scalar"], n(hgrn["vector_to_scalar"]))
                nc.scalar.activation(e, e, ACT.Exp).then_inc(hgrn["scalar_to_vector"], 1)
                squares(x, sq_in, x_ready)
                deviation(D)
                first = at["bank"]
                for dst, func in ((qc, ACT.Silu), (fc, ACT.Sigmoid), (ic, ACT.Copy), (gc, ACT.Silu)):
                    def body(i):
                        for t in range(RING):
                            slab()
                            b = (first + t) % RING
                            nc.scalar.activation(dst[:, bass.ds(i * RING + t, 1)], bank[b][:].unsqueeze(1), func)\
                                .then_inc(bank_free[b], 1)
                    turns(2, RING, body)
                    at["bank"] += 8
                with n.loop(act, C_HEADS, [(hgrn["vector_to_scalar"], 2), (hgrn["pe_to_scalar"], 4)]) as h:
                    nc.scalar.activation(c_i[:].unsqueeze(1), ic[:, bass.ds(h, 1)], ACT.Copy).then_inc(hgrn["scalar_to_pe"], 1)
                    act.wait_ge(hgrn["vector_to_scalar"], n(hgrn["vector_to_scalar"]))
                    nc.scalar.activation(c_f[:], c_f[:], ACT.Ln).then_inc(hgrn["scalar_to_vector"], 1)
                    act.wait_ge(hgrn["vector_to_scalar"], n(hgrn["vector_to_scalar"]))
                    nc.scalar.activation(c_e[:], c_b[:], ACT.Exp)
                    nc.scalar.activation(tmp[:, 0], c_d[:], ACT.Exp)
                    nc.scalar.activation(tmp[:, 1], c_d[:], ACT.Exp, scale=-1.0).then_inc(hgrn["scalar_to_vector"], 1)
                    act.wait_ge(hgrn["pe_to_scalar"], n(hgrn["pe_to_scalar"]))
                    nc.scalar.activation(c_it[:].rearrange("p t w -> p (t w)"), bank[4][:], ACT.Copy).then_inc(bank_free[4], 1)
                    act.wait_ge(hgrn["pe_to_scalar"], n(hgrn["pe_to_scalar"]))
                    nc.scalar.activation(c_kt[:].rearrange("p t w -> p (t w)"), bank[5][:], ACT.Copy).then_inc(bank_free[5], 1)
                    act.drain().then_inc(hgrn["scalar_to_pe"], 1)
                    act.wait_ge(hgrn["pe_to_scalar"], n(hgrn["pe_to_scalar"]))
                    nc.scalar.activation(c_o[:], bank[2][:], ACT.Square).then_inc(hgrn["scalar_to_pe"], 1)
                    act.wait_ge(hgrn["pe_to_scalar"], n(hgrn["pe_to_scalar"]))
                    nc.scalar.activation(tmp[:, 2], bank[3][:], ACT.Sqrt, bias=eps[:, 0:1], scale=1.0 / P)\
                        .then_inc(hgrn["scalar_to_vector"], 1)
                leave(y_mix, sq_mix, 1)

            def gated(i):
                squares(x, sq_in, x_ready)
                deviation(D)
                for t in range(14):
                    slab()
                    b = turned_bank()
                    dst = qa[:, t] if t < 5 else va[:] if t == 5 else ua[:, t - 6] if t < 10 else vva[:, t - 10]
                    nc.scalar.activation(dst, bank[b][:], ACT.Copy if t < 6 else ACT.Gelu_apprx_tanh).then_inc(bank_free[b], 1)
                act.drain().then_inc(att["scalar_to_pe"], 1)
                for v in range(2):
                    act.wait_ge(att["pe_to_scalar"], n(att["pe_to_scalar"]))
                    nc.scalar.activation(sgw_t[:, 4 * v:4 * v + 4].rearrange("p h w -> p (h w)"), bank[4 + v][:], ACT.Copy)\
                        .then_inc(bank_free[4 + v], 1)
                act.wait_ge(att["pe_to_scalar"], n(att["pe_to_scalar"]))
                nc.scalar.activation(v_tok[:].rearrange("p t w -> p (t w)"), bank[6][:], ACT.Copy).then_inc(bank_free[6], 1)
                for t in range(TT):
                    b = (7, 4, 5, 6)[t]
                    act.wait_ge(att["pe_to_scalar"], n(att["pe_to_scalar"]))
                    nc.scalar.activation(vv_tok[:, t], bank[b][:], ACT.Copy).then_inc(bank_free[b], 1)
                act.drain().then_inc(att["scalar_to_vector"], 1)
                for t in range(5):
                    nc.scalar.activation(g_t[:, t % 2], qa[:, t], ACT.Square).then_inc(att["scalar_to_pe"], 1)
                    act.wait_ge(att["pe_to_scalar"], n(att["pe_to_scalar"]))
                    nc.scalar.activation(g_t[:, 2 + t % 2], bank[4 + 2 * (t % 2)][:], ACT.Sqrt, bias=eps[:, 0:1], scale=1.0 / HEAD)\
                        .then_inc(att["scalar_to_vector"], 1)
                act.wait_ge(att["vector_to_scalar"], n(att["vector_to_scalar"]))
                nc.scalar.activation(g_small[:, 0:32], g_small[:, 0:32], ACT.Sqrt, bias=eps[:, 0:1], scale=1.0 / HEAD)\
                    .then_inc(att["scalar_to_vector"], 1)

                def exps(u):
                    act.wait_ge(att["vector_to_scalar"], n(att["vector_to_scalar"]))
                    nc.scalar.activation(prob[:, u % 2], bank[4 + u % 2][:], ACT.Exp, bias=g_small[:, 34 + u % 2:35 + u % 2],
                                         scale=HEAD ** -0.5, accum_out=g_small[:, 36 + u % 2:37 + u % 2])\
                        .then_inc(att["scalar_to_vector"], 1)

                exps(0)
                for u in range(8 * TT):
                    h, t = u // TT, u % TT
                    if u + 1 < 8 * TT:
                        exps(u + 1)
                    act.wait_ge(att["pe_to_scalar"], n(att["pe_to_scalar"]))
                    nc.scalar.activation(prob_t[:, :, t * P:(t + 1) * P], bank[6 + u % 2][:].rearrange("p (s w) -> p s w", s=TT),
                                         ACT.Copy).then_inc(bank_free[6 + u % 2], 1)
                    if t == TT - 1:
                        act.drain().then_inc(att["scalar_to_pe"], 1)
                        act.wait_ge(att["pe_to_scalar"], n(att["pe_to_scalar"]))
                        if h % 2:
                            nc.scalar.activation(oa[:, h // 2], bank[h // 2][:], ACT.Copy).then_inc(bank_free[h // 2], 1)
                act.drain().then_inc(scalar_step, 1)
                act.wait_ge(scalar_step, n(scalar_step))
                squares(oa, g_t)
                deviation(4 * P)
                act.wait_ge(att["vector_to_scalar"], n(att["vector_to_scalar"]))
                squares(ua, g_t)
                deviation(4 * P)
                stay(1)

            def stay(slabs):
                def body(i):
                    for _ in range(RING * slabs):
                        slab()
                turns(2, RING * slabs, body)
                at["bank"] += KD

            def conv_ffn(i):
                squares(x, sq_in, x_ready)
                deviation(D)
                first = at["bank"]
                base = i * 8 * KF

                def body(j):
                    for p in range(2):
                        for v in range(2):
                            slab()
                            k = j * 2 + (p + v * KF + base)
                            nc.scalar.activation(tmp[:, 2 * p + v], bank[(first + 2 * p + v) % RING][:], ACT.Identity,
                                                 scale=col_at("up_conv", k + 2 * KF), bias=col_at("up_conv", k + 6 * KF))\
                                .then_inc(act_for_dve, 1)
                        act.wait_ge(dve_for_act, n(dve_for_act))
                        nc.scalar.activation(tmp[:, 2 * p], tmp[:, 2 * p], ACT.Silu).then_inc(act_for_dve, 1)
                turns(KF // 2, RING, body, [(dve_for_act, 2)])
                at["bank"] += 2 * KF
                stay(3)

            act.wait_ge(eps_ready, 1)
            for _ in range(AHEAD):
                split()
            act.wait_ge(par_ready, 1)
            act.wait_ge(lstm_in, 16 * 6)
            for part in [ab, lambda: ffn(0), c, lambda: ffn(1), lambda: gated(0), lambda: conv_ffn(0),
                         lambda: gated(1), lambda: conv_ffn(1)][:upto]:
                part()

        @block.vector
        def _(dve):
            n = Count()
            at = {"split": 0, "bank": 0}

            def split():
                if at["split"] < N_SLABS:
                    s = at["split"] % RING
                    dve.wait_ge(hi_done, n(hi_done))
                    nc.vector.tensor_tensor(w_lo[:, s], w_raw[:, s], w_hi[:, s].bitcast(F32), ALU.subtract).then_inc(lo_done, 1)
                    at["split"] += 1

            def turns(times, slabs, body, extra=()):
                dry = at["split"] + times * slabs > N_SLABS
                k = times - dry
                if k > 1:
                    with n.loop(dve, k, [(slab_done, slabs), (hi_done, slabs)] + list(extra)) as i:
                        body(i)
                    at["split"] += (k - 1) * slabs
                elif k:
                    body(0)
                if dry:
                    body(times - 1)

            def step(ins):
                ins.then_inc(vector_step, 1)
                n(vector_step)

            def settle(s=vector_step):
                dve.wait_ge(s, n.now(s))

            def own(ins, s):
                ins.then_inc(s, 1)
                n(s)

            def flag(s):
                dve.drain().then_inc(s, 1)

            def tt(out, x0, x1, op):
                step(nc.vector.tensor_tensor(out, x0, x1, op))

            def ts(out, x0, s1, s2, op0, op1):
                if op1 is None:
                    step(nc.vector.tensor_scalar(out, x0, s1, None, op0))
                else:
                    step(nc.vector.tensor_scalar(out, x0, s1, s2, op0, op1))

            def stt(out, x0, sc, x1, op0, op1):
                step(nc.vector.scalar_tensor_tensor(out, x0, sc, x1, op0, op1))

            def inverse():
                dve.wait_ge(std_ready, n(std_ready))
                step(nc.vector.reciprocal(rinv[:], rstd[:]))
                settle()
                flag(bank_free[4])

            def parts_of_h(srcs, k0):
                for j, src in enumerate(srcs):
                    ts(h_hi[:, k0 + j], src, 1.0, None, ALU.mult, None)
                settle()
                for j, src in enumerate(srcs):
                    own(nc.vector.tensor_tensor(h_lo[:, k0 + j], src, h_hi[:, k0 + j].bitcast(F32), ALU.subtract), h_ready)
                settle(h_ready)

            def normal_h(src, gain, k0=0):
                inverse()
                for k in range(0, src.shape[1], 4):
                    for j in range(4):
                        stt(tmp[:, j], src[:, k + j], col(gain[0], gain[1] + k + j), rinv[:], ALU.mult, ALU.mult)
                    settle()
                    parts_of_h([tmp[:, j] for j in range(4)], k0 + k)

            def add_normal(y, gain):
                inverse()
                for k in range(0, KD, 4):
                    for j in range(4):
                        stt(tmp[:, j], y[:, k + j], col("norm", gain + k + j), rinv[:], ALU.mult, ALU.mult)
                    settle()
                    for j in range(4):
                        own(nc.vector.tensor_tensor(x[:, k + j], x[:, k + j], tmp[:, j], ALU.add), x_ready)
                    settle(x_ready)

            def only_split(slabs):
                for _ in range(slabs):
                    split()
                    n(slab_done)

            def leave(slabs):
                def body(i):
                    only_split(RING * slabs)
                turns(2, RING * slabs, body)
                at["bank"] += KD

            def s5_prepare():
                v = [s5_v[:, i] for i in range(24)]
                are = par[:, ROWS["a_re"]:ROWS["a_re"] + GROUPS]
                aim = par[:, ROWS["a_im"]:ROWS["a_im"] + GROUPS]
                for j in range(2):
                    dve.wait_ge(prep["pe_to_vector"], n(prep["pe_to_vector"]))
                    step(nc.vector.tensor_copy(s5_c[:, j], bank[5 + j][:].rearrange("p (g w) -> p g w", g=GROUPS)))
                    flag(bank_free[5 + j])
                dve.wait_ge(prep["scalar_to_vector"], n(prep["scalar_to_vector"]))
                settle()
                tt(v[1], v[0], are, ALU.mult)
                tt(v[2], v[0], aim, ALU.mult)
                settle()
                ts(v[3], v[2], 1.0 / TWO_PI, ROUND, ALU.mult, ALU.add)
                settle()
                ts(v[3], v[3], -ROUND, None, ALU.add, None)
                settle()
                stt(v[4], v[3], -PI_HIGH, v[2], ALU.mult, ALU.add)
                settle()
                stt(v[4], v[3], -PI_MID, v[4], ALU.mult, ALU.add)
                settle()
                stt(v[4], v[3], -PI_LOW, v[4], ALU.mult, ALU.add)
                settle()
                ts(v[4], v[4], PI_IN, -PI_IN, ALU.min, ALU.max)
                settle()
                ts(v[5], v[4], TWO_PI / 4, None, ALU.add, None)
                settle()
                ts(v[6], v[5], PI_IN, -TWO_PI, ALU.is_gt, ALU.mult)
                settle()
                tt(v[5], v[5], v[6], ALU.add)
                settle()
                nc.vector.tensor_scalar(v[5], v[5], PI_IN, -PI_IN, ALU.min, ALU.max).then_inc(prep["vector_to_scalar"], 1)
                dve.wait_ge(early_in, 16)
                dve.wait_ge(prep["scalar_to_vector"], n(prep["scalar_to_vector"]))
                tt(v[10], v[7], v[9], ALU.mult)
                tt(v[11], v[7], v[8], ALU.mult)
                tt(v[12], are, are, ALU.mult)
                tt(v[13], aim, aim, ALU.mult)
                settle()
                tt(v[12], v[12], v[13], ALU.add)
                ts(v[14], v[10], -1.0, None, ALU.add, None)
                settle()
                step(nc.vector.reciprocal(v[12], v[12]))
                tt(v[15], v[14], are, ALU.mult)
                tt(v[16], v[11], aim, ALU.mult)
                tt(v[17], v[11], are, ALU.mult)
                tt(v[18], v[14], aim, ALU.mult)
                settle()
                tt(v[15], v[15], v[16], ALU.add)
                tt(v[17], v[17], v[18], ALU.subtract)
                settle()
                tt(v[15], v[15], v[12], ALU.mult)
                tt(v[17], v[17], v[12], ALU.mult)
                settle()
                ts(v[16], v[17], sign, None, ALU.mult, None)
                settle()

                def over(t):
                    return t.unsqueeze(2).to_broadcast([P, GROUPS, GW])

                t0 = tmp[:, 0].rearrange("p (g w) -> p g w", g=GROUPS)
                t1 = tmp[:, 1].rearrange("p (g w) -> p g w", g=GROUPS)
                tt(s5_bb[:, 0], over(v[15]), s5_b[:, 0], ALU.mult)
                tt(t0, over(v[16]), s5_b[:, 1], ALU.mult)
                tt(s5_bb[:, 1], over(v[15]), s5_b[:, 1], ALU.mult)
                tt(t1, over(v[16]), s5_b[:, 0], ALU.mult)
                settle()
                tt(s5_bb[:, 0], s5_bb[:, 0], t0, ALU.add)
                tt(s5_bb[:, 1], s5_bb[:, 1], t1, ALU.subtract)
                re, im = s5_pow[:, 0], s5_pow[:, 1]
                step(nc.vector.memset(re[:, 0], 1.0))
                step(nc.vector.memset(im[:, 0], 0.0))
                step(nc.vector.tensor_copy(re[:, 1], v[10]))
                step(nc.vector.tensor_copy(im[:, 1], v[11]))
                settle()
                for m_ in (1, 2, 4):
                    def last(t):
                        return t[:, m_:m_ + 1].to_broadcast([P, m_, GROUPS])

                    t2 = tmp[:, 2].rearrange("p (k g) -> p k g", g=GROUPS)[:, 0:m_]
                    t3 = tmp[:, 3].rearrange("p (k g) -> p k g", g=GROUPS)[:, 0:m_]
                    a_, b_ = slice(1, m_ + 1), slice(m_ + 1, 2 * m_ + 1)
                    tt(re[:, b_], re[:, a_], last(re), ALU.mult)
                    tt(t2, im[:, a_], last(im), ALU.mult)
                    tt(im[:, b_], re[:, a_], last(im), ALU.mult)
                    tt(t3, im[:, a_], last(re), ALU.mult)
                    settle()
                    tt(re[:, b_], re[:, b_], t2, ALU.subtract)
                    tt(im[:, b_], im[:, b_], t3, ALU.add)
                    settle()
                ims = tmp[:, 2, 0:STEP * GROUPS].rearrange("p (k g) -> p k g", g=GROUPS)
                ts(ims, im[:, 0:STEP], sign, None, ALU.mult, None)
                settle()

                def powers(t):
                    return t.rearrange("p k g -> p g k").unsqueeze(3).to_broadcast([P, GROUPS, STEP, GW])

                def weights(t):
                    return t.unsqueeze(2).to_broadcast([P, GROUPS, STEP, GW])

                tt(s5_q[:], weights(s5_bb[:, 0]), powers(re[:, 0:STEP]), ALU.mult)
                tt(s5_big[:], weights(s5_bb[:, 1]), powers(ims), ALU.mult)
                settle()
                nc.vector.tensor_tensor(s5_q[:], s5_q[:], s5_big[:], ALU.add).then_inc(prep["vector_to_pe"], 1)
                step(nc.vector.tensor_scalar(s5_cx[:], s5_c[:, 0], sign, -1.0, ALU.mult, ALU.mult))
                settle()
                flag(prep["vector_to_pe"])
                tt(s5_out[:], weights(s5_cx[:]), powers(re[:, 1:STEP + 1]), ALU.mult)
                tt(s5_big[:], weights(s5_c[:, 1]), powers(im[:, 1:STEP + 1]), ALU.mult)
                settle()
                nc.vector.tensor_tensor(s5_out[:], s5_out[:], s5_big[:], ALU.subtract).then_inc(prep["vector_to_scalar"], 1)
                ec, es, t2, t3 = v[9], v[8], v[12], v[13]

                def square():
                    tt(t2, ec, ec, ALU.mult)
                    tt(t3, es, es, ALU.mult)
                    tt(es, ec, es, ALU.mult)
                    settle()
                    tt(ec, t2, t3, ALU.subtract)
                    ts(es, es, 2.0, None, ALU.mult, None)
                    settle()

                for _ in range(3):
                    square()
                step(nc.vector.memset(s5_cos[:, :, 0:1], 1.0))
                step(nc.vector.memset(s5_sin[:, :, 0:1], 0.0))
                settle()
                m_ = 1
                while m_ < CH:
                    def by(t):
                        return t.unsqueeze(2).to_broadcast([P, GROUPS, m_])

                    c0, s0, c1, s1 = (t[:, :, k] for t, k in ((s5_cos, slice(0, m_)), (s5_sin, slice(0, m_)),
                                                             (s5_cos, slice(m_, 2 * m_)), (s5_sin, slice(m_, 2 * m_))))
                    t0 = s5_t[:, :, 0:m_]
                    tt(c1, c0, by(ec), ALU.mult)
                    tt(t0, s0, by(es), ALU.mult)
                    tt(s1, c0, by(es), ALU.mult)
                    settle()
                    tt(c1, c1, t0, ALU.subtract)
                    settle()
                    tt(t0, s0, by(ec), ALU.mult)
                    settle()
                    tt(s1, s1, t0, ALU.add)
                    settle()
                    m_ *= 2
                    if m_ < CH:
                        square()
                ts(s5_sin[:], s5_sin[:], sign, -1.0, ALU.mult, ALU.mult)
                settle()
                dve.wait_ge(prep["scalar_to_vector"], n(prep["scalar_to_vector"]))

            def s5_run():
                def flat(t, i):
                    return t[:, 8 * i:8 * i + 8].rearrange("p g c -> p (g c)")

                for i in range(4):
                    dve.wait_ge(s5["pe_to_vector"], n(s5["pe_to_vector"]))
                    tt(flat(s5_w, i), bank[i][:], flat(s5_sin, i), ALU.mult)
                    tt(flat(s5_z, i), flat(s5_state, i), flat(s5_cos, i), ALU.mult)
                    settle()
                    flag(bank_free[i])
                    flag(bank_free[4 + i])
                    tt(flat(s5_w, i), flat(s5_w, i), flat(s5_z, i), ALU.add)
                settle()
                for g in range(GROUPS):
                    step(nc.vector.tensor_tensor_scan(s5_z[:, g], s5_r8[:, g:g + 1].to_broadcast([P, CH]), s5_w[:, g], 0.0,
                                                      ALU.mult, ALU.add))
                settle()
                flag(s5["vector_to_pe"])
                for i in range(4):
                    dve.wait_ge(s5["pe_to_vector"], n(s5["pe_to_vector"]))
                    tt(flat(s5_w, i), bank[4 + i][:], flat(s5_sin, i), ALU.mult)
                    tt(flat(s5_state, i), flat(s5_z, i), flat(s5_cos, i), ALU.mult)
                    settle()
                    flag(bank_free[4 + i])
                    nc.vector.tensor_tensor(flat(s5_state, i), flat(s5_state, i), flat(s5_w, i), ALU.subtract)\
                        .then_inc(s5["vector_to_pe"], 1)
                dve.wait_ge(ys_loaded, 16)
                for k in range(4):
                    step(nc.vector.scalar_tensor_tensor(ys[:, k], us[:, k].rearrange("p i c -> p (i c)"), col("s5_d", k),
                                                        ys[:, k], ALU.mult, ALU.add))
                settle()
                flag(s5["vector_to_scalar"])
                dve.wait_ge(s5["scalar_to_vector"], n(s5["scalar_to_vector"]))
                parts_of_h([yg[:, k] for k in range(4)], 0)
                for t in range(4):
                    split()
                    dve.wait_ge(slab_done, n(slab_done))
                    dve.wait_ge(s5["scalar_to_vector"], n(s5["scalar_to_vector"]))
                    tt(tmp[:, t].rearrange("p (c i) -> p i c", i=STEP), yg[:, t].rearrange("p (i c) -> p i c", i=STEP),
                       gate[:, t].rearrange("p (i c) -> p i c", i=STEP), ALU.mult)
                    flag(bank_free[at["bank"] % RING])
                    at["bank"] += 1
                settle()
                parts_of_h([tmp[:, t] for t in range(4)], 4)

            def lstm_run():
                dve.wait_ge(lstm_in, 16 * 6)
                for v in range(3):
                    tt(lstm_bd[:, v].rearrange("p t (n e) -> p t n e", e=4),
                       lstm_w4[:, v].unsqueeze(2).to_broadcast([P, 4, 32, 4]),
                       quad.unsqueeze(1).unsqueeze(3).to_broadcast([P, 4, 32, 4]), ALU.mult)
                for k in range(4):
                    ts(xc[:, k], xm[:, k], col("conv_w", 12 + k), col("conv_b", k), ALU.mult, ALU.add)
                settle()
                for j in (1, 2, 3):
                    for k in range(4):
                        stt(xc[:, k, j:SEQ], xm[:, k, 0:SEQ - j], col("conv_w", 4 * (3 - j) + k), xc[:, k, j:SEQ],
                            ALU.mult, ALU.add)
                    settle()
                for k in range(4):
                    flag(lstm["vector_to_scalar"])
                r = [rowv[:, j] for j in range(8)]
                dve.wait_ge(lstm["scalar_to_vector"], n(lstm["scalar_to_vector"]))
                stt(r[5], r[1], 0.0, r[4], ALU.min, ALU.subtract)
                settle()
                step(nc.vector.tensor_tensor_scan(r[6], ones[0:M_HEADS, 0:1].to_broadcast([M_HEADS, SEQ]), r[5], 0.0,
                                                  ALU.mult, ALU.add))
                settle()
                tt(r[7], r[0], r[6], ALU.subtract)
                settle()
                step(nc.vector.tensor_tensor_scan(r[2], r[7], r[7], 0.0, ALU.max, ALU.max))
                settle()
                ts(r[3], r[2], -1.0, None, ALU.mult, None)
                tt(r[4], r[6], r[2], ALU.add)
                settle()
                flag(lstm["vector_to_pe"])
                flag(lstm["vector_to_scalar"])
                dve.wait_ge(lstm["pe_to_vector"], n(lstm["pe_to_vector"]))
                step(nc.vector.tensor_copy(g_col, bank[6][:, 0:16].rearrange("p (s h) -> p s h", s=TT)))
                settle()
                flag(bank_free[6])
                for h in range(M_HEADS):
                    dve.wait_ge(lstm["scalar_to_vector"], n(lstm["scalar_to_vector"], 2))
                    flag(bank_free[4])
                    flag(bank_free[5])
                    for t in range(TT):
                        nc.vector.tensor_scalar(lstm_t[:, t, t * P:SEQ], e_m[:, 0, t * P:SEQ], g_col[:, t, h:h + 1], 0.0,
                                                ALU.add, ALU.min).then_inc(lstm["vector_to_scalar"], 1)
                    for t in range(TT):
                        dve.wait_ge(lstm["pe_to_vector"], n(lstm["pe_to_vector"]))
                        dve.wait_ge(lstm["scalar_to_vector"], n(lstm["scalar_to_vector"]))
                        tt(sc_m[:, t, t * P:SEQ], bank[6 + t % 2][:, 0:SEQ - t * P], lstm_t[:, t, t * P:SEQ], ALU.mult)
                        settle()
                        flag(bank_free[6 + t % 2])
                        nc.vector.tensor_tensor(sc_m[:, t, t * P:(t + 1) * P], sc_m[:, t, t * P:(t + 1) * P], causal, ALU.mult)\
                            .then_inc(lstm["vector_to_pe"], 1)
                    dve.wait_ge(lstm["pe_to_vector"], n(lstm["pe_to_vector"]))
                    stt(lstm_t[:, 0], bank[1][:], -1.0, e_m[:, 1], ALU.mult, ALU.max)
                    settle()
                    tt(lstm_t[:, 0], bank[1][:], lstm_t[:, 0], ALU.max)
                    settle()
                    step(nc.vector.reciprocal(lstm_t[:, 1], lstm_t[:, 0]))
                    settle()
                    tt(lstm_t[:, 2], bank[0][:], lstm_t[:, 1], ALU.mult)
                    settle()
                    flag(lstm["vector_to_pe"])
                    flag(bank_free[0])
                    flag(bank_free[1])
                    dve.wait_ge(lstm["pe_to_vector"], n(lstm["pe_to_vector"]))
                    stt(lstm_t[:, 3], bank[2][:], -1.0 / P, lstm_t[:, 2], ALU.mult, ALU.add)
                    settle()
                    flag(lstm["vector_to_scalar"])
                    flag(bank_free[2])
                    ts(tmp[:, 0], xc[:, h], col("skip", h), None, ALU.mult, None)
                    dve.wait_ge(lstm["scalar_to_vector"], n(lstm["scalar_to_vector"]))
                    flag(bank_free[3])
                    step(nc.vector.reciprocal(tmp[:, 1], lstm_t[:, 1]))
                    settle()
                    tt(tmp[:, 2], lstm_t[:, 3], tmp[:, 1], ALU.mult)
                    settle()
                    stt(tmp[:, 2], tmp[:, 2], col("mh_gain", h), tmp[:, 0], ALU.mult, ALU.add)
                    settle()
                    tt(tmp[:, 3], tmp[:, 2], zs[:, h], ALU.mult)
                    settle()
                    parts_of_h([tmp[:, 3]], h)

            def ab():
                s5_prepare()
                normal_h(x, ("norm", 0))
                only_split(12)
                at["bank"] += 12
                s5_run()
                lstm_run()
                leave(1)
                add_normal(y_mix, 8)

            def ffn(i):
                normal_h(x, ("norm", 32 * i + 16))
                first = at["bank"]

                def body(j):
                    for p in range(2):
                        only_split(2)
                        g, u = (first + 2 * p) % RING, (first + 2 * p + 1) % RING
                        dve.wait_ge(slab_done, n.now(slab_done))
                        dve.wait_ge(act_for_dve, n(act_for_dve))
                        k = bass.ds(j * 2 + p, 1)
                        tt(tmp[:, 2 + p], bank[u][:], tmp[:, p], ALU.mult)
                        flag(bank_free[g])
                        flag(bank_free[u])
                        settle()
                        ts(hid_hi[:, k], tmp[:, 2 + p:3 + p], 1.0, None, ALU.mult, None)
                        settle()
                        own(nc.vector.tensor_tensor(hid_lo[:, k], tmp[:, 2 + p:3 + p], hid_hi[:, k].bitcast(F32), ALU.subtract),
                            hid_ready)
                        settle(hid_ready)
                turns(KF // 2, RING, body, [(act_for_dve, 2), (vector_step, 4), (hid_ready, 2)])
                at["bank"] += 2 * KF
                leave(3)
                add_normal(y_ffn, 32 * i + 24)

            def c():
                e, w = small[:, 0:16], small[:, 16:32]
                r0, r1 = (par[:, ROWS["lb_raw"] + 8 * j:ROWS["lb_raw"] + 8 * j + 8] for j in range(2))
                tt(w[:, 0:8], r0, r1, ALU.max)
                settle()
                tt(e[:, 0:8], r0, w[:, 0:8], ALU.subtract)
                tt(e[:, 8:16], r1, w[:, 0:8], ALU.subtract)
                settle()
                flag(hgrn["vector_to_scalar"])
                dve.wait_ge(hgrn["scalar_to_vector"], n(hgrn["scalar_to_vector"]))
                tt(w[:, 0:8], e[:, 0:8], e[:, 8:16], ALU.add)
                settle()
                step(nc.vector.reciprocal(w[:, 8:16], w[:, 0:8]))
                settle()
                tt(e[:, 0:8], e[:, 0:8], w[:, 8:16], ALU.mult)
                tt(e[:, 8:16], e[:, 8:16], w[:, 8:16], ALU.mult)
                settle()
                tt(w[:, 0:8], e[:, 0:8], e[:, 8:16], ALU.add)
                settle()
                tt(lb[:, 0], w[:, 0:8], e[:, 0:8], ALU.subtract)
                settle()
                ts(lb[:, 1], lb[:, 0], -1.0, 1.0, ALU.mult, ALU.add)
                ts(lb[:, 2], lb[:, 0], 1.0, None, ALU.subtract, None)
                settle()
                normal_h(x, ("norm", 32))
                for j in range(4):
                    def body(i):
                        only_split(RING)
                    turns(2, RING, body)
                    at["bank"] += 8
                chunk = 8
                decay = small[:, 32:40]
                per = [(hgrn["scalar_to_vector"], 3), (hgrn["pe_to_vector"], 2), (vector_step, 18), (h_ready, 1)]
                with n.loop(dve, C_HEADS, per) as h:
                    k = bass.ds(h, 1)
                    low, free, less = lb[:, 0, k], lb[:, 1, k], lb[:, 2, k]
                    ts(c_k[:].unsqueeze(1), fc[:, k], less, free, ALU.mult, ALU.add)
                    nc.vector.tensor_scalar(c_f[:].unsqueeze(1), fc[:, k], free, low, ALU.mult, ALU.add)\
                        .then_inc(hgrn["vector_to_scalar"], 1)
                    dve.wait_ge(hgrn["scalar_to_vector"], n(hgrn["scalar_to_vector"]))
                    step(nc.vector.tensor_tensor_scan(c_b[:], restart, c_f[:], 0.0, ALU.mult, ALU.add))
                    settle()
                    b3 = c_b[:].rearrange("p (c t) -> p c t", c=chunk)
                    nc.vector.tensor_tensor(c_d[:].rearrange("p (c t) -> p c t", c=chunk), b3,
                                            b3[:, :, C_CHUNK - 1:C_CHUNK].to_broadcast([P, chunk, C_CHUNK]), ALU.subtract)\
                        .then_inc(hgrn["vector_to_scalar"], 1)
                    dve.wait_ge(hgrn["scalar_to_vector"], n(hgrn["scalar_to_vector"]))
                    step(nc.vector.tensor_copy(decay, c_e[:].rearrange("p (c t) -> p c t", c=chunk)[:, :, C_CHUNK - 1]))
                    settle()
                    tt(c_e[:].unsqueeze(1), qc[:, k], c_e[:].unsqueeze(1), ALU.mult)
                    tt(c_d[:].unsqueeze(1), qc[:, k], tmp[:, 0:1], ALU.mult)
                    tt(c_k[:], c_k[:], tmp[:, 1], ALU.mult)
                    flag(hgrn["vector_to_pe"])
                    dve.wait_ge(hgrn["pe_to_vector"], n(hgrn["pe_to_vector"]))
                    tt(c_s[:], bank[6][:].rearrange("p (t w) -> p t w", t=TT), causal_c.unsqueeze(1).to_broadcast([P, TT, P]),
                       ALU.mult)
                    flag(bank_free[6])
                    flag(hgrn["vector_to_pe"])
                    dve.wait_ge(hgrn["pe_to_vector"], n(hgrn["pe_to_vector"]))
                    step(nc.vector.tensor_copy(c_state[:, 1], bank[0][:, 0:P]))
                    for j in range(1, 7):
                        settle()
                        stt(c_state[:, j + 1], c_state[:, j], decay[:, j:j + 1], bank[j % 2][:, (j // 2) * P:(j // 2 + 1) * P],
                            ALU.mult, ALU.add)
                    flag(bank_free[0])
                    flag(bank_free[1])
                    flag(hgrn["vector_to_pe"])
                    dve.wait_ge(hgrn["scalar_to_vector"], n(hgrn["scalar_to_vector"]))
                    step(nc.vector.reciprocal(tmp[:, 3], tmp[:, 2]))
                    flag(bank_free[3])
                    settle()
                    tt(tmp[:, 1], bank[2][:], tmp[:, 3], ALU.mult)
                    flag(bank_free[2])
                    settle()
                    stt(tmp[:, 0:1], tmp[:, 1:2], col_at("c_gain", h), gc[:, k], ALU.mult, ALU.mult)
                    settle()
                    ts(h_hi[:, k], tmp[:, 0:1], 1.0, None, ALU.mult, None)
                    settle()
                    own(nc.vector.tensor_tensor(h_lo[:, k], tmp[:, 0:1], h_hi[:, k].bitcast(F32), ALU.subtract), h_ready)
                    settle(h_ready)
                leave(1)
                add_normal(y_mix, 40)

            def gated(i):
                normal_h(x, ("attn_norm", 8 * i))
                only_split(14)
                at["bank"] += 14
                dve.wait_ge(late_in, 16 * 11 * (i + 1))
                dve.wait_ge(att["scalar_to_vector"], n(att["scalar_to_vector"]))
                for t in range(5):
                    dve.wait_ge(att["scalar_to_vector"], n(att["scalar_to_vector"]))
                    flag(bank_free[4 + 2 * (t % 2)])
                    step(nc.vector.reciprocal(tmp[:, 0], g_t[:, 2 + t % 2]))
                    settle()
                    nc.vector.scalar_tensor_tensor(qa[:, t], qa[:, t], col("q_norm" if t < 4 else "k_norm", i), tmp[:, 0],
                                                   ALU.mult, ALU.mult).then_inc(att["vector_to_pe"], 1)
                    dve.wait_ge(att["pe_to_vector"], n(att["pe_to_vector"]))
                    tt(tmp[:, 1], bank[5 + 2 * (t % 2)][:], sin, ALU.mult)
                    tt(qa[:, t], qa[:, t], cos, ALU.mult)
                    settle()
                    flag(bank_free[5 + 2 * (t % 2)])
                    tt(qa[:, t], qa[:, t], tmp[:, 1], ALU.add)
                settle()
                flag(att["vector_to_pe"])
                dve.wait_ge(att["pe_to_vector"], n(att["pe_to_vector"]))
                step(nc.vector.tensor_copy(k_swap[:], bank[6][:]))
                settle()
                flag(bank_free[6])
                for t in range(TT):
                    tt(tmp[:, t], vv_tok[:, t], vv_tok[:, t], ALU.mult)
                settle()
                for t in range(TT):
                    step(nc.vector.tensor_reduce(g_small[:, 8 * t:8 * t + 8], tmp[:, t].rearrange("p (h d) -> p h d", h=8),
                                                 AX.X, ALU.add))
                settle()
                flag(att["vector_to_scalar"])
                dve.wait_ge(att["scalar_to_vector"], n(att["scalar_to_vector"]))
                step(nc.vector.reciprocal(g_small[:, 0:32], g_small[:, 0:32]))
                settle()
                for t in range(TT):
                    tt(vv_tok[:, t].rearrange("p (h d) -> p h d", h=8), vv_tok[:, t].rearrange("p (h d) -> p h d", h=8),
                       g_small[:, 8 * t:8 * t + 8].unsqueeze(2).to_broadcast([P, 8, HEAD]), ALU.mult)
                settle()
                for t in range(TT):
                    tt(vv_tok[:, t], vv_tok[:, t], sgn[:], ALU.mult)
                settle()
                flag(att["vector_to_pe"])
                for j in range(4):
                    dve.wait_ge(att["pe_to_vector"], n(att["pe_to_vector"]))
                    tt(tmp[:, j].rearrange("p (c w) -> p c w", c=TT), bank[j][:].rearrange("p (c w) -> p c w", c=TT),
                       sgb[:, j].unsqueeze(1).to_broadcast([P, TT, P]), ALU.add)
                    settle()
                    flag(bank_free[j])
                    tt(ua[:, j], ua[:, j], tmp[:, j], ALU.mult)
                settle()

                def maxima(u):
                    dve.wait_ge(att["pe_to_vector"], n(att["pe_to_vector"]))
                    step(nc.vector.tensor_reduce(g_small[:, 32 + u % 2:33 + u % 2], bank[4 + u % 2][:], AX.X, ALU.max))
                    settle()
                    nc.vector.tensor_scalar(g_small[:, 34 + u % 2:35 + u % 2], g_small[:, 32 + u % 2:33 + u % 2], -HEAD ** -0.5,
                                            None, ALU.mult).then_inc(att["vector_to_scalar"], 1)

                maxima(0)
                for u in range(8 * TT):
                    if u + 1 < 8 * TT:
                        maxima(u + 1)
                    dve.wait_ge(att["scalar_to_vector"], n(att["scalar_to_vector"]))
                    flag(bank_free[4 + u % 2])
                    step(nc.vector.reciprocal(g_small[:, 38 + u % 2:39 + u % 2], g_small[:, 36 + u % 2:37 + u % 2]))
                    settle()
                    nc.vector.tensor_scalar(prob[:, u % 2], prob[:, u % 2], g_small[:, 38 + u % 2:39 + u % 2], None, ALU.mult)\
                        .then_inc(att["vector_to_pe"], 1)
                normal_h(oa, ("attn_gain", 4 * i), 0)
                flag(att["vector_to_scalar"])
                normal_h(ua, ("sg_gain", 4 * i), 4)
                add_result(1)

            def add_result(slabs):
                first = at["bank"]

                def body(i):
                    for t in range(RING):
                        only_split(slabs)
                        b = (first + t) % RING
                        dve.wait_ge(slab_done, n.now(slab_done))
                        k = bass.ds(i * RING + t, 1)
                        own(nc.vector.tensor_tensor(x[:, k], x[:, k], bank[b][:].unsqueeze(1), ALU.add), x_ready)
                        flag(bank_free[b])
                turns(2, RING * slabs, body, [(x_ready, RING)])
                at["bank"] += KD

            def conv_ffn(i):
                normal_h(x, ("ffn_norm", 8 * i))
                first = at["bank"]
                base = i * 8 * KF

                def body(j):
                    for p in range(2):
                        only_split(2)
                        for v in range(2):
                            b = (first + 2 * p + v) % RING
                            k = j * 2 + (p + v * KF + base)
                            c_ = tmp[:, 2 * p + v]
                            dve.wait_ge(act_for_dve, n(act_for_dve))
                            stt(c_[:, 1:SEQ], bank[b][:, 0:SEQ - 1], col_at("up_conv", k), c_[:, 1:SEQ], ALU.mult, ALU.add)
                            settle()
                            ins = nc.vector.scalar_tensor_tensor(c_[:, 0:SEQ - 1], bank[b][:, 1:SEQ],
                                                                 col_at("up_conv", k + 4 * KF), c_[:, 0:SEQ - 1], ALU.mult, ALU.add)
                            if v == 0:
                                ins.then_inc(dve_for_act, 1)
                            else:
                                step(ins)
                        settle()
                        dve.wait_ge(act_for_dve, n(act_for_dve))
                        kk = bass.ds(j * 2 + p, 1)
                        tt(tmp[:, 2 * p + 1], tmp[:, 2 * p], tmp[:, 2 * p + 1], ALU.mult)
                        settle()
                        ts(hid_hi[:, kk], tmp[:, 2 * p + 1:2 * p + 2], 1.0, None, ALU.mult, None)
                        settle()
                        own(nc.vector.tensor_tensor(hid_lo[:, kk], tmp[:, 2 * p + 1:2 * p + 2], hid_hi[:, kk].bitcast(F32),
                                                    ALU.subtract), hid_ready)
                        flag(bank_free[(first + 2 * p) % RING])
                        flag(bank_free[(first + 2 * p + 1) % RING])
                        settle(hid_ready)
                turns(KF // 2, RING, body, [(act_for_dve, 6), (vector_step, 10), (hid_ready, 2)])
                at["bank"] += 2 * KF
                add_result(3)

            nc.vector.memset(eps[:], EPS).then_inc(eps_ready, 1)
            for b in range(8):
                flag(bank_free[b])
            for k in range(KD):
                dve.wait_ge(x_turned, n(x_turned))
                step(nc.vector.tensor_copy(x[:, k], bank[k % RING][:]))
                settle()
                flag(bank_free[k % RING])
                own(dve.drain(), x_ready)
            at["bank"] += KD
            for b in range(ROW_BLOCKS):
                dve.wait_ge(par_turned, n(par_turned))
                r = block_rows(b)
                step(nc.vector.tensor_copy(par[:, b * P:b * P + r], bank[4 + b % 4][:, 0:r]))
                settle()
                flag(bank_free[4 + b % 4])
            flag(par_ready)
            for _ in range(AHEAD):
                split()
            for part in [ab, lambda: ffn(0), c, lambda: ffn(1), lambda: gated(0), lambda: conv_ffn(0),
                         lambda: gated(1), lambda: conv_ffn(1)][:upto]:
                part()
            for t in range(TT):
                for v in range(2):
                    b = 4 + (2 * t + v) % 4
                    dve.wait_ge(out_turned, n(out_turned))
                    step(nc.vector.tensor_copy(out_tok[:, t, 512 * v:512 * v + 512], bank[b][:]))
                    settle()
                    flag(bank_free[b])
                    flag(out_ready)


_NAMES = ["x", "norm_g", "ab_w_in", "ab_conv_w", "ab_conv_b", "ab_wq", "ab_wk", "ab_wv", "ab_w_if", "ab_b_if", "ab_mh_gain",
          "ab_skip", "ab_a_re", "ab_a_im", "ab_log_dt", "ab_b_re", "ab_b_im", "ab_c_re", "ab_c_im", "ab_d", "ab_w_glu",
          "ab_b_glu", "ab_w_out", "c_w_in", "c_lb_raw", "c_g_gain", "c_w_out", "ffn_w1", "ffn_w3", "ffn_w2",
          "attn_norm_g_2", "w_in_2", "q_norm_g_2", "k_norm_g_2", "sg_norm_g_2", "sg_w_2", "sg_b_2", "attn_out_g_2",
          "sg_out_g_2", "w_o_2", "ffn_norm_g_2", "w_up_2", "conv_w_2", "conv_b_2", "w_down_2"]


def kernel(**inputs):
    import concourse.bacc as bacc
    from concourse.bass_utils import run_bass_kernel_spmd

    nc = bacc.Bacc("TRN2", target_bir_lowering=False, num_devices=1)
    arrays = {f"in_{k}": np.ascontiguousarray(inputs[k]) for k in _NAMES}
    arrays.update({f"in_{k}": v for k, v in constants().items()})
    aps = {k[3:]: nc.dram_tensor(k, v.shape, F32, kind="ExternalInput").ap() for k, v in arrays.items()}
    aps["out"] = nc.dram_tensor("out_x", (1, SEQ, D), F32, kind="ExternalOutput").ap()
    program(nc, aps, UPTO)
    r = run_bass_kernel_spmd(nc, [arrays], core_ids=[0])
    return r.results[0]["out_x"]


UPTO = 8
```

```python
from contextlib import ExitStack, contextmanager

import numpy as np

import concourse.bass as bass
from concourse import mybir

F32 = mybir.dt.float32
F32R = mybir.dt.float32r
ALU = mybir.AluOpType
ACT = mybir.ActivationFunctionType
AX = mybir.AxisListType

P = 128
SEQ = 512
D = 1024
KD = D // P
TT = SEQ // P
D_FF = 2816
KF = D_FF // P
EPS = 1e-6
UNITS = 8 * TT
MIX_AT = (8, 12, 16, 20)
IN_ORDER = [4, 5, 0, 1, 2, 3, 10, 11, 12, 13, 6, 7, 8, 9]
RING = 4
AHEAD = 4
GROUP = 3
SLAB_K = 8
DOWN = [8, 8, KF - 16]
M_HEADS = 4
GROUPS, GW, STATE = 32, 16, 64
STEP = 8
CH = SEQ // STEP
C_HEADS = 8
C_CHUNK = 64
HEAD = 64
IN2 = 1792
TWO_PI = float(2 * np.pi)
PI_HIGH = 6.28125
PI_MID = float(np.float32(2 * np.pi - 6.28125))
PI_LOW = float(2 * np.pi - 6.28125 - np.float64(np.float32(2 * np.pi - 6.28125)))
ROUND = 1.5 * 2.0 ** 23
HUGE = 3.0e38
PI_IN = 3.1415925

ROWS = {}


def plan_rows():
    at = 0
    for name, count in (("norm", 64), ("attn_norm", 16), ("ffn_norm", 16), ("conv_w", 16), ("conv_b", 4),
                        ("mh_gain", 4), ("skip", 4), ("s5_d", 4),
                        ("b_glu", 4), ("lb_raw", 16), ("c_gain", 8), ("attn_gain", 8), ("sg_gain", 8),
                        ("q_norm", 2), ("k_norm", 2), ("a_re", 32), ("a_im", 32),
                        ("pad", 16), ("up_conv", 2 * 4 * 2 * KF)):
        ROWS[name] = at
        at += count
    return at


N_ROWS = plan_rows()
ROW_BLOCKS = -(-N_ROWS // P)


def constants():
    k = np.arange(P)
    zid = np.zeros((P, 2 * P), np.float32)
    zid[k, P + k] = 1
    lead = np.concatenate([zid, np.ones((P, P), np.float32)], 1)
    quad = (k[:, None] // 4 == np.arange(32)[None, :]).astype(np.float32)
    pick = np.zeros((P, M_HEADS, P), np.float32)
    for h in range(M_HEADS):
        pick[h, h] = 1
    causal = (k[:, None] <= k[None, :]).astype(np.float32)
    causal_c = causal * (k[:, None] // C_CHUNK == k[None, :] // C_CHUNK)
    restart = np.broadcast_to((np.arange(SEQ) % C_CHUNK != 0).astype(np.float32), (P, SEQ))
    swap = (k[:, None] == (k[None, :] + HEAD) % P).astype(np.float32)
    sign = np.where(k < HEAD, -1.0, 1.0).astype(np.float32)[:, None]
    early = np.concatenate([quad, pick.reshape(P, -1), causal, causal_c, restart, swap, sign], 1)
    inv = (1.0 / (np.float32(10000.0) ** (np.arange(0, 32, 2, dtype=np.float32) / np.float32(32)))).astype(np.float32)
    t = np.arange(SEQ)
    within = k % HEAD
    pos = np.where((within < 32)[:, None], (t // 64)[None, :], (t % 64)[None, :]).astype(np.float32)
    ang = pos * inv[within % 16][:, None]
    upper = (within % 32) >= 16
    cos = np.cos(ang).astype(np.float32)
    sin = (np.sin(ang) * np.where(upper, 1, -1)[:, None]).astype(np.float32)
    partner = np.where(upper, k - 16, k + 16)
    turn = (k[:, None] == partner[None, :]).astype(np.float32)
    block = (k[:, None] // HEAD == k[None, :] // HEAD).astype(np.float32)
    late = np.concatenate([cos, sin, turn, block], 1)
    return {"lead": lead, "early": np.ascontiguousarray(early), "late": late}


class Count:

    def __init__(self):
        self.seen, self.shift = {}, {}

    def __call__(self, sem, by=1):
        self.seen[sem.name] = self.seen.get(sem.name, 0) + by
        return self.now(sem)

    def now(self, sem):
        value = self.seen.get(sem.name, 0)
        return value if sem.name not in self.shift else self.shift[sem.name] + value

    @contextmanager
    def loop(self, eng, times, per):
        before = dict(self.seen)
        with eng.Fori(0, times) as i:
            self.shift = {sem.name: i * by for sem, by in per}
            yield i
        self.shift = {}
        turn = {k: v - before.get(k, 0) for k, v in self.seen.items() if v != before.get(k, 0)}
        want = {sem.name: by for sem, by in per}
        assert turn == want, f"per turn {turn}, not {want}"
        for k, v in want.items():
            self.seen[k] += (times - 1) * v


def program(nc, a, upto):
    ctx = ExitStack()
    with ctx:
        top = [-(-nc.sbuf_base // 64) * 64]

        def place(name, shape, dt=F32, at=None):
            size = 4 * int(np.prod(shape[1:]))
            if at is None:
                at = top[0]
                top[0] += -(-size // 32) * 32
                assert top[0] <= nc.sbuf_usable_end, (name, top[0])
            return nc.alloc_sbuf_tensor_at(name, list(shape), dt, offset=at)

        def sem(name):
            return ctx.enter_context(nc.semaphore(name))

        w_raw = place("w_raw", [P, RING, SLAB_K, P])
        w_hi = place("w_hi", [P, RING, SLAB_K, P], F32R)
        w_lo = place("w_lo", [P, RING, SLAB_K, P], F32R)
        x = place("x", [P, KD, SEQ])
        H0 = top[0]
        h_hi = place("h_hi", [P, KD, SEQ], F32R)
        h_lo = place("h_lo", [P, KD, SEQ], F32R)
        M0 = top[0]
        hid_hi = place("hid_hi", [P, KF, SEQ], F32R)
        hid_lo = place("hid_lo", [P, KF, SEQ], F32R)
        M1 = top[0]
        par = place("par", [P, ROW_BLOCKS * P])
        lead = place("lead", [P, 3 * P])
        shifted, ident, ones = lead[:, 0:2 * P], lead[:, P:2 * P], lead[:, 2 * P:3 * P]
        early = place("early", [P, 32 + 4 * P + 2 * P + SEQ + P + 1])
        quad = early[:, 0:32]
        pick = early[0:M_HEADS, 32:32 + 4 * P].rearrange("k (h m) -> k h m", h=M_HEADS)
        causal = early[:, 544:672]
        causal_c = early[:, 672:800]
        restart = early[:, 800:1312]
        swap = early[:, 1312:1440]
        sign = early[:, 1440:1441]
        eps = place("eps", [P, 1])
        sq_sum = place("sq_sum", [P, SEQ])
        dev = place("dev", [P, TT])
        inv = place("inv", [P, TT])
        warm = place("warm", [P, 1])
        tmp = place("tmp", [P, 4, SEQ])
        small = place("small", [P, 256])
        lstm_w4 = place("lstm_w4", [P, 3, 4, 4])
        lstm_wif = place("lstm_wif", [P, 12, 8])
        lstm_bif = place("lstm_bif", [M_HEADS, 2])
        lb = place("lb", [P, 8, 8])

        def m(name, shape, kb, dt=F32):
            assert M0 + 1024 * kb + 4 * int(np.prod(shape[1:])) <= M1, name
            return place(name, shape, dt, at=M0 + int(1024 * kb))

        def hm(name, shape, kb):
            assert H0 + 1024 * kb + 4 * int(np.prod(shape[1:])) <= M0, name
            return place(name, shape, F32, at=H0 + int(1024 * kb))

        x_tok = m("x_tok", [P, TT, D], 0)
        rows = m("rows", [P, ROW_BLOCKS, P], 16)
        out_tok = m("out_tok", [P, TT, D], 0)
        sq_ab = m("sq_ab", [P, KD, SEQ], 0)
        sq_in = m("sq_in", [P, KD, SEQ], 64)
        y_mix = m("y_mix", [P, KD, SEQ], 64)
        sq_mix = m("sq_mix", [P, KD, SEQ], 0)
        y_ffn = hm("y_ffn", [P, KD, SEQ], 0)
        sq_ffn = hm("sq_ffn", [P, KD, SEQ], 16)
        xm = m("xm", [P, 4, SEQ], 0)
        zs = m("zs", [P, 4, SEQ], 8)
        us = m("us", [P, 4, STEP, CH], 16)
        s5_in = m("s5_in", [P, GROUPS, P], 24)
        s5_out = m("s5_out", [P, GROUPS, STEP, GW], 40)
        s5_conv = m("s5_conv", [P, GROUPS, STEP, GW], 56)
        s5_cos = m("s5_cos", [P, GROUPS, CH], 72)
        s5_sin = m("s5_sin", [P, GROUPS, CH], 80)
        s5_q = m("s5_q", [P, GROUPS, STEP, GW], 56)
        s5_b = hm("s5_b", [P, 2, GROUPS, GW], 0)
        s5_bb = hm("s5_bb", [P, 2, GROUPS, GW], 4)
        s5_crow = hm("s5_crow", [P, 2, 4, P], 8)
        s5_c = hm("s5_c", [P, 2, GROUPS, GW], 12)
        s5_cx = hm("s5_cx", [P, GROUPS, GW], 16)
        s5_k = hm("s5_k", [P, GROUPS, GW], 18)
        s5_pow = hm("s5_pow", [P, 2, STEP + 1, GROUPS], 20)
        s5_ldt = hm("s5_ldt", [P, GROUPS], 23)
        s5_v = hm("s5_v", [P, 24, GROUPS], 24)
        s5_r8 = place("s5_r8", [P, GROUPS])
        s5_big = m("s5_big", [P, GROUPS, STEP, GW], 0)
        s5_t = hm("s5_t", [P, GROUPS, CH // 2], 28)
        u_step = hm("u_step", [P, GROUPS, CH], 0)
        s5_state = hm("s5_state", [P, GROUPS, CH], 8)
        s5_w = hm("s5_w", [P, GROUPS, CH], 16)
        s5_z = hm("s5_z", [P, GROUPS, CH], 24)
        ys_step = hm("ys_step", [P, GROUPS, CH], 16)
        ys = m("ys", [P, 4, SEQ], 24)
        yg = m("yg", [P, 4, SEQ], 32)
        gate = m("gate", [P, 4, SEQ], 40)
        xc = m("xc", [P, 4, SEQ], 16)
        qm = m("qm", [P, 4, SEQ], 24)
        km = m("km", [P, 4, SEQ], 32)
        vf = m("vf", [P, 4, SEQ], 40)
        vt = m("vt", [P, 4, TT, P], 48)
        sc_m = m("sc_m", [P, TT, SEQ], 56)
        lstm_bd = m("lstm_bd", [P, 3, 4, P], 64)
        rowv = m("rowv", [M_HEADS, 8, SEQ], 70)
        e_m = m("e_m", [P, 2, SEQ], 64)
        g_col = small[:, 0:16].rearrange("p (s h) -> p s h", s=TT)
        lstm_t = m("lstm_t", [P, 4, SEQ], 40)
        c_q = m("c_q", [P, SEQ], 16)
        c_sig = m("c_sig", [P, 3, SEQ], 18)
        gc = m("gc", [P, 8, SEQ], 0)
        mix_hi = m("mix_hi", [P, 8, SEQ], 32, F32R)
        mix_lo = m("mix_lo", [P, 8, SEQ], 48, F32R)
        c_k = m("c_k", [P, SEQ], 64)
        c_f = m("c_f", [P, SEQ], 66)
        c_b = m("c_b", [P, SEQ], 68)
        c_d = m("c_d", [P, SEQ], 70)
        c_e = m("c_e", [P, SEQ], 72)
        c_kt = m("c_kt", [P, TT, P], 74)
        c_it = m("c_it", [P, TT, P], 76)
        c_s = m("c_s", [P, TT, P], 78)
        c_state = m("c_state", [P, 8, P], 80)
        c_i = m("c_i", [P, SEQ], 84)
        c_o = m("c_o", [P, SEQ], 86)
        late = m("late", [P, 2 * SEQ + 2 * P], 0)
        cos, sin = late[:, 0:SEQ], late[:, SEQ:2 * SEQ]
        turn, halves = late[:, 2 * SEQ:2 * SEQ + P], late[:, 2 * SEQ + P:2 * SEQ + 2 * P]
        qa = m("qa", [P, 5, SEQ], 6)
        va = m("va", [P, SEQ], 16)
        ua = m("ua", [P, 4, SEQ], 18)
        vva = m("vva", [P, 4, SEQ], 26)
        v_tok = m("v_tok", [P, TT, P], 34)
        vv_tok = m("vv_tok", [P, TT, SEQ], 36)
        sgw = m("sgw", [P, 8, P], 44)
        mixed = m("mixed", [P, SEQ], 44)
        sgw_t = m("sgw_t", [P, 8, P], 48)
        sgb = m("sgb", [P, 4, P], 52)
        sgn = m("sgn", [P, SEQ], 54)
        k_pad = m("k_pad", [P, 4, SEQ], 56)
        prob = tmp
        prob_t = [m("prob_t0", [P, TT, SEQ], 64), m("prob_t1", [P, TT, SEQ], 26)]
        qk_sq = m("qk_sq", [P, 5, SEQ], 72)
        oa = m("oa", [P, 4, SEQ], 72)
        oa_sq = m("oa_sq", [P, 4, SEQ], 80)
        ua_sq = m("ua_sq", [P, 4, SEQ], 36)
        head_dev = small[:, 64:64 + 40]
        gate_dev = small[:, 104:104 + 32]
        top_score = small[:, 136:140]
        shift = small[:, 140:144]
        total = small[:, 144:148]
        share = small[:, 148:152]

        bank = [ctx.enter_context(nc.psum_tensor(f"bank{b}", [P, 512], F32)) for b in range(8)]

        us_dram = nc.dram_tensor("us_dram", [4 * P, STEP, CH], F32, kind="Internal").ap()
        ys_dram = nc.dram_tensor("ys_dram", [4 * P, STEP, CH], F32, kind="Internal").ap()

        bank_free = [sem(f"bank{b}_free") for b in range(8)]
        raw_full = [sem(f"raw{s}_full") for s in range(RING)]
        hi_done = sem("hi_done")
        lo_done = sem("lo_done")
        slab_done = sem("slab_done")
        lead_in, x_in, early_in, rows_in = sem("lead_in"), sem("x_in"), sem("early_in"), sem("rows_in")
        s5_in_sem, lstm_in = sem("s5_in"), sem("lstm_in")
        x_turned, x_ready = sem("x_turned"), sem("x_ready")
        par_turned, par_ready = sem("par_turned"), sem("par_ready")
        eps_ready = sem("eps_ready")
        sq_ready, sum_ready, stat_ready, std_ready = (sem(k) for k in ("sq_ready", "sum_ready", "stat_ready", "std_ready"))
        inv_ready, scale_ready, pool_step = sem("inv_ready"), sem("scale_ready"), sem("pool_step")
        h_ready, hid_ready, evac_ready = sem("h_ready"), sem("hid_ready"), sem("evac_ready")
        act_for_dve, dve_for_act = sem("ffn_scalar_to_vector"), sem("ffn_vector_to_scalar")
        vector_step = sem("vector_step")
        scalar_step = sem("scalar_step")

        def five(name):
            return {k: sem(f"{name}_{k}") for k in ("pe_to_vector", "pe_to_scalar", "vector_to_pe",
                                                     "scalar_to_pe", "vector_to_scalar", "scalar_to_vector")}

        prep, s5, lstm, hgrn = five("prep"), five("s5"), five("lstm"), five("hgrn")
        qk_squared, qk_summed, qk_rooted, qk_inverted, qk_spread, qk_normal, qk_partner, k_turned, q_turned = (
            sem(f"qk_{k}") for k in ("squared", "summed", "rooted", "inverted", "spread", "normal", "partner", "k", "q"))
        k_swapped, v_in, v_turned, v_copied = (sem(k) for k in ("k_swapped", "v_in", "v_turned", "v_copied"))
        vv_in, sgw_turned, sgw_copied, vv_turned, vv_copied, vv_summed, vv_rooted, vv_normal, gate_mixed, gated_ready = (
            sem(k) for k in ("vv_in", "sgw_turned", "sgw_copied", "vv_turned", "vv_copied", "vv_summed", "vv_rooted",
                             "vv_normal", "gate_mixed", "gated_ready"))
        score_ready, max_ready, exp_ready, prob_ready, prob_turned, prob_copied, head_done = (
            sem(k) for k in ("score_ready", "max_ready", "exp_ready", "prob_ready", "prob_turned", "prob_copied", "head_done"))
        us_stored, us_loaded, ys_stored, ys_loaded = (sem(k) for k in ("us_stored", "us_loaded", "ys_stored", "ys_loaded"))
        late_in, us_ready, ys_ready = sem("late_in"), sem("us_ready"), sem("ys_ready")
        out_turned, out_ready, out_stored = sem("out_turned"), sem("out_ready"), sem("out_stored")

        def cols(w):
            return w.rearrange("(k p) n -> p k n", p=P)

        SIZE = {"ab_in": 12, "ab_glu": 4, "ab_out": 8, "ffn1": 44, "ffn2": 24, "c_in": 32, "c_out": 8,
                "s_in": 14, "s_out": 8, "up": 44, "down": 24}
        parts = [["ab_in", "ab_glu", "ab_out"], ["ffn1", "ffn2"], ["c_in", "c_out"], ["ffn1", "ffn2"],
                 ["s_in", "s_out"], ["up", "down"], ["s_in", "s_out"], ["up", "down"]][:upto]
        row_dmas = [0]

        def block_rows(b):
            return ROWS["pad"] - P if b == 1 else min(P, N_ROWS - b * P)

        N_SLABS = sum(SIZE[s] for part in parts for s in part)

        def col(name, i=0):
            c = ROWS[name] + i
            return par[:, c:c + 1]

        def col_at(name, i):
            return par[:, bass.ds(i + ROWS[name], 1)]

        block = ctx.enter_context(nc.Block())

        @block.sync
        def _(sp):
            n = Count()
            sp.dma_start(lead[:], a["lead"]).then_inc(lead_in, 16)
            sp.dma_start(x_tok[:], a["x"][0].rearrange("(t p) d -> p t d", p=P)).then_inc(x_in, 16)
            slab = [0]

            def load(src):
                s = slab[0] % RING
                if slab[0] >= RING:
                    sp.wait_ge(lo_done, n(lo_done))
                sp.dma_start(w_raw[:, s, 0:src.shape[1]], src).then_inc(raw_full[s], 16)
                slab[0] += 1

            def stream(times, slabs, turn):
                if times > 1:
                    with n.loop(sp, times, [(lo_done, slabs)]) as i:
                        turn(i)
                    slab[0] += (times - 1) * slabs
                else:
                    turn(0)

            def plain(w, tiles):
                w = cols(w)

                def turn(i):
                    for t in range(RING):
                        load(w[:, :, bass.ds(i * (RING * P) + t * P, P)])
                stream(tiles // RING, RING, turn)

            def pairs(w, v, at):
                w, v = cols(w), cols(v)

                def turn(i):
                    for t in range(RING // 2):
                        load(w[:, :, bass.ds(i * (RING // 2 * P) + t * P, P)])
                        load(v[:, :, bass.ds(i * (RING // 2 * P) + (t * P + at), P)])
                stream(KF // 2, RING, turn)

            def deep(w):
                w = cols(w)

                def turn(i):
                    for t in range(RING):
                        for k, c in ((0, 8), (8, 8), (16, KF - 16)):
                            load(w[:, k:k + c, bass.ds(i * (RING * P) + t * P, P)])
                stream(2, RING * len(DOWN), turn)

            def ab():
                w = cols(a["ab_w_in"][0])
                for t in range(12):
                    load(w[:, :, t * P:(t + 1) * P])
                w = cols(a["ab_w_glu"][0])
                for t in range(4):
                    load(w[:, :, t * P:(t + 1) * P])
                plain(a["ab_w_out"][0], 8)

            def c():
                w = cols(a["c_w_in"][0])

                def turn(h):
                    for v in (0, 1, 3, 2):
                        load(w[:, :, bass.ds(h * P + v * D, P)])
                stream(C_HEADS, RING, turn)
                plain(a["c_w_out"][0], 8)

            def ffn(i):
                pairs(a["ffn_w1"][i], a["ffn_w3"][i], 0)
                deep(a["ffn_w2"][i])

            def gated(i):
                w = cols(a["w_in_2"][i])
                for t in IN_ORDER:
                    load(w[:, :, t * P:(t + 1) * P])
                plain(a["w_o_2"][i], 8)

            def conv_ffn(i):
                pairs(a["w_up_2"][i], a["w_up_2"][i], D_FF)
                deep(a["w_down_2"][i])

            for part in [ab, lambda: ffn(0), c, lambda: ffn(1), lambda: gated(0), lambda: conv_ffn(0),
                         lambda: gated(1), lambda: conv_ffn(1)][:upto]:
                part()
            out = a["out"][0].rearrange("(t p) d -> p t d", p=P)
            for t in range(TT):
                sp.wait_ge(out_ready, 2 * t + 2)
                sp.dma_start(out[:, t], out_tok[:, t]).then_inc(out_stored, 16)
            sp.wait_ge(out_stored, 16 * TT)

        @block.gpsimd
        def _(pool):
            n = Count()

            def load_rows(src, first):
                at = 0
                while at < src.shape[0]:
                    r = (first + at) % P
                    k = min(P - r, src.shape[0] - at)
                    pool.dma_start(rows[r:r + k, (first + at) // P, 0:src.shape[1]] if src.shape[1] == P else None,
                                   src[at:at + k]).then_inc(rows_in, 16)
                    row_dmas[0] += 1
                    at += k

            def twice(src, first):
                r, b = first % P, first // P
                for h in range(2):
                    pool.dma_start(rows[r:r + src.shape[0], b, HEAD * h:HEAD * h + HEAD], src).then_inc(rows_in, 16)
                    row_dmas[0] += 1

            load_rows(a["norm_g"].rearrange("l j (k p) -> (l j k) p", p=P), ROWS["norm"])
            for key, name in (("attn_norm_g_2", "attn_norm"), ("ffn_norm_g_2", "ffn_norm"), ("ab_conv_b", "conv_b"),
                              ("ab_mh_gain", "mh_gain"), ("ab_skip", "skip"), ("ab_d", "s5_d"), ("ab_b_glu", "b_glu"),
                              ("c_lb_raw", "lb_raw"), ("c_g_gain", "c_gain"), ("attn_out_g_2", "attn_gain"),
                              ("sg_out_g_2", "sg_gain")):
                load_rows(a[key].rearrange("l (k p) -> (l k) p", p=P), ROWS[name])
            load_rows(a["ab_conv_w"][0].rearrange("t (k p) -> (t k) p", p=P), ROWS["conv_w"])
            twice(a["q_norm_g_2"], ROWS["q_norm"])
            twice(a["k_norm_g_2"], ROWS["k_norm"])
            twice(a["ab_a_re"][0], ROWS["a_re"])
            twice(a["ab_a_im"][0], ROWS["a_im"])
            for i in range(2):
                first = ROWS["up_conv"] + i * 4 * 2 * KF
                load_rows(a["conv_w_2"][i].rearrange("t (k p) -> (t k) p", p=P), first)
                load_rows(a["conv_b_2"][i].rearrange("(k p) -> k p", p=P), first + 3 * 2 * KF)
            b_re, b_im = (a[k][0].rearrange("g n p -> n g p") for k in ("ab_b_re", "ab_b_im"))
            c_re, c_im = (a[k][0].rearrange("g p n -> (g p) n").rearrange("(b q) n -> q b n", q=P)
                          for k in ("ab_c_re", "ab_c_im"))
            for v, (first, second) in enumerate(((b_re, b_im), (b_im, b_re))):
                pool.dma_start(s5_b[0:STATE, v], first).then_inc(s5_in_sem, 16)
                pool.dma_start(s5_b[STATE:P, v], second).then_inc(s5_in_sem, 16)
            for v, (first, second) in enumerate(((c_re, c_im), (c_im, c_re))):
                pool.dma_start(s5_crow[:, v, :, 0:STATE], first).then_inc(s5_in_sem, 16)
                pool.dma_start(s5_crow[:, v, :, STATE:P], second).then_inc(s5_in_sem, 16)
            pool.dma_start(s5_ldt[:], a["ab_log_dt"][0].partition_broadcast(P)).then_inc(s5_in_sem, 16)
            pool.dma_start(early[:], a["early"]).then_inc(early_in, 16)
            for v, key in enumerate(("ab_wq", "ab_wk", "ab_wv")):
                pool.dma_start(lstm_w4[:, v], a[key][0].rearrange("n d e -> (n d) e").rearrange("(t p) e -> p t e", p=P))\
                    .then_inc(lstm_in, 16)
            pool.dma_start(lstm_wif[:], a["ab_w_if"][0].rearrange("(k p) g -> p k g", p=P)).then_inc(lstm_in, 16)
            for v in range(2):
                pool.dma_start(lstm_bif[:, v:v + 1], a["ab_b_if"][0, M_HEADS * v:M_HEADS * v + M_HEADS].unsqueeze(1))\
                    .then_inc(lstm_in, 16)

            def add_squares(sq):
                n(sq_ready, 1)
                for k in range(1, KD - 1):
                    pool.wait_ge(sq_ready, n(sq_ready))
                    if k > 1:
                        pool.wait_ge(pool_step, n(pool_step))
                    nc.gpsimd.tensor_tensor(sq_sum[:], sq[:, 0] if k == 1 else sq_sum[:], sq[:, k], ALU.add)\
                        .then_inc(pool_step if k < KD - 2 else sum_ready, 1)
                n(sq_ready, 1)

            add_squares(sq_ab)
            pool.wait_ge(us_ready, 1)
            pool.dma_start(us_dram.rearrange("(k p) i c -> p k i c", p=P), us[:]).then_inc(us_stored, 16)
            pool.wait_ge(us_stored, 16)
            by_step = us_dram.rearrange("(g p) i c -> i p g c", p=GW)
            for i in range(STEP):
                k = STEP - 1 - i
                pool.dma_start(u_step[GW * k:GW * k + GW], by_step[i]).then_inc(us_loaded, 16)
            pool.wait_ge(ys_ready, 1)
            by_step = ys_dram.rearrange("(g p) j c -> j p g c", p=GW)
            for j in range(STEP):
                pool.dma_start(by_step[j], ys_step[GW * j:GW * j + GW]).then_inc(ys_stored, 16)
            pool.wait_ge(ys_stored, 16 * STEP)
            pool.dma_start(ys[:], ys_dram.rearrange("(k p) j c -> p k (j c)", p=P)).then_inc(ys_loaded, 16)

            for part, norms in enumerate(((sq_mix,), (sq_in, sq_ffn), (sq_in, sq_mix), (sq_in, sq_ffn), (sq_in,))):
                if part < upto:
                    for sq in norms:
                        add_squares(sq)
            for i in range(2):
                if upto <= 4 + 2 * i:
                    break
                if i:
                    add_squares(sq_ffn)
                pool.wait_ge(x_ready, 8 * (5 + 2 * i))
                pool.dma_start(late[:], a["late"]).then_inc(late_in, 16)
                pool.dma_start(sgw[:], a["sg_w_2"][i].rearrange("h p q -> p h q")).then_inc(late_in, 16)
                for h in range(8):
                    pool.dma_start(sgb[HEAD * (h % 2):HEAD * (h % 2) + HEAD, h // 2],
                                   a["sg_b_2"][i, h].partition_broadcast(HEAD)).then_inc(late_in, 16)
                pool.dma_start(sgn[:], a["sg_norm_g_2"][i].rearrange("h d -> (h d)").partition_broadcast(P))\
                    .then_inc(late_in, 16)
                n(sq_ready, 8)
                if upto > 5 + 2 * i:
                    add_squares(sq_in)

        @block.tensor
        def _(pe):
            n = Count()
            at = {"slab": 0, "bank": 0}

            def take(b):
                pe.wait_ge(bank_free[b], n(bank_free[b]))
                return bank[b]

            def product(hi, lo, slabs, tiles, last=None):
                for _ in range(tiles):
                    out = take(at["bank"] % RING)
                    kt = 0
                    for many in slabs:
                        s = at["slab"] % RING
                        pe.wait_ge(lo_done, n(lo_done))
                        for k in range(many):
                            if last and kt == sum(slabs) - 1:
                                pe.wait_ge(*last)
                            for w, v in ((w_hi, hi), (w_lo, hi), (w_hi, lo)):
                                mm = nc.tensor.matmul(out[:], w[:, s, k], v[:, kt],
                                                      start=(kt == 0 and w is w_hi and v is hi),
                                                      stop=(kt == sum(slabs) - 1 and v is lo))
                            kt += 1
                        mm.then_inc(slab_done, 1)
                        at["slab"] += 1
                    at["bank"] += 1

            def products(hi, lo, slabs, tiles, last=None):
                times = tiles // RING
                per = [(lo_done, RING * len(slabs))] + [(bank_free[b], 1) for b in range(RING)]
                if times == 1:
                    product(hi, lo, slabs, RING, last)
                    return
                with n.loop(pe, times, per):
                    product(hi, lo, slabs, RING, last)
                at["slab"] += (times - 1) * RING * len(slabs)
                at["bank"] += (times - 1) * RING

            def group(hi, lo, order=range(KD), between=None):
                outs = [take((at["bank"] + t) % RING) for t in range(GROUP)]
                for j, k in enumerate(order):
                    pe.wait_ge(h_ready, n(h_ready))
                    for t in range(GROUP):
                        s = (at["slab"] + t) % RING
                        if j == 0:
                            pe.wait_ge(lo_done, n(lo_done))
                        for w, v in ((w_hi, hi), (w_lo, hi), (w_hi, lo)):
                            mm = nc.tensor.matmul(outs[t][:], w[:, s, k], v[:, k], start=(j == 0 and w is w_hi and v is hi),
                                                  stop=(j == KD - 1 and v is lo))
                        if j == KD - 1:
                            mm.then_inc(slab_done, 1)
                    if between and (j % 2 and j < KD - 1 or j == KD - 2):
                        between()
                at["slab"] += GROUP
                at["bank"] += GROUP

            def from_h(tiles):
                group(h_hi, h_lo)
                product(h_hi, h_lo, [KD], -(GROUP - tiles) % RING)
                if tiles - GROUP >= RING:
                    products(h_hi, h_lo, [KD], (tiles - GROUP) // RING * RING)

            def sums(squares, tiles):
                out = take(4)
                if tiles == KD:
                    pe.wait_ge(sum_ready, n(sum_ready))
                    n(sq_ready, KD - 1)
                    terms = [sq_sum[:], squares[:, KD - 1]]
                else:
                    terms = [squares[:, k] for k in range(tiles)]
                pe.wait_ge(sq_ready, n(sq_ready, 1 if tiles == KD else tiles))
                for t in range(TT):
                    for k, term in enumerate(terms):
                        mm = nc.tensor.matmul(out[:, t:t + 1], term[:, t * P:(t + 1) * P], ones[:, 0:1], start=(k == 0),
                                              stop=(k == len(terms) - 1))
                mm.then_inc(stat_ready, 1)
                out = take(5)
                pe.wait_ge(inv_ready, n(inv_ready))
                for t in range(TT):
                    mm = nc.tensor.matmul(out[:, t * P:(t + 1) * P], inv[:, t:t + 1].to_broadcast([P, P]), ident,
                                          start=True, stop=True)
                mm.then_inc(scale_ready, 1)

            pe.wait_ge(lead_in, 16)
            pe.wait_ge(x_in, 16)
            for k in range(KD):
                out = take(k % RING)
                for t in range(TT):
                    mm = nc.tensor.transpose(out[:, t * P:(t + 1) * P], x_tok[:, t, k * P:(k + 1) * P], ident)
                mm.then_inc(x_turned, 1)
            pe.wait_ge(rows_in, 16 * row_dmas[0])
            for b in range(ROW_BLOCKS):
                out = take(4 + b % 4)
                r = block_rows(b)
                nc.tensor.transpose(out[:, 0:r], rows[0:r, b], ident[0:r, 0:r]).then_inc(par_turned, 1)

            def s5_prepare():
                pe.wait_ge(s5_in_sem, 16 * 9)
                for v in range(2):
                    out = take(5 + v)
                    for b in range(4):
                        mm = nc.tensor.transpose(out[:, b * P:(b + 1) * P], s5_crow[:, v, b], ident)
                    mm.then_inc(prep["pe_to_vector"], 1)
                pe.wait_ge(prep["vector_to_pe"], n(prep["vector_to_pe"]))
                for i in range(GROUPS // 4):
                    out = take(4 + i % 4)
                    for g in range(4):
                        mm = nc.tensor.transpose(out[:, g * P:(g + 1) * P],
                                                 s5_q[:, 4 * i + g].rearrange("p k w -> p (k w)"), ident)
                    mm.then_inc(prep["pe_to_scalar"], 1)
                pe.wait_ge(prep["vector_to_pe"], n(prep["vector_to_pe"]))
                out = take(4)
                for g in range(GROUPS):
                    mm = nc.tensor.matmul(out[:, g * GW:(g + 1) * GW], s5_q[:, g].rearrange("p k w -> p (k w)"),
                                          s5_cx[:, g], start=True, stop=True)
                mm.then_inc(prep["pe_to_scalar"], 1)
                pe.wait_ge(prep["scalar_to_pe"], n(prep["scalar_to_pe"]))
                for j in range(STEP):
                    out = take(5 + j % 3)
                    off = P - GW * (STEP - 1 - j)
                    nc.tensor.matmul(out[:], shifted[:, off:off + P], s5_k[:].rearrange("p g w -> p (g w)"),
                                     start=True, stop=True).then_inc(prep["pe_to_scalar"], 1)

            def s5_run():
                pe.wait_ge(us_loaded, 16 * STEP)
                for i in range(4):
                    out = take(4 + i)
                    for g in range(8):
                        mm = nc.tensor.matmul(out[:, g * CH:(g + 1) * CH], s5_in[:, 8 * i + g], u_step[:, 8 * i + g],
                                              start=True, stop=True)
                    mm.then_inc(s5["pe_to_scalar"], 1)
                for i in range(4):
                    out = take(i)
                    pe.wait_ge(s5["scalar_to_pe"], n(s5["scalar_to_pe"]))
                    nc.tensor.matmul(out[:], swap, s5_state[:, 8 * i:8 * i + 8].rearrange("p g c -> p (g c)"),
                                     start=True, stop=True).then_inc(s5["pe_to_vector"], 1)
                pe.wait_ge(s5["vector_to_pe"], n(s5["vector_to_pe"]))
                for i in range(4):
                    out = take(4 + i)
                    nc.tensor.matmul(out[:], swap, s5_z[:, 8 * i:8 * i + 8].rearrange("p g c -> p (g c)"),
                                     start=True, stop=True).then_inc(s5["pe_to_vector"], 1)
                for i in range(4):
                    out = take(i)
                    pe.wait_ge(s5["vector_to_pe"], n(s5["vector_to_pe"]))
                    for g in range(8):
                        c = g * CH
                        nc.tensor.matmul(out[:, c:c + CH], s5_conv[:, 8 * i + g].rearrange("p j w -> p (j w)"),
                                         u_step[:, 8 * i + g], start=True, stop=False)
                        mm = nc.tensor.matmul(out[:, c + 1:c + CH], s5_out[:, 8 * i + g].rearrange("p j w -> p (j w)"),
                                              s5_state[:, 8 * i + g, 0:CH - 1], start=False, stop=True)
                    mm.then_inc(s5["pe_to_scalar"], 1)

            def lstm_run():
                for k in range(4):
                    pe.wait_ge(lstm["scalar_to_pe"], n(lstm["scalar_to_pe"]))
                    for v, src in ((0, xc), (1, xc), (2, xm)):
                        out = take(4 + v)
                        nc.tensor.matmul(out[:], lstm_bd[:, v, k], src[:, k], start=True, stop=True)\
                            .then_inc(lstm["pe_to_scalar"], 1)
                    out = take(7)
                    for t in range(TT):
                        mm = nc.tensor.matmul(out[:, t * P:(t + 1) * P], xm[:, k, t * P:(t + 1) * P], lstm_bd[:, 2, k],
                                              start=True, stop=True)
                    mm.then_inc(lstm["pe_to_scalar"], 1)
                pe.wait_ge(lstm["scalar_to_pe"], n(lstm["scalar_to_pe"]))
                for v in range(2):
                    out = take(4 + v)
                    for j in range(12):
                        mm = nc.tensor.matmul(out[0:M_HEADS, :], lstm_wif[:, j, 4 * v:4 * v + 4], (qm, km, vf)[j // 4][:, j % 4],
                                              start=(j == 0), stop=(j == 11))
                    mm.then_inc(lstm["pe_to_scalar"], 1)
                pe.wait_ge(lstm["vector_to_pe"], n(lstm["vector_to_pe"]))
                out = take(6)
                for t in range(TT):
                    mm = nc.tensor.transpose(out[:, 4 * t:4 * t + 4], rowv[:, 7, t * P:(t + 1) * P], ident[0:4, 0:4])
                mm.then_inc(lstm["pe_to_vector"], 1)
                pe.wait_ge(lstm["scalar_to_pe"], n(lstm["scalar_to_pe"]))
                for h in range(M_HEADS):
                    for v, row in ((0, 3), (1, 5)):
                        out = take(4 + v)
                        nc.tensor.matmul(out[:], pick[:, h], rowv[:, row], start=True, stop=True)\
                            .then_inc(lstm["pe_to_scalar"], 1)
                    for t in range(TT):
                        out = take(6 + t % 2)
                        nc.tensor.matmul(out[:, 0:SEQ - t * P], km[:, h, t * P:(t + 1) * P], qm[:, h, t * P:SEQ],
                                         start=True, stop=True).then_inc(lstm["pe_to_vector"], 1)
                    num, den = take(0), take(1)
                    for t in range(TT):
                        pe.wait_ge(lstm["vector_to_pe"], n(lstm["vector_to_pe"]))
                        nc.tensor.matmul(num[:, t * P:SEQ], vt[:, h, t], sc_m[:, t, t * P:SEQ], start=(t == 0), stop=(t == 3))
                        mm = nc.tensor.matmul(den[:, t * P:SEQ], ones, sc_m[:, t, t * P:SEQ], start=(t == 0), stop=(t == 3))
                    mm.then_inc(lstm["pe_to_vector"], 1)
                    out = take(2)
                    pe.wait_ge(lstm["vector_to_pe"], n(lstm["vector_to_pe"]))
                    nc.tensor.matmul(out[:], ones, lstm_t[:, 2], start=True, stop=True).then_inc(lstm["pe_to_vector"], 1)
                    out = take(3)
                    pe.wait_ge(lstm["scalar_to_pe"], n(lstm["scalar_to_pe"]))
                    nc.tensor.matmul(out[:], ones, lstm_t[:, 0], start=True, stop=True).then_inc(lstm["pe_to_scalar"], 1)

            def ab():
                s5_prepare()
                sums(sq_ab, KD)
                from_h(12)
                s5_run()
                pe.wait_ge(h_ready, n(h_ready, 4))
                product(h_hi, h_lo, [4], 4)
                lstm_run()
                pe.wait_ge(h_ready, n(h_ready, 8))
                products(h_hi, h_lo, [8], 8)
                sums(sq_mix, KD)

            def down():
                pe.wait_ge(hid_ready, n(hid_ready, KF - 1))
                products(hid_hi, hid_lo, DOWN, 8, (hid_ready, n(hid_ready)))

            def ffn(i):
                sums(sq_in, KD)
                from_h(2 * KF)
                down()
                sums(sq_ffn, KD)

            def c():
                def weigh():
                    out = take(4)
                    pe.wait_ge(hgrn["scalar_to_pe"], n(hgrn["scalar_to_pe"]))
                    for t in range(TT):
                        mm = nc.tensor.transpose(out[:, t * P:(t + 1) * P], c_i[:, t * P:(t + 1) * P], ident)
                    mm.then_inc(hgrn["pe_to_scalar"], 1)
                    out = take(5)
                    pe.wait_ge(hgrn["vector_to_pe"], n(hgrn["vector_to_pe"]))
                    for t in range(TT):
                        mm = nc.tensor.transpose(out[:, t * P:(t + 1) * P], c_k[:, t * P:(t + 1) * P], ident)
                    mm.then_inc(hgrn["pe_to_scalar"], 1)
                    out = take(6)
                    for t in range(TT):
                        mm = nc.tensor.matmul(out[:, t * P:(t + 1) * P], c_k[:, t * P:(t + 1) * P], c_d[:, t * P:(t + 1) * P],
                                              start=True, stop=True)
                    mm.then_inc(hgrn["pe_to_vector"], 1)

                def update():
                    u = take(7), take(4)
                    pe.wait_ge(hgrn["scalar_to_pe"], n(hgrn["scalar_to_pe"]))
                    for j in range(7):
                        r = C_CHUNK * (j % 2)
                        mm = nc.tensor.matmul(u[j % 2][:, (j // 2) * P:(j // 2 + 1) * P], c_kt[r:r + C_CHUNK, j // 2],
                                              c_it[r:r + C_CHUNK, j // 2], start=True, stop=True)
                    mm.then_inc(hgrn["pe_to_vector"], 1)

                def read():
                    out = take(5)
                    pe.wait_ge(hgrn["vector_to_pe"], n(hgrn["vector_to_pe"], 2))
                    for t in range(TT):
                        nc.tensor.matmul(out[:, t * P:(t + 1) * P], c_it[:, t], c_s[:, t], start=True, stop=False)
                        for j in (2 * t, 2 * t + 1):
                            if j:
                                mm = nc.tensor.matmul(out[:, j * C_CHUNK:(j + 1) * C_CHUNK], c_state[:, j],
                                                      c_e[:, j * C_CHUNK:(j + 1) * C_CHUNK], start=False, stop=(j % 2 == 1))
                    mm.then_inc(hgrn["pe_to_scalar"], 1)

                def square():
                    out = take(6)
                    pe.wait_ge(hgrn["scalar_to_pe"], n(hgrn["scalar_to_pe"]))
                    nc.tensor.matmul(out[:], ones, c_o[:], start=True, stop=True).then_inc(hgrn["pe_to_scalar"], 1)

                sums(sq_in, KD)
                group(h_hi, h_lo)
                product(h_hi, h_lo, [KD], 1)
                per = [(hgrn["scalar_to_pe"], 3), (hgrn["vector_to_pe"], 3), (lo_done, 4)] + [
                    (bank_free[b], 2 if b in (4, 5, 6) else 1) for b in range(8)]
                with n.loop(pe, C_HEADS - 1, per):
                    for step in (weigh, update, read, square):
                        product(h_hi, h_lo, [KD], 1)
                        step()
                at["slab"] += RING * (C_HEADS - 2)
                at["bank"] += RING * (C_HEADS - 2)
                steps = iter((weigh, update, read, square))
                group(mix_hi, mix_lo, between=lambda: next(steps)())
                product(mix_hi, mix_lo, [KD], 1)
                products(mix_hi, mix_lo, [KD], 4)
                sums(sq_mix, KD)

            def gated(i):
                sums(sq_ffn if i else sq_in, KD)
                group(h_hi, h_lo)
                product(h_hi, h_lo, [KD], 4)
                out = take(4)
                pe.wait_ge(qk_squared, n(qk_squared, 5))
                pe.wait_ge(late_in, n(late_in, 16 * 11))
                for t in range(TT):
                    for j in range(5):
                        c = 2 * (5 * t + j)
                        mm = nc.tensor.matmul(out[:, c:c + 2], qk_sq[:, j, t * P:(t + 1) * P], halves[:, 0:P:HEAD],
                                              start=True, stop=True)
                mm.then_inc(qk_summed, 1)
                product(h_hi, h_lo, [KD], 1)
                pe.wait_ge(qk_inverted, n(qk_inverted))
                for j in (4, 0, 1, 2, 3):
                    out = take(4 + j % 4)
                    for t in range(TT):
                        for hh in range(2):
                            c = 2 * (5 * t + j) + hh
                            mm = nc.tensor.matmul(out[HEAD * hh:HEAD * hh + HEAD, t * P:(t + 1) * P],
                                                  head_dev[:, c:c + 1].to_broadcast([P, HEAD]), ident, start=True, stop=True)
                    mm.then_inc(qk_spread, 1)
                product(h_hi, h_lo, [KD], 1)
                for j in (4, 0, 1, 2, 3):
                    out = take(4 + j % 4)
                    pe.wait_ge(qk_normal, n(qk_normal))
                    nc.tensor.matmul(out[:], turn, qa[:, j], start=True, stop=True).then_inc(qk_partner, 1)
                product(h_hi, h_lo, [KD], 1)
                out = take(4)
                pe.wait_ge(k_turned, n(k_turned))
                nc.tensor.matmul(out[:], swap, qa[:, 4], start=True, stop=True).then_inc(k_swapped, 1)
                out = take(5)
                pe.wait_ge(v_in, n(v_in))
                for t in range(TT):
                    mm = nc.tensor.transpose(out[:, t * P:(t + 1) * P], va[:, t * P:(t + 1) * P], ident)
                mm.then_inc(v_turned, 1)
                for v in range(2):
                    out = take(6 + v)
                    for h in range(4):
                        mm = nc.tensor.transpose(out[:, h * P:(h + 1) * P], sgw[:, 4 * v + h], ident)
                    mm.then_inc(sgw_turned, 1)
                product(h_hi, h_lo, [KD], 1)
                pe.wait_ge(vv_in, n(vv_in))
                for t in range(TT):
                    out = take(4 + t)
                    for f in range(4):
                        mm = nc.tensor.transpose(out[:, f * P:(f + 1) * P], vva[:, f, t * P:(t + 1) * P], ident)
                    mm.then_inc(vv_turned, 1)
                product(h_hi, h_lo, [KD], 3)

                def scores(u):
                    h, t = u // TT, u % TT
                    out = take(2 + u % 3)
                    nc.tensor.matmul(out[:], qa[:, h // 2, t * P:(t + 1) * P], k_pad[:, 2 * (h // 4) + h % 2],
                                     start=True, stop=True).then_inc(score_ready, 1)

                def mix(j):
                    out = take(5)
                    if j == 0:
                        pe.wait_ge(vv_normal, n(vv_normal))
                        pe.wait_ge(sgw_copied, n(sgw_copied))
                    for t in range(TT):
                        for hh in range(2):
                            mm = nc.tensor.matmul(out[HEAD * hh:HEAD * hh + HEAD, t * P:(t + 1) * P],
                                                  vv_tok[:, t, (2 * j + hh) * HEAD:(2 * j + hh + 1) * HEAD],
                                                  sgw_t[:, 2 * j + hh], start=True, stop=True)
                    mm.then_inc(gate_mixed, 1)

                def values(h):
                    r, b = HEAD * (h % 2), (h // 2) % 2
                    out = take(b) if h % 2 == 0 else bank[b]
                    pe.wait_ge(prob_copied, n(prob_copied, TT))
                    for s in range(TT):
                        mm = nc.tensor.matmul(out[r:r + HEAD, :], v_tok[:, s, HEAD * (h // 4):HEAD * (h // 4) + HEAD],
                                              prob_t[h % 2][:, s], start=(s == 0), stop=(s == TT - 1))
                    mm.then_inc(head_done, 1)

                pe.wait_ge(q_turned, n(q_turned))
                pe.wait_ge(v_copied, n(v_copied))
                scores(0)
                scores(1)
                for u in range(UNITS):
                    if u + 2 < UNITS:
                        scores(u + 2)
                    out = take(6 + u % 2)
                    pe.wait_ge(prob_ready, n(prob_ready))
                    for s in range(TT):
                        mm = nc.tensor.transpose(out[:, s * P:(s + 1) * P], prob[:, u % 4, s * P:(s + 1) * P], ident)
                    mm.then_inc(prob_turned, 1)
                    if u % TT == 1 and u > TT:
                        values(u // TT - 1)
                    if u in MIX_AT:
                        mix(MIX_AT.index(u))
                values(7)
                sums(ua_sq, 4)
                sums(oa_sq, 4)
                group(h_hi, h_lo, (4, 5, 6, 7, 0, 1, 2, 3))
                product(h_hi, h_lo, [KD], 1)
                products(h_hi, h_lo, [KD], 4)

            def conv_ffn(i):
                sums(sq_in, KD)
                from_h(2 * KF)
                down()

            for part in [ab, lambda: ffn(0), c, lambda: ffn(1), lambda: gated(0), lambda: conv_ffn(0),
                         lambda: gated(1), lambda: conv_ffn(1)][:upto]:
                part()
            pe.wait_ge(x_ready, KD * (1 + upto))
            for t in range(TT):
                for v in range(2):
                    out = take(4 + (2 * t + v) % 4)
                    for k in range(4):
                        mm = nc.tensor.transpose(out[:, k * P:(k + 1) * P], x[:, 4 * v + k, t * P:(t + 1) * P], ident)
                    mm.then_inc(out_turned, 1)

        @block.scalar
        def _(act):
            n = Count()
            at = {"split": 0, "bank": 0}

            def split():
                if at["split"] < N_SLABS:
                    s = at["split"] % RING
                    act.wait_ge(raw_full[s], n(raw_full[s], 16))
                    nc.scalar.activation(w_hi[:, s], w_raw[:, s], ACT.Copy).then_inc(hi_done, 1)
                    at["split"] += 1

            def slab():
                act.wait_ge(slab_done, n(slab_done))
                split()

            def turns(times, slabs, body, extra=()):
                dry = at["split"] + times * slabs > N_SLABS
                k = times - dry
                if k > 1:
                    per = [(slab_done, slabs)] + [(raw_full[s], 16 * slabs // RING) for s in range(RING)] + list(extra)
                    with n.loop(act, k, per) as i:
                        body(i)
                    at["split"] += (k - 1) * slabs
                elif k:
                    body(0)
                if dry:
                    body(times - 1)

            def turned_bank():
                at["bank"] += 1
                return (at["bank"] - 1) % RING

            def squares(src, dst, wait=None):
                for k in range(src.shape[1]):
                    if wait is not None:
                        act.wait_ge(wait, n(wait))
                    nc.scalar.activation(dst[:, k], src[:, k], ACT.Square).then_inc(sq_ready, 1)

            def load_root():
                nc.scalar.activation(warm[:], eps[:], ACT.Sqrt)

            def deviation(width):
                act.wait_ge(stat_ready, n(stat_ready))
                nc.scalar.activation(dev[:], bank[4][:, 0:TT], ACT.Sqrt, bias=eps[:, 0:1], scale=1.0 / width)\
                    .then_inc(std_ready, 1)

            def leave(y, sq, slabs):
                first = at["bank"]
                load_root()

                def body(i):
                    for t in range(RING):
                        for _ in range(slabs):
                            slab()
                        b = (first + t) % RING
                        k = bass.ds(i * RING + t, 1)
                        nc.scalar.activation(sq[:, k], bank[b][:].unsqueeze(1), ACT.Square).then_inc(sq_ready, 1)
                        nc.scalar.activation(y[:, k], bank[b][:].unsqueeze(1), ACT.Copy).then_inc(bank_free[b], 1)
                turns(2, RING * slabs, body)
                at["bank"] += KD
                deviation(D)

            def s5_prepare():
                v = [s5_v[:, i] for i in range(24)]
                act.wait_ge(s5_in_sem, 16 * 9)
                nc.scalar.activation(v[0], s5_ldt[:], ACT.Exp).then_inc(prep["scalar_to_vector"], 1)
                act.wait_ge(prep["vector_to_scalar"], n(prep["vector_to_scalar"]))
                nc.scalar.activation(v[7], v[1], ACT.Exp)
                nc.scalar.activation(s5_r8[:], v[1], ACT.Exp, scale=float(STEP))
                nc.scalar.activation(v[8], v[4], ACT.Sin)
                nc.scalar.activation(v[9], v[5], ACT.Sin).then_inc(prep["scalar_to_vector"], 1)
                for i in range(GROUPS // 4):
                    act.wait_ge(prep["pe_to_scalar"], n(prep["pe_to_scalar"]))
                    nc.scalar.activation(s5_in[:, 4 * i:4 * i + 4], bank[4 + i % 4][:].rearrange("p (g w) -> p g w", g=4),
                                         ACT.Copy).then_inc(bank_free[4 + i % 4], 1)
                act.wait_ge(prep["pe_to_scalar"], n(prep["pe_to_scalar"]))
                nc.scalar.activation(s5_k[:], bank[4][:].rearrange("p (g w) -> p g w", g=GROUPS), ACT.Copy)\
                    .then_inc(prep["scalar_to_pe"], 1)
                act.drain().then_inc(bank_free[4], 1)
                for j in range(STEP):
                    act.wait_ge(prep["pe_to_scalar"], n(prep["pe_to_scalar"]))
                    nc.scalar.activation(s5_conv[:, :, j], bank[5 + j % 3][:].rearrange("p (g w) -> p g w", g=GROUPS),
                                         ACT.Copy).then_inc(bank_free[5 + j % 3], 1)
                act.drain().then_inc(prep["scalar_to_vector"], 1)

            def s5_run():
                for i in range(4):
                    act.wait_ge(s5["pe_to_scalar"], n(s5["pe_to_scalar"]))
                    nc.scalar.activation(s5_state[:, 8 * i:8 * i + 8], bank[4 + i][:].rearrange("p (g c) -> p g c", g=8),
                                         ACT.Copy).then_inc(s5["scalar_to_pe"], 1)
                for i in range(4):
                    act.wait_ge(s5["pe_to_scalar"], n(s5["pe_to_scalar"]))
                    nc.scalar.activation(ys_step[:, 8 * i:8 * i + 8], bank[i][:].rearrange("p (g c) -> p g c", g=8),
                                         ACT.Copy).then_inc(bank_free[i], 1)
                act.drain().then_inc(ys_ready, 1)
                act.wait_ge(s5["vector_to_scalar"], n(s5["vector_to_scalar"]))
                nc.scalar.activation(yg[:], ys[:], ACT.Gelu_apprx_tanh).then_inc(s5["scalar_to_vector"], 1)
                for t in range(4):
                    slab()
                    nc.scalar.activation(gate[:, t], bank[turned_bank()][:], ACT.Sigmoid, bias=col("b_glu", t))\
                        .then_inc(s5["scalar_to_vector"], 1)

            def lstm_run():
                for k in range(4):
                    act.wait_ge(lstm["vector_to_scalar"], n(lstm["vector_to_scalar"]))
                    nc.scalar.activation(xc[:, k], xc[:, k], ACT.Silu).then_inc(lstm["scalar_to_pe"], 1)
                for k in range(4):
                    for v, (dst, scale) in enumerate(((qm, 1.0), (km, float(P) ** -0.5), (vf, 1.0), (vt, 1.0))):
                        act.wait_ge(lstm["pe_to_scalar"], n(lstm["pe_to_scalar"]))
                        to = dst[:, k] if v < 3 else dst[:, k].rearrange("p t w -> p (t w)")
                        nc.scalar.activation(to, bank[4 + v][:], ACT.Copy, scale=scale).then_inc(bank_free[4 + v], 1)
                act.drain().then_inc(lstm["scalar_to_pe"], 1)
                act.wait_ge(lstm["pe_to_scalar"], n(lstm["pe_to_scalar"], 2))
                i_b, f_b = lstm_bif[:, 0:1], lstm_bif[:, 1:2]
                r = [rowv[:, j] for j in range(8)]
                nc.scalar.activation(r[2], bank[5][0:M_HEADS, :], ACT.Abs, bias=f_b).then_inc(scalar_step, 1)
                nc.scalar.activation(r[1], bank[5][0:M_HEADS, :], ACT.Identity, bias=f_b).then_inc(bank_free[5], 1)
                nc.scalar.activation(r[0], bank[4][0:M_HEADS, :], ACT.Identity, bias=i_b).then_inc(bank_free[4], 1)
                act.wait_ge(scalar_step, n(scalar_step))
                nc.scalar.activation(r[3], r[2], ACT.Exp, scale=-1.0).then_inc(scalar_step, 1)
                act.wait_ge(scalar_step, n(scalar_step))
                nc.scalar.activation(r[4], r[3], ACT.Ln, bias=1.0).then_inc(lstm["scalar_to_vector"], 1)
                act.wait_ge(lstm["vector_to_scalar"], n(lstm["vector_to_scalar"]))
                nc.scalar.activation(r[5], r[4], ACT.Exp, scale=-1.0).then_inc(lstm["scalar_to_pe"], 1)
                for h in range(M_HEADS):
                    for v in range(2):
                        act.wait_ge(lstm["pe_to_scalar"], n(lstm["pe_to_scalar"]))
                        nc.scalar.activation(e_m[:, v], bank[4 + v][:], ACT.Copy).then_inc(lstm["scalar_to_vector"], 1)
                    for t in range(TT):
                        act.wait_ge(lstm["vector_to_scalar"], n(lstm["vector_to_scalar"]))
                        nc.scalar.activation(lstm_t[:, t, t * P:SEQ], lstm_t[:, t, t * P:SEQ], ACT.Exp)\
                            .then_inc(lstm["scalar_to_vector"], 1)
                    act.wait_ge(lstm["vector_to_scalar"], n(lstm["vector_to_scalar"]))
                    nc.scalar.activation(lstm_t[:, 0], lstm_t[:, 3], ACT.Square).then_inc(lstm["scalar_to_pe"], 1)
                    act.wait_ge(lstm["pe_to_scalar"], n(lstm["pe_to_scalar"]))
                    nc.scalar.activation(lstm_t[:, 1], bank[3][:], ACT.Sqrt, bias=eps[:, 0:1], scale=1.0 / P)\
                        .then_inc(lstm["scalar_to_vector"], 1)

            def ab():
                s5_prepare()
                act.wait_ge(hgrn["vector_to_scalar"], n(hgrn["vector_to_scalar"]))
                nc.scalar.activation(small[:, 0:16], small[:, 0:16], ACT.Exp).then_inc(hgrn["scalar_to_vector"], 1)
                act.wait_ge(prep["vector_to_scalar"], n(prep["vector_to_scalar"]))
                squares(x, sq_ab, x_ready)
                deviation(D)
                for t in range(12):
                    slab()
                    b = turned_bank()
                    if t < 4:
                        ins = nc.scalar.activation(xm[:, t], bank[b][:], ACT.Copy)
                    elif t < 8:
                        ins = nc.scalar.activation(zs[:, t - 4], bank[b][:], ACT.Silu)
                    else:
                        ins = nc.scalar.activation(us[:, t - 8], bank[b][:].rearrange("p (c i) -> p i c", i=STEP), ACT.Copy)
                    ins.then_inc(bank_free[b], 1)
                act.drain().then_inc(us_ready, 1)
                s5_run()
                lstm_run()
                leave(y_mix, sq_mix, 1)

            def ffn(i):
                squares(x, sq_in, x_ready)
                deviation(D)
                first = at["bank"]

                def body(i):
                    for p in range(2):
                        slab()
                        nc.scalar.activation(tmp[:, p], bank[(first + 2 * p) % RING][:], ACT.Silu).then_inc(act_for_dve, 1)
                        slab()
                turns(KF // 2, RING, body)
                at["bank"] += 2 * KF
                leave(y_ffn, sq_ffn, 3)

            def c():
                squares(x, sq_in, x_ready)
                deviation(D)
                first = at["bank"]
                bank_of = [bank[(first + t) % RING] for t in range(RING)]
                free = [bank_free[(first + t) % RING] for t in range(RING)]

                def sigmoid(t):
                    slab()
                    nc.scalar.activation(c_sig[:, t], bank_of[t][:], ACT.Sigmoid).then_inc(hgrn["scalar_to_vector"], 1)

                def turn(gemm, mixer):
                    if gemm:
                        sigmoid(0)
                    if mixer:
                        act.wait_ge(hgrn["pe_to_scalar"], n(hgrn["pe_to_scalar"]))
                        nc.scalar.activation(c_it[:].rearrange("p t w -> p (t w)"), bank[4][:], ACT.Copy).then_inc(bank_free[4], 1)
                        act.wait_ge(hgrn["pe_to_scalar"], n(hgrn["pe_to_scalar"]))
                        nc.scalar.activation(c_kt[:].rearrange("p t w -> p (t w)"), bank[5][:], ACT.Copy).then_inc(bank_free[5], 1)
                        act.drain().then_inc(hgrn["scalar_to_pe"], 1)
                    if gemm:
                        sigmoid(1)
                        sigmoid(2)
                    if mixer:
                        act.wait_ge(hgrn["pe_to_scalar"], n(hgrn["pe_to_scalar"]))
                        nc.scalar.activation(c_o[:], bank[5][:], ACT.Square).then_inc(hgrn["scalar_to_pe"], 1)
                    if gemm:
                        act.wait_ge(hgrn["vector_to_scalar"], n(hgrn["vector_to_scalar"]))
                        nc.scalar.activation(c_f[:], c_f[:], ACT.Ln).then_inc(hgrn["scalar_to_vector"], 1)
                        act.wait_ge(hgrn["vector_to_scalar"], n(hgrn["vector_to_scalar"]))
                        nc.scalar.activation(c_e[:], c_b[:], ACT.Exp)
                        nc.scalar.activation(tmp[:, 0], c_d[:], ACT.Exp)
                        nc.scalar.activation(tmp[:, 1], c_d[:], ACT.Exp, scale=-1.0).then_inc(hgrn["scalar_to_vector"], 1)
                        slab()
                        nc.scalar.activation(c_i[:], bank_of[3][:], ACT.Copy).then_inc(free[3], 1)
                        act.drain().then_inc(hgrn["scalar_to_pe"], 1)
                    if mixer:
                        act.wait_ge(hgrn["pe_to_scalar"], n(hgrn["pe_to_scalar"]))
                        nc.scalar.activation(tmp[:, 2], bank[6][:], ACT.Sqrt, bias=eps[:, 0:1], scale=1.0 / P)\
                            .then_inc(hgrn["scalar_to_vector"], 1)

                turn(True, False)
                per = [(slab_done, RING), (hgrn["vector_to_scalar"], 2), (hgrn["pe_to_scalar"], 4)] + [
                    (raw_full[s], 16) for s in range(RING)]
                with n.loop(act, C_HEADS - 1, per):
                    turn(True, True)
                at["split"] += RING * (C_HEADS - 2)
                turn(False, True)
                at["bank"] += RING * C_HEADS
                leave(y_mix, sq_mix, 1)

            def gated(i):
                if i == 0:
                    squares(x, sq_in, x_ready)
                deviation(D)
                for t in IN_ORDER:
                    if t == IN_ORDER[6]:
                        act.wait_ge(qk_summed, n(qk_summed))
                        nc.scalar.activation(head_dev, bank[4][:, 0:40], ACT.Sqrt, bias=eps[:, 0:1], scale=1.0 / HEAD)\
                            .then_inc(qk_rooted, 1)
                    slab()
                    b = turned_bank()
                    if t < 5:
                        nc.scalar.activation(qk_sq[:, t], bank[b][:], ACT.Square).then_inc(qk_squared, 1)
                        nc.scalar.activation(qa[:, t], bank[b][:], ACT.Copy).then_inc(bank_free[b], 1)
                    elif t == 5:
                        nc.scalar.activation(va[:], bank[b][:], ACT.Copy).then_inc(bank_free[b], 1)
                        act.drain().then_inc(v_in, 1)
                    else:
                        dst = ua[:, t - 6] if t < 10 else vva[:, t - 10]
                        nc.scalar.activation(dst, bank[b][:], ACT.Gelu_apprx_tanh).then_inc(bank_free[b], 1)
                    if t == 13:
                        act.drain().then_inc(vv_in, 1)
                        act.wait_ge(v_turned, n(v_turned))
                        nc.scalar.activation(v_tok[:].rearrange("p t w -> p (t w)"), bank[5][:], ACT.Copy).then_inc(bank_free[5], 1)
                        act.drain().then_inc(v_copied, 1)
                        for v in range(2):
                            act.wait_ge(sgw_turned, n(sgw_turned))
                            nc.scalar.activation(sgw_t[:, 4 * v:4 * v + 4].rearrange("p h w -> p (h w)"), bank[6 + v][:],
                                                 ACT.Copy).then_inc(bank_free[6 + v], 1)
                        act.drain().then_inc(sgw_copied, 1)
                    if t == 6:
                        for v in range(TT):
                            act.wait_ge(vv_turned, n(vv_turned))
                            nc.scalar.activation(vv_tok[:, v], bank[4 + v][:], ACT.Copy).then_inc(bank_free[4 + v], 1)
                        act.drain().then_inc(vv_copied, 1)
                act.wait_ge(vv_summed, n(vv_summed))
                nc.scalar.activation(gate_dev, gate_dev, ACT.Sqrt, bias=eps[:, 0:1], scale=1.0 / HEAD).then_inc(vv_rooted, 1)

                def exps(u):
                    act.wait_ge(max_ready, n(max_ready))
                    nc.scalar.activation(prob[:, u % 4], bank[2 + u % 3][:], ACT.Exp, bias=shift[:, u % 4:u % 4 + 1],
                                         scale=HEAD ** -0.5, accum_out=total[:, u % 4:u % 4 + 1]).then_inc(exp_ready, 1)

                def head_out(j):
                    act.wait_ge(head_done, n(head_done, 2))
                    nc.scalar.activation(oa_sq[:, j], bank[j % 2][:], ACT.Square).then_inc(sq_ready, 1)
                    nc.scalar.activation(oa[:, j], bank[j % 2][:], ACT.Copy).then_inc(bank_free[j % 2], 1)

                exps(0)
                for u in range(UNITS):
                    if u + 1 < UNITS:
                        exps(u + 1)
                    h, t = u // TT, u % TT
                    act.wait_ge(prob_turned, n(prob_turned))
                    nc.scalar.activation(prob_t[h % 2][:, :, t * P:(t + 1) * P], bank[6 + u % 2][:].rearrange("p (s w) -> p s w", s=TT),
                                         ACT.Copy).then_inc(bank_free[6 + u % 2], 1)
                    act.drain().then_inc(prob_copied, 1)
                    if t == 2 and h % 2 == 0 and h:
                        head_out(h // 2 - 1)
                    j = u - MIX_AT[-1] - 4
                    if 0 <= j < 4:
                        if j == 0:
                            act.wait_ge(gated_ready, n(gated_ready, 4))
                        nc.scalar.activation(ua_sq[:, j], ua[:, j], ACT.Square).then_inc(sq_ready, 1)
                deviation(4 * P)
                head_out(3)
                deviation(4 * P)
                stay(1, sq_in)

            def stay(slabs, sq):
                load_root()

                def body(i):
                    for t in range(RING):
                        for _ in range(slabs - 1):
                            slab()
                        act.wait_ge(slab_done, n(slab_done))
                        if sq is not None:
                            act.wait_ge(x_ready, n(x_ready))
                        split()
                        if sq is not None:
                            k = bass.ds(i * RING + t, 1)
                            nc.scalar.activation(sq[:, k], x[:, k], ACT.Square).then_inc(sq_ready, 1)
                turns(2, RING * slabs, body, [(x_ready, RING)] if sq is not None else [])
                at["bank"] += KD

            def conv_ffn(i):
                deviation(D)
                first = at["bank"]
                base = i * 8 * KF

                def body(j):
                    for p in range(2):
                        for v in range(2):
                            slab()
                            k = j * 2 + (p + v * KF + base)
                            nc.scalar.activation(tmp[:, 2 * p + v], bank[(first + 2 * p + v) % RING][:], ACT.Identity,
                                                 scale=col_at("up_conv", k + 2 * KF), bias=col_at("up_conv", k + 6 * KF))\
                                .then_inc(act_for_dve, 1)
                        act.wait_ge(dve_for_act, n(dve_for_act))
                        nc.scalar.activation(tmp[:, 2 * p], tmp[:, 2 * p], ACT.Silu).then_inc(act_for_dve, 1)
                turns(KF // 2, RING, body, [(dve_for_act, 2)])
                at["bank"] += 2 * KF
                stay(3, sq_ffn if i == 0 else None)

            act.wait_ge(eps_ready, 1)
            for _ in range(AHEAD):
                split()
            act.wait_ge(par_ready, 1)
            act.wait_ge(lstm_in, 16 * 6)
            for part in [ab, lambda: ffn(0), c, lambda: ffn(1), lambda: gated(0), lambda: conv_ffn(0),
                         lambda: gated(1), lambda: conv_ffn(1)][:upto]:
                part()

        @block.vector
        def _(dve):
            n = Count()
            at = {"split": 0, "bank": 0}

            def split():
                if at["split"] < N_SLABS:
                    s = at["split"] % RING
                    dve.wait_ge(hi_done, n(hi_done))
                    nc.vector.tensor_tensor(w_lo[:, s], w_raw[:, s], w_hi[:, s].bitcast(F32), ALU.subtract).then_inc(lo_done, 1)
                    at["split"] += 1

            def turns(times, slabs, body, extra=()):
                dry = at["split"] + times * slabs > N_SLABS
                k = times - dry
                if k > 1:
                    with n.loop(dve, k, [(slab_done, slabs), (hi_done, slabs)] + list(extra)) as i:
                        body(i)
                    at["split"] += (k - 1) * slabs
                elif k:
                    body(0)
                if dry:
                    body(times - 1)

            def step(ins):
                ins.then_inc(vector_step, 1)
                n(vector_step)

            def settle(s=vector_step):
                dve.wait_ge(s, n.now(s))

            def own(ins, s):
                ins.then_inc(s, 1)
                n(s)

            def flag(s):
                dve.drain().then_inc(s, 1)

            def tt(out, x0, x1, op):
                step(nc.vector.tensor_tensor(out, x0, x1, op))

            def ts(out, x0, s1, s2, op0, op1):
                if op1 is None:
                    step(nc.vector.tensor_scalar(out, x0, s1, None, op0))
                else:
                    step(nc.vector.tensor_scalar(out, x0, s1, s2, op0, op1))

            def stt(out, x0, sc, x1, op0, op1):
                step(nc.vector.scalar_tensor_tensor(out, x0, sc, x1, op0, op1))

            def inverse():
                dve.wait_ge(std_ready, n(std_ready))
                nc.vector.reciprocal(inv[:], dev[:]).then_inc(inv_ready, 1)
                flag(bank_free[4])
                dve.wait_ge(scale_ready, n(scale_ready))

            def parts_of_h(srcs, k0):
                for j, src in enumerate(srcs):
                    ts(h_hi[:, k0 + j], src, 1.0, None, ALU.mult, None)
                settle()
                for j, src in enumerate(srcs):
                    own(nc.vector.tensor_tensor(h_lo[:, k0 + j], src, h_hi[:, k0 + j].bitcast(F32), ALU.subtract), h_ready)
                settle(h_ready)

            def normal_h(src, gain, k0=0):
                inverse()
                for k in range(0, src.shape[1], 2):
                    ts_ = [tmp[:, (k + j) % 4] for j in range(2)]
                    for j in range(2):
                        stt(ts_[j], src[:, k + j], col(gain[0], gain[1] + k + j), bank[5][:], ALU.mult, ALU.mult)
                    settle()
                    parts_of_h(ts_, k0 + k)
                flag(bank_free[5])

            def add_normal(y, gain):
                inverse()
                for k in range(0, KD, 2):
                    for j in range(2):
                        stt(tmp[:, (k + j) % 4], y[:, k + j], col("norm", gain + k + j), bank[5][:], ALU.mult, ALU.mult)
                    settle()
                    for j in range(2):
                        own(nc.vector.tensor_tensor(x[:, k + j], x[:, k + j], tmp[:, (k + j) % 4], ALU.add), x_ready)
                    if k:
                        settle(x_ready)
                flag(bank_free[5])

            def only_split(slabs):
                for _ in range(slabs):
                    split()
                    n(slab_done)

            def leave(slabs):
                def body(i):
                    only_split(RING * slabs)
                turns(2, RING * slabs, body)
                at["bank"] += KD

            def s5_prepare():
                v = [s5_v[:, i] for i in range(24)]
                are = par[:, ROWS["a_re"]:ROWS["a_re"] + GROUPS]
                aim = par[:, ROWS["a_im"]:ROWS["a_im"] + GROUPS]
                for j in range(2):
                    dve.wait_ge(prep["pe_to_vector"], n(prep["pe_to_vector"]))
                    step(nc.vector.tensor_copy(s5_c[:, j], bank[5 + j][:].rearrange("p (g w) -> p g w", g=GROUPS)))
                    flag(bank_free[5 + j])
                dve.wait_ge(prep["scalar_to_vector"], n(prep["scalar_to_vector"]))
                settle()
                tt(v[1], v[0], are, ALU.mult)
                tt(v[2], v[0], aim, ALU.mult)
                settle()
                ts(v[3], v[2], 1.0 / TWO_PI, ROUND, ALU.mult, ALU.add)
                settle()
                ts(v[3], v[3], -ROUND, None, ALU.add, None)
                settle()
                stt(v[4], v[3], -PI_HIGH, v[2], ALU.mult, ALU.add)
                settle()
                stt(v[4], v[3], -PI_MID, v[4], ALU.mult, ALU.add)
                settle()
                stt(v[4], v[3], -PI_LOW, v[4], ALU.mult, ALU.add)
                settle()
                ts(v[4], v[4], PI_IN, -PI_IN, ALU.min, ALU.max)
                settle()
                ts(v[5], v[4], TWO_PI / 4, None, ALU.add, None)
                settle()
                ts(v[6], v[5], PI_IN, -TWO_PI, ALU.is_gt, ALU.mult)
                settle()
                tt(v[5], v[5], v[6], ALU.add)
                settle()
                nc.vector.tensor_scalar(v[5], v[5], PI_IN, -PI_IN, ALU.min, ALU.max).then_inc(prep["vector_to_scalar"], 1)
                dve.wait_ge(early_in, 16)
                dve.wait_ge(prep["scalar_to_vector"], n(prep["scalar_to_vector"]))
                tt(v[10], v[7], v[9], ALU.mult)
                tt(v[11], v[7], v[8], ALU.mult)
                tt(v[12], are, are, ALU.mult)
                tt(v[13], aim, aim, ALU.mult)
                settle()
                tt(v[12], v[12], v[13], ALU.add)
                ts(v[14], v[10], -1.0, None, ALU.add, None)
                settle()
                step(nc.vector.reciprocal(v[12], v[12]))
                tt(v[15], v[14], are, ALU.mult)
                tt(v[16], v[11], aim, ALU.mult)
                tt(v[17], v[11], are, ALU.mult)
                tt(v[18], v[14], aim, ALU.mult)
                settle()
                tt(v[15], v[15], v[16], ALU.add)
                tt(v[17], v[17], v[18], ALU.subtract)
                settle()
                tt(v[15], v[15], v[12], ALU.mult)
                tt(v[17], v[17], v[12], ALU.mult)
                settle()
                ts(v[16], v[17], sign, None, ALU.mult, None)
                settle()

                def over(t):
                    return t.unsqueeze(2).to_broadcast([P, GROUPS, GW])

                t0 = tmp[:, 0].rearrange("p (g w) -> p g w", g=GROUPS)
                t1 = tmp[:, 1].rearrange("p (g w) -> p g w", g=GROUPS)
                tt(s5_bb[:, 0], over(v[15]), s5_b[:, 0], ALU.mult)
                tt(t0, over(v[16]), s5_b[:, 1], ALU.mult)
                tt(s5_bb[:, 1], over(v[15]), s5_b[:, 1], ALU.mult)
                tt(t1, over(v[16]), s5_b[:, 0], ALU.mult)
                settle()
                tt(s5_bb[:, 0], s5_bb[:, 0], t0, ALU.add)
                tt(s5_bb[:, 1], s5_bb[:, 1], t1, ALU.subtract)
                re, im = s5_pow[:, 0], s5_pow[:, 1]
                step(nc.vector.memset(re[:, 0], 1.0))
                step(nc.vector.memset(im[:, 0], 0.0))
                step(nc.vector.tensor_copy(re[:, 1], v[10]))
                step(nc.vector.tensor_copy(im[:, 1], v[11]))
                settle()
                for m_ in (1, 2, 4):
                    def last(t):
                        return t[:, m_:m_ + 1].to_broadcast([P, m_, GROUPS])

                    t2 = tmp[:, 2].rearrange("p (k g) -> p k g", g=GROUPS)[:, 0:m_]
                    t3 = tmp[:, 3].rearrange("p (k g) -> p k g", g=GROUPS)[:, 0:m_]
                    a_, b_ = slice(1, m_ + 1), slice(m_ + 1, 2 * m_ + 1)
                    tt(re[:, b_], re[:, a_], last(re), ALU.mult)
                    tt(t2, im[:, a_], last(im), ALU.mult)
                    tt(im[:, b_], re[:, a_], last(im), ALU.mult)
                    tt(t3, im[:, a_], last(re), ALU.mult)
                    settle()
                    tt(re[:, b_], re[:, b_], t2, ALU.subtract)
                    tt(im[:, b_], im[:, b_], t3, ALU.add)
                    settle()
                ims = tmp[:, 2, 0:STEP * GROUPS].rearrange("p (k g) -> p k g", g=GROUPS)
                ts(ims, im[:, 0:STEP], sign, None, ALU.mult, None)
                settle()

                def powers(t):
                    return t.rearrange("p k g -> p g k").unsqueeze(3).to_broadcast([P, GROUPS, STEP, GW])

                def weights(t):
                    return t.unsqueeze(2).to_broadcast([P, GROUPS, STEP, GW])

                tt(s5_q[:], weights(s5_bb[:, 0]), powers(re[:, 0:STEP]), ALU.mult)
                tt(s5_big[:], weights(s5_bb[:, 1]), powers(ims), ALU.mult)
                settle()
                nc.vector.tensor_tensor(s5_q[:], s5_q[:], s5_big[:], ALU.add).then_inc(prep["vector_to_pe"], 1)
                step(nc.vector.tensor_scalar(s5_cx[:], s5_c[:, 0], sign, -1.0, ALU.mult, ALU.mult))
                settle()
                flag(prep["vector_to_pe"])
                tt(s5_out[:], weights(s5_cx[:]), powers(re[:, 1:STEP + 1]), ALU.mult)
                tt(s5_big[:], weights(s5_c[:, 1]), powers(im[:, 1:STEP + 1]), ALU.mult)
                settle()
                nc.vector.tensor_tensor(s5_out[:], s5_out[:], s5_big[:], ALU.subtract).then_inc(prep["vector_to_scalar"], 1)
                ec, es, t2, t3 = v[9], v[8], v[12], v[13]

                def square():
                    tt(t2, ec, ec, ALU.mult)
                    tt(t3, es, es, ALU.mult)
                    tt(es, ec, es, ALU.mult)
                    settle()
                    tt(ec, t2, t3, ALU.subtract)
                    ts(es, es, 2.0, None, ALU.mult, None)
                    settle()

                for _ in range(3):
                    square()
                step(nc.vector.memset(s5_cos[:, :, 0:1], 1.0))
                step(nc.vector.memset(s5_sin[:, :, 0:1], 0.0))
                settle()
                m_ = 1
                while m_ < CH:
                    def by(t):
                        return t.unsqueeze(2).to_broadcast([P, GROUPS, m_])

                    c0, s0, c1, s1 = (t[:, :, k] for t, k in ((s5_cos, slice(0, m_)), (s5_sin, slice(0, m_)),
                                                             (s5_cos, slice(m_, 2 * m_)), (s5_sin, slice(m_, 2 * m_))))
                    t0 = s5_t[:, :, 0:m_]
                    tt(c1, c0, by(ec), ALU.mult)
                    tt(t0, s0, by(es), ALU.mult)
                    tt(s1, c0, by(es), ALU.mult)
                    settle()
                    tt(c1, c1, t0, ALU.subtract)
                    settle()
                    tt(t0, s0, by(ec), ALU.mult)
                    settle()
                    tt(s1, s1, t0, ALU.add)
                    settle()
                    m_ *= 2
                    if m_ < CH:
                        square()
                ts(s5_sin[:], s5_sin[:], sign, -1.0, ALU.mult, ALU.mult)
                settle()
                dve.wait_ge(prep["scalar_to_vector"], n(prep["scalar_to_vector"]))

            def s5_run():
                def flat(t, i):
                    return t[:, 8 * i:8 * i + 8].rearrange("p g c -> p (g c)")

                for i in range(4):
                    dve.wait_ge(s5["pe_to_vector"], n(s5["pe_to_vector"]))
                    tt(flat(s5_w, i), bank[i][:], flat(s5_sin, i), ALU.mult)
                    tt(flat(s5_z, i), flat(s5_state, i), flat(s5_cos, i), ALU.mult)
                    settle()
                    flag(bank_free[i])
                    flag(bank_free[4 + i])
                    tt(flat(s5_w, i), flat(s5_w, i), flat(s5_z, i), ALU.add)
                settle()
                for g in range(GROUPS):
                    step(nc.vector.tensor_tensor_scan(s5_z[:, g], s5_r8[:, g:g + 1].to_broadcast([P, CH]), s5_w[:, g], 0.0,
                                                      ALU.mult, ALU.add))
                settle()
                flag(s5["vector_to_pe"])
                for i in range(4):
                    dve.wait_ge(s5["pe_to_vector"], n(s5["pe_to_vector"]))
                    tt(flat(s5_w, i), bank[4 + i][:], flat(s5_sin, i), ALU.mult)
                    tt(flat(s5_state, i), flat(s5_z, i), flat(s5_cos, i), ALU.mult)
                    settle()
                    flag(bank_free[4 + i])
                    nc.vector.tensor_tensor(flat(s5_state, i), flat(s5_state, i), flat(s5_w, i), ALU.subtract)\
                        .then_inc(s5["vector_to_pe"], 1)
                dve.wait_ge(ys_loaded, 16)
                for k in range(4):
                    step(nc.vector.scalar_tensor_tensor(ys[:, k], us[:, k].rearrange("p i c -> p (i c)"), col("s5_d", k),
                                                        ys[:, k], ALU.mult, ALU.add))
                settle()
                flag(s5["vector_to_scalar"])
                dve.wait_ge(s5["scalar_to_vector"], n(s5["scalar_to_vector"]))
                parts_of_h([yg[:, k] for k in range(4)], 0)
                for t in range(4):
                    split()
                    dve.wait_ge(slab_done, n(slab_done))
                    dve.wait_ge(s5["scalar_to_vector"], n(s5["scalar_to_vector"]))
                    tt(tmp[:, t].rearrange("p (c i) -> p i c", i=STEP), yg[:, t].rearrange("p (i c) -> p i c", i=STEP),
                       gate[:, t].rearrange("p (i c) -> p i c", i=STEP), ALU.mult)
                    flag(bank_free[at["bank"] % RING])
                    at["bank"] += 1
                settle()
                parts_of_h([tmp[:, t] for t in range(4)], 4)

            def lstm_run():
                dve.wait_ge(lstm_in, 16 * 6)
                for v in range(3):
                    tt(lstm_bd[:, v].rearrange("p t (n e) -> p t n e", e=4),
                       lstm_w4[:, v].unsqueeze(2).to_broadcast([P, 4, 32, 4]),
                       quad.unsqueeze(1).unsqueeze(3).to_broadcast([P, 4, 32, 4]), ALU.mult)
                for k in range(4):
                    ts(xc[:, k], xm[:, k], col("conv_w", 12 + k), col("conv_b", k), ALU.mult, ALU.add)
                settle()
                for j in (1, 2, 3):
                    for k in range(4):
                        stt(xc[:, k, j:SEQ], xm[:, k, 0:SEQ - j], col("conv_w", 4 * (3 - j) + k), xc[:, k, j:SEQ],
                            ALU.mult, ALU.add)
                    settle()
                for k in range(4):
                    flag(lstm["vector_to_scalar"])
                r = [rowv[:, j] for j in range(8)]
                dve.wait_ge(lstm["scalar_to_vector"], n(lstm["scalar_to_vector"]))
                stt(r[5], r[1], 0.0, r[4], ALU.min, ALU.subtract)
                settle()
                step(nc.vector.tensor_tensor_scan(r[6], ones[0:M_HEADS, 0:1].to_broadcast([M_HEADS, SEQ]), r[5], 0.0,
                                                  ALU.mult, ALU.add))
                settle()
                tt(r[7], r[0], r[6], ALU.subtract)
                settle()
                step(nc.vector.tensor_tensor_scan(r[2], r[7], r[7], 0.0, ALU.max, ALU.max))
                settle()
                ts(r[3], r[2], -1.0, None, ALU.mult, None)
                tt(r[4], r[6], r[2], ALU.add)
                settle()
                flag(lstm["vector_to_pe"])
                flag(lstm["vector_to_scalar"])
                dve.wait_ge(lstm["pe_to_vector"], n(lstm["pe_to_vector"]))
                step(nc.vector.tensor_copy(g_col, bank[6][:, 0:16].rearrange("p (s h) -> p s h", s=TT)))
                settle()
                flag(bank_free[6])
                for h in range(M_HEADS):
                    dve.wait_ge(lstm["scalar_to_vector"], n(lstm["scalar_to_vector"], 2))
                    flag(bank_free[4])
                    flag(bank_free[5])
                    for t in range(TT):
                        nc.vector.tensor_scalar(lstm_t[:, t, t * P:SEQ], e_m[:, 0, t * P:SEQ], g_col[:, t, h:h + 1], 0.0,
                                                ALU.add, ALU.min).then_inc(lstm["vector_to_scalar"], 1)
                    for t in range(TT):
                        dve.wait_ge(lstm["pe_to_vector"], n(lstm["pe_to_vector"]))
                        dve.wait_ge(lstm["scalar_to_vector"], n(lstm["scalar_to_vector"]))
                        tt(sc_m[:, t, t * P:SEQ], bank[6 + t % 2][:, 0:SEQ - t * P], lstm_t[:, t, t * P:SEQ], ALU.mult)
                        settle()
                        flag(bank_free[6 + t % 2])
                        nc.vector.tensor_tensor(sc_m[:, t, t * P:(t + 1) * P], sc_m[:, t, t * P:(t + 1) * P], causal, ALU.mult)\
                            .then_inc(lstm["vector_to_pe"], 1)
                    dve.wait_ge(lstm["pe_to_vector"], n(lstm["pe_to_vector"]))
                    stt(lstm_t[:, 0], bank[1][:], -1.0, e_m[:, 1], ALU.mult, ALU.max)
                    settle()
                    tt(lstm_t[:, 0], bank[1][:], lstm_t[:, 0], ALU.max)
                    settle()
                    step(nc.vector.reciprocal(lstm_t[:, 1], lstm_t[:, 0]))
                    settle()
                    tt(lstm_t[:, 2], bank[0][:], lstm_t[:, 1], ALU.mult)
                    settle()
                    flag(lstm["vector_to_pe"])
                    flag(bank_free[0])
                    flag(bank_free[1])
                    dve.wait_ge(lstm["pe_to_vector"], n(lstm["pe_to_vector"]))
                    stt(lstm_t[:, 3], bank[2][:], -1.0 / P, lstm_t[:, 2], ALU.mult, ALU.add)
                    settle()
                    flag(lstm["vector_to_scalar"])
                    flag(bank_free[2])
                    ts(tmp[:, 0], xc[:, h], col("skip", h), None, ALU.mult, None)
                    dve.wait_ge(lstm["scalar_to_vector"], n(lstm["scalar_to_vector"]))
                    flag(bank_free[3])
                    step(nc.vector.reciprocal(tmp[:, 1], lstm_t[:, 1]))
                    settle()
                    tt(tmp[:, 2], lstm_t[:, 3], tmp[:, 1], ALU.mult)
                    settle()
                    stt(tmp[:, 2], tmp[:, 2], col("mh_gain", h), tmp[:, 0], ALU.mult, ALU.add)
                    settle()
                    tt(tmp[:, 3], tmp[:, 2], zs[:, h], ALU.mult)
                    settle()
                    parts_of_h([tmp[:, 3]], h)

            def lower_bounds():
                e, w = small[:, 0:16], small[:, 16:32]
                r0, r1 = (par[:, ROWS["lb_raw"] + 8 * j:ROWS["lb_raw"] + 8 * j + 8] for j in range(2))
                tt(w[:, 0:8], r0, r1, ALU.max)
                settle()
                tt(e[:, 0:8], r0, w[:, 0:8], ALU.subtract)
                tt(e[:, 8:16], r1, w[:, 0:8], ALU.subtract)
                settle()
                flag(hgrn["vector_to_scalar"])
                dve.wait_ge(hgrn["scalar_to_vector"], n(hgrn["scalar_to_vector"]))
                tt(w[:, 0:8], e[:, 0:8], e[:, 8:16], ALU.add)
                settle()
                step(nc.vector.reciprocal(w[:, 8:16], w[:, 0:8]))
                settle()
                tt(e[:, 0:8], e[:, 0:8], w[:, 8:16], ALU.mult)
                tt(e[:, 8:16], e[:, 8:16], w[:, 8:16], ALU.mult)
                settle()
                tt(w[:, 0:8], e[:, 0:8], e[:, 8:16], ALU.add)
                settle()
                tt(lb[:, 0], w[:, 0:8], e[:, 0:8], ALU.subtract)
                settle()
                ts(lb[:, 1], lb[:, 0], -1.0, 1.0, ALU.mult, ALU.add)
                ts(lb[:, 2], lb[:, 0], 1.0, None, ALU.subtract, None)
                settle()

            def ab():
                s5_prepare()
                lower_bounds()
                normal_h(x, ("norm", 0))
                only_split(12)
                at["bank"] += 12
                s5_run()
                lstm_run()
                leave(1)
                add_normal(y_mix, 8)

            def ffn(i):
                normal_h(x, ("norm", 32 * i + 16))
                first = at["bank"]

                def body(j):
                    for p in range(2):
                        only_split(2)
                        g, u = (first + 2 * p) % RING, (first + 2 * p + 1) % RING
                        dve.wait_ge(slab_done, n.now(slab_done))
                        dve.wait_ge(act_for_dve, n(act_for_dve))
                        k = bass.ds(j * 2 + p, 1)
                        tt(tmp[:, 2 + p], bank[u][:], tmp[:, p], ALU.mult)
                        flag(bank_free[g])
                        flag(bank_free[u])
                        settle()
                        ts(hid_hi[:, k], tmp[:, 2 + p:3 + p], 1.0, None, ALU.mult, None)
                        settle()
                        own(nc.vector.tensor_tensor(hid_lo[:, k], tmp[:, 2 + p:3 + p], hid_hi[:, k].bitcast(F32), ALU.subtract),
                            hid_ready)
                        settle(hid_ready)
                turns(KF // 2, RING, body, [(act_for_dve, 2), (vector_step, 4), (hid_ready, 2)])
                at["bank"] += 2 * KF
                leave(3)
                add_normal(y_ffn, 32 * i + 24)

            def c():
                normal_h(x, ("norm", 32))
                chunk = 8
                decay = small[:, 32:40]
                first = at["bank"]
                bank_of = [bank[(first + t) % RING] for t in range(RING)]
                free = [bank_free[(first + t) % RING] for t in range(RING)]
                b3, d3, e3 = (t[:].rearrange("p (c t) -> p c t", c=chunk) for t in (c_b, c_d, c_e))

                def turn(gemm, mixer):
                    if gemm is not None:
                        k = bass.ds(gemm, 1)
                        low, kept, less = lb[:, 0, k], lb[:, 1, k], lb[:, 2, k]
                        only_split(1)
                        dve.wait_ge(hgrn["scalar_to_vector"], n(hgrn["scalar_to_vector"]))
                        tt(c_q[:], bank_of[0][:], c_sig[:, 0], ALU.mult)
                        flag(free[0])
                        only_split(1)
                    if mixer is not None:
                        dve.wait_ge(hgrn["pe_to_vector"], n(hgrn["pe_to_vector"]))
                        ts(c_s[:], bank[6][:].rearrange("p (t w) -> p t w", t=TT), HUGE, -HUGE, ALU.min, ALU.max)
                        flag(bank_free[6])
                        settle()
                        tt(c_s[:], c_s[:], causal_c.unsqueeze(1).to_broadcast([P, TT, P]), ALU.mult)
                        flag(hgrn["vector_to_pe"])
                    if mixer is not None:
                        dve.wait_ge(hgrn["pe_to_vector"], n(hgrn["pe_to_vector"]))
                        step(nc.vector.tensor_copy(c_state[:, 1], bank[7][:, 0:P]))
                        for j in range(1, 7):
                            settle()
                            stt(c_state[:, j + 1], c_state[:, j], decay[:, j:j + 1],
                                bank[4 if j % 2 else 7][:, (j // 2) * P:(j // 2 + 1) * P], ALU.mult, ALU.add)
                        flag(bank_free[7])
                        flag(bank_free[4])
                        flag(hgrn["vector_to_pe"])
                    if gemm is not None:
                        dve.wait_ge(hgrn["scalar_to_vector"], n(hgrn["scalar_to_vector"]))
                        ts(c_k[:].unsqueeze(1), c_sig[:, 1:2], less, kept, ALU.mult, ALU.add)
                        nc.vector.tensor_scalar(c_f[:].unsqueeze(1), c_sig[:, 1:2], kept, low, ALU.mult, ALU.add)\
                            .then_inc(hgrn["vector_to_scalar"], 1)
                        flag(free[1])
                        only_split(1)
                        dve.wait_ge(hgrn["scalar_to_vector"], n(hgrn["scalar_to_vector"]))
                        tt(gc[:, k], bank_of[2][:].unsqueeze(1), c_sig[:, 2:3], ALU.mult)
                        flag(free[2])
                        dve.wait_ge(hgrn["scalar_to_vector"], n(hgrn["scalar_to_vector"]))
                        step(nc.vector.tensor_tensor_scan(c_b[:], restart, c_f[:], 0.0, ALU.mult, ALU.add))
                        settle()
                        nc.vector.tensor_tensor(d3, b3, b3[:, :, C_CHUNK - 1:C_CHUNK].to_broadcast([P, chunk, C_CHUNK]), ALU.subtract)\
                            .then_inc(hgrn["vector_to_scalar"], 1)
                        dve.wait_ge(hgrn["scalar_to_vector"], n(hgrn["scalar_to_vector"]))
                        step(nc.vector.tensor_copy(decay, e3[:, :, C_CHUNK - 1]))
                        settle()
                        tt(c_e[:], c_q[:], c_e[:], ALU.mult)
                        tt(c_d[:], c_q[:], tmp[:, 0], ALU.mult)
                        tt(c_k[:], c_k[:], tmp[:, 1], ALU.mult)
                        flag(hgrn["vector_to_pe"])
                        only_split(1)
                    if mixer is not None:
                        k = bass.ds(mixer, 1)
                        dve.wait_ge(hgrn["scalar_to_vector"], n(hgrn["scalar_to_vector"]))
                        step(nc.vector.reciprocal(tmp[:, 3], tmp[:, 2]))
                        flag(bank_free[6])
                        settle()
                        tt(tmp[:, 2], bank[5][:], tmp[:, 3], ALU.mult)
                        flag(bank_free[5])
                        settle()
                        stt(tmp[:, 3:4], tmp[:, 2:3], col_at("c_gain", mixer), gc[:, k], ALU.mult, ALU.mult)
                        settle()
                        ts(mix_hi[:, k], tmp[:, 3:4], 1.0, None, ALU.mult, None)
                        settle()
                        own(nc.vector.tensor_tensor(mix_lo[:, k], tmp[:, 3:4], mix_hi[:, k].bitcast(F32), ALU.subtract), h_ready)
                        settle(h_ready)

                turn(0, None)
                per = [(slab_done, RING), (hi_done, RING), (hgrn["scalar_to_vector"], 6), (hgrn["pe_to_vector"], 2),
                       (vector_step, 21), (h_ready, 1)]
                with n.loop(dve, C_HEADS - 1, per) as i:
                    turn(i + 1, i)
                at["split"] += RING * (C_HEADS - 2)
                turn(None, C_HEADS - 1)
                at["bank"] += RING * C_HEADS
                leave(1)
                add_normal(y_mix, 40)

            def gated(i):
                normal_h(x, ("attn_norm", 8 * i))
                for v, half in enumerate((slice(HEAD, P), slice(0, HEAD), slice(HEAD, P), slice(0, HEAD))):
                    step(nc.vector.memset(k_pad[half, v], 0.0))
                only_split(6)
                dve.wait_ge(qk_rooted, n(qk_rooted))
                own(nc.vector.reciprocal(head_dev, head_dev), qk_inverted)
                flag(bank_free[4])
                only_split(1)
                dve.wait_ge(late_in, 16 * 11 * (i + 1))
                for j in (4, 0, 1, 2, 3):
                    dve.wait_ge(qk_spread, n(qk_spread))
                    own(nc.vector.scalar_tensor_tensor(qa[:, j], qa[:, j], col("q_norm" if j < 4 else "k_norm", i),
                                                       bank[4 + j % 4][:], ALU.mult, ALU.mult), qk_normal)
                    flag(bank_free[4 + j % 4])
                only_split(1)
                settle(qk_normal)
                for place_, j in enumerate((4, 0, 1, 2, 3)):
                    a_, b = tmp[:, place_ % 4], 4 + j % 4
                    dve.wait_ge(qk_partner, n(qk_partner))
                    tt(a_, bank[b][:], sin, ALU.mult)
                    tt(qa[:, j], qa[:, j], cos, ALU.mult)
                    settle()
                    flag(bank_free[b])
                    if j == 4:
                        own(nc.vector.tensor_tensor(qa[:, j], qa[:, j], a_, ALU.add), k_turned)
                    else:
                        tt(qa[:, j], qa[:, j], a_, ALU.add)
                    if j == 0:
                        settle(k_turned)
                        step(nc.vector.tensor_copy(k_pad[0:HEAD, 0], qa[0:HEAD, 4]))
                        step(nc.vector.tensor_copy(k_pad[HEAD:P, 3], qa[HEAD:P, 4]))
                        only_split(1)
                    if j == 2:
                        only_split(1)
                dve.wait_ge(k_swapped, n(k_swapped))
                step(nc.vector.tensor_copy(k_pad[0:HEAD, 2], bank[4][0:HEAD]))
                step(nc.vector.tensor_copy(k_pad[HEAD:P, 1], bank[4][HEAD:P]))
                flag(bank_free[4])
                flag(q_turned)
                only_split(2)
                dve.wait_ge(vv_copied, n(vv_copied))
                for t in range(TT):
                    tt(tmp[:, t], vv_tok[:, t], vv_tok[:, t], ALU.mult)
                settle()
                for t in range(TT):
                    step(nc.vector.tensor_reduce(gate_dev[:, 8 * t:8 * t + 8], tmp[:, t].rearrange("p (h d) -> p h d", h=8),
                                                 AX.X, ALU.add))
                flag(vv_summed)
                only_split(2)
                dve.wait_ge(vv_rooted, n(vv_rooted))
                settle()
                step(nc.vector.reciprocal(gate_dev, gate_dev))
                settle()
                for t in range(TT):
                    tt(vv_tok[:, t].rearrange("p (h d) -> p h d", h=8), vv_tok[:, t].rearrange("p (h d) -> p h d", h=8),
                       gate_dev[:, 8 * t:8 * t + 8].unsqueeze(2).to_broadcast([P, 8, HEAD]), ALU.mult)
                settle()
                for t in range(TT):
                    tt(vv_tok[:, t], vv_tok[:, t], sgn[:], ALU.mult)
                flag(vv_normal)

                def maxima(u):
                    c = u % 4
                    dve.wait_ge(score_ready, n(score_ready))
                    step(nc.vector.tensor_reduce(top_score[:, c:c + 1], bank[2 + u % 3][:], AX.X, ALU.max))
                    settle()
                    own(nc.vector.tensor_scalar(shift[:, c:c + 1], top_score[:, c:c + 1], -HEAD ** -0.5, None, ALU.mult), max_ready)

                maxima(0)
                maxima(1)
                for u in range(UNITS):
                    c = u % 4
                    dve.wait_ge(exp_ready, n(exp_ready))
                    step(nc.vector.reciprocal(share[:, c:c + 1], total[:, c:c + 1]))
                    flag(bank_free[2 + u % 3])
                    settle()
                    own(nc.vector.tensor_scalar(prob[:, c], prob[:, c], share[:, c:c + 1], None, ALU.mult), prob_ready)
                    if u + 2 < UNITS:
                        maxima(u + 2)
                    if u - 1 in MIX_AT:
                        j = MIX_AT.index(u - 1)
                        dve.wait_ge(gate_mixed, n(gate_mixed))
                        tt(mixed[:].rearrange("p (c w) -> p c w", c=TT), bank[5][:].rearrange("p (c w) -> p c w", c=TT),
                           sgb[:, j].unsqueeze(1).to_broadcast([P, TT, P]), ALU.add)
                        settle()
                        flag(bank_free[5])
                        own(nc.vector.tensor_tensor(ua[:, j], ua[:, j], mixed[:], ALU.mult), gated_ready)
                settle(prob_ready)
                at["bank"] += len(IN_ORDER)
                normal_h(ua, ("sg_gain", 4 * i), 4)
                normal_h(oa, ("attn_gain", 4 * i), 0)
                add_result(1)

            def add_result(slabs):
                first = at["bank"]

                def body(i):
                    for t in range(RING):
                        only_split(slabs - 1)
                        b = (first + t) % RING
                        dve.wait_ge(slab_done, n(slab_done))
                        k = bass.ds(i * RING + t, 1)
                        own(nc.vector.tensor_tensor(x[:, k], x[:, k], bank[b][:].unsqueeze(1), ALU.add), x_ready)
                        flag(bank_free[b])
                        split()
                turns(2, RING * slabs, body, [(x_ready, RING)])
                at["bank"] += KD

            def conv_ffn(i):
                normal_h(x, ("ffn_norm", 8 * i))
                first = at["bank"]
                base = i * 8 * KF

                def body(j):
                    for p in range(2):
                        only_split(2)
                        for v in range(2):
                            b = (first + 2 * p + v) % RING
                            k = j * 2 + (p + v * KF + base)
                            c_ = tmp[:, 2 * p + v]
                            dve.wait_ge(act_for_dve, n(act_for_dve))
                            stt(c_[:, 1:SEQ], bank[b][:, 0:SEQ - 1], col_at("up_conv", k), c_[:, 1:SEQ], ALU.mult, ALU.add)
                            settle()
                            ins = nc.vector.scalar_tensor_tensor(c_[:, 0:SEQ - 1], bank[b][:, 1:SEQ],
                                                                 col_at("up_conv", k + 4 * KF), c_[:, 0:SEQ - 1], ALU.mult, ALU.add)
                            if v == 0:
                                ins.then_inc(dve_for_act, 1)
                            else:
                                step(ins)
                        settle()
                        dve.wait_ge(act_for_dve, n(act_for_dve))
                        kk = bass.ds(j * 2 + p, 1)
                        tt(tmp[:, 2 * p + 1], tmp[:, 2 * p], tmp[:, 2 * p + 1], ALU.mult)
                        settle()
                        ts(hid_hi[:, kk], tmp[:, 2 * p + 1:2 * p + 2], 1.0, None, ALU.mult, None)
                        settle()
                        own(nc.vector.tensor_tensor(hid_lo[:, kk], tmp[:, 2 * p + 1:2 * p + 2], hid_hi[:, kk].bitcast(F32),
                                                    ALU.subtract), hid_ready)
                        flag(bank_free[(first + 2 * p) % RING])
                        flag(bank_free[(first + 2 * p + 1) % RING])
                        settle(hid_ready)
                turns(KF // 2, RING, body, [(act_for_dve, 6), (vector_step, 10), (hid_ready, 2)])
                at["bank"] += 2 * KF
                add_result(3)

            nc.vector.memset(eps[:], EPS).then_inc(eps_ready, 1)
            for b in range(8):
                flag(bank_free[b])
            for k in range(KD):
                dve.wait_ge(x_turned, n(x_turned))
                step(nc.vector.tensor_copy(x[:, k], bank[k % RING][:]))
                settle()
                flag(bank_free[k % RING])
                own(dve.drain(), x_ready)
            at["bank"] += KD
            for b in range(ROW_BLOCKS):
                dve.wait_ge(par_turned, n(par_turned))
                r = block_rows(b)
                step(nc.vector.tensor_copy(par[:, b * P:b * P + r], bank[4 + b % 4][:, 0:r]))
                settle()
                flag(bank_free[4 + b % 4])
            flag(par_ready)
            for _ in range(AHEAD):
                split()
            for part in [ab, lambda: ffn(0), c, lambda: ffn(1), lambda: gated(0), lambda: conv_ffn(0),
                         lambda: gated(1), lambda: conv_ffn(1)][:upto]:
                part()
            for t in range(TT):
                for v in range(2):
                    b = 4 + (2 * t + v) % 4
                    dve.wait_ge(out_turned, n(out_turned))
                    step(nc.vector.tensor_copy(out_tok[:, t, 512 * v:512 * v + 512], bank[b][:]))
                    settle()
                    flag(bank_free[b])
                    flag(out_ready)


_NAMES = ["x", "norm_g", "ab_w_in", "ab_conv_w", "ab_conv_b", "ab_wq", "ab_wk", "ab_wv", "ab_w_if", "ab_b_if", "ab_mh_gain",
          "ab_skip", "ab_a_re", "ab_a_im", "ab_log_dt", "ab_b_re", "ab_b_im", "ab_c_re", "ab_c_im", "ab_d", "ab_w_glu",
          "ab_b_glu", "ab_w_out", "c_w_in", "c_lb_raw", "c_g_gain", "c_w_out", "ffn_w1", "ffn_w3", "ffn_w2",
          "attn_norm_g_2", "w_in_2", "q_norm_g_2", "k_norm_g_2", "sg_norm_g_2", "sg_w_2", "sg_b_2", "attn_out_g_2",
          "sg_out_g_2", "w_o_2", "ffn_norm_g_2", "w_up_2", "conv_w_2", "conv_b_2", "w_down_2"]


def kernel(**inputs):
    import concourse.bacc as bacc
    from concourse.bass_utils import run_bass_kernel_spmd

    nc = bacc.Bacc("TRN2", target_bir_lowering=False, num_devices=1)
    arrays = {f"in_{k}": np.ascontiguousarray(inputs[k]) for k in _NAMES}
    arrays.update({f"in_{k}": v for k, v in constants().items()})
    aps = {k[3:]: nc.dram_tensor(k, v.shape, F32, kind="ExternalInput").ap() for k, v in arrays.items()}
    aps["out"] = nc.dram_tensor("out_x", (1, SEQ, D), F32, kind="ExternalOutput").ap()
    program(nc, aps, UPTO)
    r = run_bass_kernel_spmd(nc, [arrays], core_ids=[0])
    return r.results[0]["out_x"]


UPTO = 8
```

```python
from contextlib import ExitStack, contextmanager

import numpy as np

import concourse.bass as bass
from concourse import mybir

F32 = mybir.dt.float32
F32R = mybir.dt.float32r
ALU = mybir.AluOpType
ACT = mybir.ActivationFunctionType
AX = mybir.AxisListType

P = 128
SEQ = 512
D = 1024
KD = D // P
TT = SEQ // P
D_FF = 2816
KF = D_FF // P
EPS = 1e-6
UNITS = 8 * TT
MIX_AT = (8, 12, 16, 20)
AB_ORDER = (0, 1, 2, 3, 8, 9, 10, 11, 4, 5, 6, 7)
PARTNERS = ((4, 5), (0, 6), (1, 7), (2, 5), (3, 6))
IN_ORDER = [4, 5, 0, 1, 2, 3, 10, 11, 12, 13, 6, 7, 8, 9]
RING = 4
AHEAD = 4
GROUP = 3
SLAB_K = 8
DOWN = [8, 8, KF - 16]
M_HEADS = 4
GATE_ROW = 32
GATE_COLS = GATE_ROW + M_HEADS
GROUPS, GW, STATE = 32, 16, 64
STEP = 8
CH = SEQ // STEP
C_HEADS = 8
C_CHUNK = 64
HEAD = 64
TWO_PI = float(2 * np.pi)
PI_HIGH = 6.28125
PI_MID = float(np.float32(2 * np.pi - 6.28125))
PI_LOW = float(2 * np.pi - 6.28125 - np.float64(np.float32(2 * np.pi - 6.28125)))
ROUND = 1.5 * 2.0 ** 23
HUGE = 3.0e38
PI_IN = 3.1415925

ROWS = {}


def plan_rows():
    at = 0
    for name, count in (("norm", 64), ("attn_norm", 16), ("ffn_norm", 16), ("conv_w", 16), ("conv_b", 4),
                        ("mh_gain", 4), ("skip", 4), ("s5_d", 4),
                        ("b_glu", 4), ("lb_raw", 16), ("c_gain", 8), ("attn_gain", 8), ("sg_gain", 8),
                        ("q_norm", 2), ("k_norm", 2), ("a_re", 32), ("a_im", 32),
                        ("sg_norm", 8), ("pad", 8), ("up_conv", 2 * 4 * 2 * KF)):
        ROWS[name] = at
        at += count
    return at


N_ROWS = plan_rows()
GAINS = ROWS["attn_norm"]
ROW_BLOCKS = -(-N_ROWS // P)


def constants():
    k = np.arange(P)
    zid = np.zeros((P, 2 * P), np.float32)
    zid[k, P + k] = 1
    lead = np.concatenate([zid, np.ones((P, P), np.float32)], 1)
    quad = (k[:, None] // 4 == np.arange(32)[None, :]).astype(np.float32)
    pick = np.zeros((P, M_HEADS, P), np.float32)
    for h in range(M_HEADS):
        pick[h, h] = 1
    causal = (k[:, None] <= k[None, :]).astype(np.float32)
    causal_c = causal * (k[:, None] // C_CHUNK == k[None, :] // C_CHUNK)
    restart = np.broadcast_to((np.arange(SEQ) % C_CHUNK != 0).astype(np.float32), (P, SEQ))
    swap = (k[:, None] == (k[None, :] + HEAD) % P).astype(np.float32)
    sign = np.where(k < HEAD, -1.0, 1.0).astype(np.float32)[:, None]
    early = np.concatenate([quad, pick.reshape(P, -1), causal, causal_c, restart, swap, sign], 1)
    inv = (1.0 / (np.float32(10000.0) ** (np.arange(0, 32, 2, dtype=np.float32) / np.float32(32)))).astype(np.float32)
    t = np.arange(SEQ)
    within = k % HEAD
    pos = np.where((within < 32)[:, None], (t // 64)[None, :], (t % 64)[None, :]).astype(np.float32)
    ang = pos * inv[within % 16][:, None]
    upper = (within % 32) >= 16
    cos = np.cos(ang).astype(np.float32)
    sin = (np.sin(ang) * np.where(upper, 1, -1)[:, None]).astype(np.float32)
    partner = np.where(upper, k - 16, k + 16)
    turn = (k[:, None] == partner[None, :]).astype(np.float32)
    block = (k[:, None] // HEAD == k[None, :] // HEAD).astype(np.float32)
    late = np.concatenate([cos, sin, turn, block], 1)
    return {"lead": lead, "early": np.ascontiguousarray(early), "late": late}


class Count:

    def __init__(self):
        self.seen, self.shift = {}, {}

    def __call__(self, sem, by=1):
        self.seen[sem.name] = self.seen.get(sem.name, 0) + by
        return self.now(sem)

    def now(self, sem):
        value = self.seen.get(sem.name, 0)
        return value if sem.name not in self.shift else self.shift[sem.name] + value

    @contextmanager
    def loop(self, eng, times, per):
        before = dict(self.seen)
        with eng.Fori(0, times) as i:
            self.shift = {sem.name: i * by for sem, by in per}
            yield i
        self.shift = {}
        turn = {k: v - before.get(k, 0) for k, v in self.seen.items() if v != before.get(k, 0)}
        want = {sem.name: by for sem, by in per}
        assert turn == want, f"per turn {turn}, not {want}"
        for k, v in want.items():
            self.seen[k] += (times - 1) * v


def program(nc, a):
    ctx = ExitStack()
    with ctx:
        top = [-(-nc.sbuf_base // 64) * 64]

        def place(name, shape, dt=F32, at=None):
            size = 4 * int(np.prod(shape[1:]))
            if at is None:
                at = top[0]
                top[0] += -(-size // 32) * 32
                assert top[0] <= nc.sbuf_usable_end, (name, top[0])
            return nc.alloc_sbuf_tensor_at(name, list(shape), dt, offset=at)

        def sem(name):
            return ctx.enter_context(nc.semaphore(name))

        w_raw = place("w_raw", [P, RING, SLAB_K, P])
        w_hi = place("w_hi", [P, RING, SLAB_K, P], F32R)
        w_lo = place("w_lo", [P, RING, SLAB_K, P], F32R)
        x = place("x", [P, KD, SEQ])
        H0 = top[0]
        h_hi = place("h_hi", [P, KD, SEQ], F32R)
        h_lo = place("h_lo", [P, KD, SEQ], F32R)
        M0 = top[0]
        hid_hi = place("hid_hi", [P, KF, SEQ], F32R)
        hid_lo = place("hid_lo", [P, KF, SEQ], F32R)
        M1 = top[0]
        par = place("par", [P, ROW_BLOCKS * P])
        lead = place("lead", [P, 3 * P])
        shifted, ident, ones = lead[:, 0:2 * P], lead[:, P:2 * P], lead[:, 2 * P:3 * P]
        early = place("early", [P, 32 + 4 * P + 2 * P + SEQ + P + 1])
        quad = early[:, 0:32]
        pick = early[0:M_HEADS, 32:32 + 4 * P].rearrange("k (h m) -> k h m", h=M_HEADS)
        causal = early[:, 544:672]
        causal_c = early[:, 672:800]
        restart = early[:, 800:1312]
        swap = early[:, 1312:1440]
        sign = early[:, 1440:1441]
        eps = place("eps", [P, 1])
        sq_sum = place("sq_sum", [P, SEQ])
        dev = place("dev", [P, TT])
        inv = place("inv", [P, TT])
        inv_all = sq_sum[:]
        warm = place("warm", [P, 1])
        tmp = place("tmp", [P, 4, SEQ])
        small = place("small", [P, 256])
        lstm_w4 = place("lstm_w4", [P, 3, 4, 4])
        lstm_wif = place("lstm_wif", [P, 12, 8])
        lstm_bif = place("lstm_bif", [GATE_COLS, 2])
        lb = place("lb", [P, 8, 8])

        def m(name, shape, kb, dt=F32):
            assert M0 + 1024 * kb + 4 * int(np.prod(shape[1:])) <= M1, name
            return place(name, shape, dt, at=M0 + int(1024 * kb))

        def hm(name, shape, kb):
            assert H0 + 1024 * kb + 4 * int(np.prod(shape[1:])) <= M0, name
            return place(name, shape, F32, at=H0 + int(1024 * kb))

        x_tok = m("x_tok", [P, TT, D], 0)
        rows = m("rows", [P, ROW_BLOCKS, P], 16)
        out_tok = m("out_tok", [P, TT, D], 0)
        sq_ab = m("sq_ab", [P, KD, SEQ], 56)
        sq_in = m("sq_in", [P, KD, SEQ], 64)
        y_mix = m("y_mix", [P, KD, SEQ], 64)
        sq_mix = m("sq_mix", [P, KD, SEQ], 0)
        y_ffn = hm("y_ffn", [P, KD, SEQ], 0)
        sq_ffn = hm("sq_ffn", [P, KD, SEQ], 16)
        xm = m("xm", [P, 4, SEQ], 0)
        zs = m("zs", [P, 4, SEQ], 8)
        us = m("us", [P, 4, STEP, CH], 16)
        s5_in = m("s5_in", [P, GROUPS, P], 24)
        s5_out = m("s5_out", [P, GROUPS, STEP, GW], 40)
        s5_conv = m("s5_conv", [P, GROUPS, STEP, GW], 56)
        s5_cos = m("s5_cos", [P, GROUPS, CH], 72)
        s5_sin = m("s5_sin", [P, GROUPS, CH], 80)
        s5_q = m("s5_q", [P, GROUPS, STEP, GW], 56)
        s5_b = m("s5_b", [P, 2, GROUPS, GW], 72)
        s5_bb = m("s5_bb", [P, 2, GROUPS, GW], 76)
        s5_crow = m("s5_crow", [P, 2, 4, P], 40)
        s5_c = m("s5_c", [P, 2, GROUPS, GW], 80)
        s5_cx = m("s5_cx", [P, GROUPS, GW], 84)
        s5_k = sq_sum[:].rearrange("p (g w) -> p g w", g=GROUPS)
        s5_pow = m("s5_pow", [P, 2, STEP + 1, GROUPS], 20)
        s5_big = m("s5_big", [P, GROUPS // 4, STEP, GW], 16)
        s5_v = place("s5_v", [P, 16, GROUPS])
        gate_w = s5_v[:].rearrange("p v g -> p (v g)")[:, 0:12 * GATE_COLS].rearrange("p (k g) -> p k g", k=12)
        s5_ldt = small[:, 152:152 + GROUPS]
        s5_t = tmp[:, 0:2].rearrange("p t n -> p (t n)").rearrange("p (g c) -> p g c", g=GROUPS)
        s5_r8 = place("s5_r8", [P, GROUPS])
        u_step = m("u_step", [P, GROUPS, CH], 16)
        s5_state = hm("s5_state", [P, GROUPS, CH], 8)
        s5_w = hm("s5_w", [P, GROUPS, CH], 16)
        s5_z = hm("s5_z", [P, GROUPS, CH], 24)
        ys_step = hm("ys_step", [P, GROUPS, CH], 16)
        ys = m("ys", [P, 4, SEQ], 64)
        gate = hm("gate", [P, 4, SEQ], 8)
        gated_ys = m("gated_ys", [P, 4, SEQ], 16)
        xc = tmp
        lstm_bd = m("lstm_bd", [P, 4, 4, P], 24)
        neg_top = sq_sum
        qm = m("qm", [P, 4, SEQ], 32)
        vt = m("vt", [P, 4, TT, P], 40)
        rowv = m("rowv", [M_HEADS, 8, SEQ], 48)
        km = m("km", [P, 4, SEQ], 72)
        vf = m("vf", [P, 4, SEQ], 80)
        lstm_v = m("lstm_v", [P, 4, SEQ], 0)
        sc_m = m("sc_m", [P, TT, SEQ], 16)
        num_sq = m("num_sq", [P, SEQ], 64)
        g_col, low_col = (small[:, 16 * v:16 * v + 16].rearrange("p (s h) -> p s h", s=TT) for v in range(2))
        den_col, var_col, dev_col, scale_col, value_mean = (small[:, 32 + TT * v:32 + TT * v + TT] for v in range(5))
        lstm_t = m("lstm_t", [P, 4, SEQ], 80)
        c_q = m("c_q", [P, SEQ], 16)
        c_sig = m("c_sig", [P, 3, SEQ], 18)
        gc = m("gc", [P, 8, SEQ], 0)
        mix_hi = m("mix_hi", [P, 8, SEQ], 32, F32R)
        mix_lo = m("mix_lo", [P, 8, SEQ], 48, F32R)
        c_k = m("c_k", [P, SEQ], 64)
        c_f = m("c_f", [P, SEQ], 66)
        c_b = m("c_b", [P, SEQ], 68)
        c_d = m("c_d", [P, SEQ], 70)
        c_e = m("c_e", [P, SEQ], 72)
        c_kt = m("c_kt", [P, TT, P], 74)
        c_it = m("c_it", [P, TT, P], 76)
        c_s = m("c_s", [P, TT, P], 78)
        c_state = m("c_state", [P, 8, P], 80)
        c_i = m("c_i", [P, SEQ], 84)
        c_o = m("c_o", [P, SEQ], 86)
        late = m("late", [P, 2 * SEQ + 2 * P], 0)
        cos, sin = late[:, 0:SEQ], late[:, SEQ:2 * SEQ]
        turn, halves = late[:, 2 * SEQ:2 * SEQ + P], late[:, 2 * SEQ + P:2 * SEQ + 2 * P]
        qa = m("qa", [P, 5, SEQ], 6)
        va = m("va", [P, SEQ], 16)
        ua = m("ua", [P, 4, SEQ], 18)
        vva = m("vva", [P, 4, SEQ], 26)
        v_tok = m("v_tok", [P, TT, P], 34)
        vv_tok = m("vv_tok", [P, TT, SEQ], 36)
        sgw = m("sgw", [P, 8, P], 44)
        mixed = m("mixed", [P, SEQ], 44)
        sgw_t = m("sgw_t", [P, 8, P], 48)
        sgb = m("sgb", [P, 4, P], 52)
        k_pad = m("k_pad", [P, 4, SEQ], 56)
        prob = tmp
        prob_t = [m("prob_t0", [P, TT, SEQ], 64), m("prob_t1", [P, TT, SEQ], 26),
                  hm("prob_t2", [P, TT, SEQ], 0), hm("prob_t3", [P, TT, SEQ], 16)]
        qk_sq = m("qk_sq", [P, 5, SEQ], 72)
        oa = m("oa", [P, 4, SEQ], 72)
        oa_sq = m("oa_sq", [P, 4, SEQ], 80)
        ua_sq = m("ua_sq", [P, 4, SEQ], 36)
        head_dev = small[:, 64:64 + 40]
        head_scale = small[:, 152:152 + 40]
        gate_dev = small[:, 104:104 + 32]
        top_score = small[:, 136:140]
        shift = small[:, 140:144]
        total = small[:, 144:148]
        share = small[:, 148:152]

        bank = [ctx.enter_context(nc.psum_tensor(f"bank{b}", [P, 512], F32)) for b in range(8)]

        us_dram = nc.dram_tensor("us_dram", [4 * P, STEP, CH], F32, kind="Internal").ap()
        ys_dram = nc.dram_tensor("ys_dram", [4 * P, STEP, CH], F32, kind="Internal").ap()

        bank_free = [sem(f"bank{b}_free") for b in range(8)]
        raw_full = [sem(f"raw{s}_full") for s in range(RING)]
        hi_done = sem("hi_done")
        lo_done = sem("lo_done")
        slab_done = sem("slab_done")
        lead_in, x_in, x_in_rest, early_in, gains_in, rows_in, rows_in_fast = (
            sem(k) for k in ("lead_in", "x_in", "x_in_rest", "early_in", "gains_in", "rows_in", "rows_in_fast"))
        s5_in_sem, lstm_in = sem("s5_in"), sem("lstm_in")
        x_turned, x_ready = sem("x_turned"), sem("x_ready")
        gains_turned, par_turned, par_ready = sem("gains_turned"), sem("par_turned"), sem("par_ready")
        eps_ready = sem("eps_ready")
        sq_ready, sum_ready, stat_ready, std_ready = (sem(k) for k in ("sq_ready", "sum_ready", "stat_ready", "std_ready"))
        inv_ready, scale_ready, pool_step = sem("inv_ready"), sem("scale_ready"), sem("pool_step")
        h_scaled, h_high, h_ready, hid_ready = (sem(k) for k in ("h_scaled", "h_high", "h_ready", "hid_ready"))
        act_for_dve, dve_for_act = sem("ffn_scalar_to_vector"), sem("ffn_vector_to_scalar")
        vector_step = sem("vector_step")
        scalar_step = sem("scalar_step")

        def signals(name):
            return {k: sem(f"{name}_{k}") for k in ("pe_to_vector", "pe_to_scalar", "vector_to_pe",
                                                     "scalar_to_pe", "vector_to_scalar", "scalar_to_vector")}

        prep, s5, lstm, hgrn = signals("prep"), signals("s5"), signals("lstm"), signals("hgrn")
        qk_squared, qk_in, qk_summed, qk_rooted, qk_inverted, qk_spread, qk_partner, k_turned, q_turned = (
            sem(f"qk_{k}") for k in ("squared", "in", "summed", "rooted", "inverted", "spread", "partner", "k", "q"))
        k_swapped, v_in, v_turned, v_copied = (sem(k) for k in ("k_swapped", "v_in", "v_turned", "v_copied"))
        vv_in, sgw_turned, sgw_copied, vv_turned, vv_copied, vv_summed, vv_rooted, vv_normal, gate_mixed, gated_ready = (
            sem(k) for k in ("vv_in", "sgw_turned", "sgw_copied", "vv_turned", "vv_copied", "vv_summed", "vv_rooted",
                             "vv_normal", "gate_mixed", "gated_ready"))
        score_ready, max_ready, exp_ready, prob_ready, prob_turned, prob_copied, head_done = (
            sem(k) for k in ("score_ready", "max_ready", "exp_ready", "prob_ready", "prob_turned", "prob_copied", "head_done"))
        top_out, top_in, expo_ready, weight_ready, scored, weighed, head_scaled = (
            sem(f"lstm_{k}") for k in ("top_out", "top_in", "exponent", "weight", "scored", "weighed", "scaled"))
        us_stored, us_loaded, us_back, ys_stored, ys_loaded = (sem(k) for k in ("us_stored", "us_loaded", "us_back", "ys_stored", "ys_loaded"))
        late_in, us_ready, ys_ready = sem("late_in"), sem("us_ready"), sem("ys_ready")
        out_turned, out_ready, out_copied, out_stored = (sem(f"out_{k}") for k in ("turned", "ready", "copied", "stored"))

        def cols(w):
            return w.rearrange("(k p) n -> p k n", p=P)

        SIZE = {"ab_in": 12, "ab_glu": 4, "ab_out": 8, "ffn1": 44, "ffn2": 24, "c_in": 32, "c_out": 8,
                "s_in": 14, "s_out": 8, "up": 44, "down": 24}
        parts = [["ab_in", "ab_glu", "ab_out"], ["ffn1", "ffn2"], ["c_in", "c_out"], ["ffn1", "ffn2"],
                 ["s_in", "s_out"], ["up", "down"], ["s_in", "s_out"], ["up", "down"]]
        row_dmas = {gains_in: 0, rows_in: 0, rows_in_fast: 0}

        def block_rows(b):
            return ROWS["pad"] - P if b == 1 else min(P, N_ROWS - b * P)

        N_SLABS = sum(SIZE[s] for part in parts for s in part)

        def col(name, i=0):
            c = ROWS[name] + i
            return par[:, c:c + 1]

        def col_at(name, i):
            return par[:, bass.ds(i + ROWS[name], 1)]

        def load_rows(queue, landed, src, first):
            at = 0
            while at < src.shape[0]:
                r = (first + at) % P
                k = min(P - r, src.shape[0] - at)
                queue.dma_start(rows[r:r + k, (first + at) // P], src[at:at + k]).then_inc(landed, 16)
                row_dmas[landed] += 1
                at += k

        def load_twice(queue, landed, src, first):
            r, b = first % P, first // P
            for h in range(2):
                queue.dma_start(rows[r:r + src.shape[0], b, HEAD * h:HEAD * h + HEAD], src).then_inc(landed, 16)
                row_dmas[landed] += 1

        block = ctx.enter_context(nc.Block())

        @block.sync
        def _(sp):
            n = Count()
            sp.dma_start(lead[:], a["lead"]).then_inc(lead_in, 16)
            x_rows = a["x"][0].rearrange("(t p) d -> p t d", p=P)
            for half, landed in ((slice(0, D // 2), x_in), (slice(D // 2, D), x_in_rest)):
                sp.dma_start(x_tok[:, :, half], x_rows[:, :, half]).then_inc(landed, 16)
            slab = [0]

            def load(src):
                s = slab[0] % RING
                if slab[0] >= RING:
                    sp.wait_ge(lo_done, n(lo_done))
                sp.dma_start(w_raw[:, s, 0:src.shape[1]], src).then_inc(raw_full[s], 16)
                slab[0] += 1

            def stream(times, slabs, turn):
                if times > 1:
                    with n.loop(sp, times, [(lo_done, slabs)]) as i:
                        turn(i)
                    slab[0] += (times - 1) * slabs
                else:
                    turn(0)

            def plain(w, tiles):
                w = cols(w)

                def turn(i):
                    for t in range(RING):
                        load(w[:, :, bass.ds(i * (RING * P) + t * P, P)])
                stream(tiles // RING, RING, turn)

            def pairs(w, v, at):
                w, v = cols(w), cols(v)

                def turn(i):
                    for t in range(RING // 2):
                        load(w[:, :, bass.ds(i * (RING // 2 * P) + t * P, P)])
                        load(v[:, :, bass.ds(i * (RING // 2 * P) + (t * P + at), P)])
                stream(KF // 2, RING, turn)

            def deep(w):
                w = cols(w)

                def turn(i):
                    for t in range(RING):
                        for k, c in ((0, 8), (8, 8), (16, KF - 16)):
                            load(w[:, k:k + c, bass.ds(i * (RING * P) + t * P, P)])
                stream(2, RING * len(DOWN), turn)

            def first_rows():
                load_rows(sp, rows_in_fast, a["ab_conv_w"][0].rearrange("t (k p) -> (t k) p", p=P), ROWS["conv_w"])
                for i in range(2):
                    first = ROWS["up_conv"] + i * 4 * 2 * KF
                    load_rows(sp, rows_in_fast, a["conv_w_2"][i].rearrange("t (k p) -> (t k) p", p=P), first)
                    load_rows(sp, rows_in_fast, a["conv_b_2"][i].rearrange("(k p) -> k p", p=P), first + 3 * 2 * KF)
                load_rows(sp, rows_in_fast, a["sg_norm_g_2"].rearrange("l h d -> l (h d)").rearrange("l (k p) -> (l k) p", p=P),
                          ROWS["sg_norm"])
                for key, name in (("q_norm_g_2", "q_norm"), ("k_norm_g_2", "k_norm")):
                    load_twice(sp, rows_in_fast, a[key], ROWS[name])
                for key, name in (("ab_a_re", "a_re"), ("ab_a_im", "a_im")):
                    load_twice(sp, rows_in_fast, a[key][0], ROWS[name])

            def s5_parameters():
                b_re, b_im = (a[k][0].rearrange("g n p -> n g p") for k in ("ab_b_re", "ab_b_im"))
                c_re, c_im = (a[k][0].rearrange("g p n -> (g p) n").rearrange("(b q) n -> q b n", q=P)
                              for k in ("ab_c_re", "ab_c_im"))
                for v, (first, second) in enumerate(((b_re, b_im), (b_im, b_re))):
                    sp.dma_start(s5_b[0:STATE, v], first).then_inc(s5_in_sem, 16)
                    sp.dma_start(s5_b[STATE:P, v], second).then_inc(s5_in_sem, 16)
                for v, (first, second) in enumerate(((c_re, c_im), (c_im, c_re))):
                    sp.dma_start(s5_crow[:, v, :, 0:STATE], first).then_inc(s5_in_sem, 16)
                    sp.dma_start(s5_crow[:, v, :, STATE:P], second).then_inc(s5_in_sem, 16)
                sp.dma_start(s5_ldt[:], a["ab_log_dt"][0].partition_broadcast(P)).then_inc(s5_in_sem, 16)

            def ab():
                w = cols(a["ab_w_in"][0])
                for t in AB_ORDER:
                    if t == AB_ORDER[RING]:
                        s5_parameters()
                        first_rows()
                    load(w[:, :, t * P:(t + 1) * P])
                w = cols(a["ab_w_glu"][0])
                for t in range(4):
                    load(w[:, :, t * P:(t + 1) * P])
                plain(a["ab_w_out"][0], 8)

            def c():
                w = cols(a["c_w_in"][0])

                def turn(h):
                    for v in (0, 1, 3, 2):
                        load(w[:, :, bass.ds(h * P + v * D, P)])
                stream(C_HEADS, RING, turn)
                plain(a["c_w_out"][0], 8)

            def ffn(i):
                pairs(a["ffn_w1"][i], a["ffn_w3"][i], 0)
                deep(a["ffn_w2"][i])

            def gated(i):
                w = cols(a["w_in_2"][i])
                for t in IN_ORDER:
                    load(w[:, :, t * P:(t + 1) * P])
                plain(a["w_o_2"][i], 8)

            def conv_ffn(i):
                pairs(a["w_up_2"][i], a["w_up_2"][i], D_FF)
                deep(a["w_down_2"][i])

            for part in [ab, lambda: ffn(0), c, lambda: ffn(1), lambda: gated(0), lambda: conv_ffn(0),
                         lambda: gated(1), lambda: conv_ffn(1)]:
                part()
            out = a["out"][0].rearrange("(t p) d -> p t d", p=P)
            for t in range(TT):
                sp.wait_ge(out_ready, t + 1)
                sp.wait_ge(out_copied, t + 1)
                sp.dma_start(out[:, t], out_tok[:, t]).then_inc(out_stored, 16)
            sp.wait_ge(out_stored, 16 * TT)

        @block.gpsimd
        def _(pool):
            n = Count()

            load_rows(pool, gains_in, a["norm_g"].rearrange("l j (k p) -> (l j k) p", p=P), ROWS["norm"])
            def add_squares(sq):
                n(sq_ready, 1)
                for k in range(1, KD - 1):
                    pool.wait_ge(sq_ready, n(sq_ready))
                    if k > 1:
                        pool.wait_ge(pool_step, n(pool_step))
                    nc.gpsimd.tensor_tensor(sq_sum[:], sq[:, 0] if k == 1 else sq_sum[:], sq[:, k], ALU.add)\
                        .then_inc(pool_step if k < KD - 2 else sum_ready, 1)
                n(sq_ready, 1)

            add_squares(sq_ab)
            for key, name in (("attn_norm_g_2", "attn_norm"), ("ffn_norm_g_2", "ffn_norm"), ("ab_conv_b", "conv_b"),
                              ("ab_mh_gain", "mh_gain"), ("ab_skip", "skip"), ("ab_d", "s5_d"), ("ab_b_glu", "b_glu"),
                              ("c_lb_raw", "lb_raw"), ("c_g_gain", "c_gain"), ("attn_out_g_2", "attn_gain"),
                              ("sg_out_g_2", "sg_gain")):
                load_rows(pool, rows_in, a[key].rearrange("l (k p) -> (l k) p", p=P), ROWS[name])
            pool.dma_start(early[:], a["early"]).then_inc(early_in, 16)
            for v, key in enumerate(("ab_wq", "ab_wk", "ab_wv")):
                pool.dma_start(lstm_w4[:, v], a[key][0].rearrange("n d e -> (n d) e").rearrange("(t p) e -> p t e", p=P))\
                    .then_inc(lstm_in, 16)
            pool.dma_start(lstm_wif[:], a["ab_w_if"][0].rearrange("(k p) g -> p k g", p=P)).then_inc(lstm_in, 16)
            for v in range(2):
                pool.dma_start(lstm_bif[GATE_ROW * v:GATE_ROW * v + M_HEADS, v:v + 1],
                               a["ab_b_if"][0, M_HEADS * v:M_HEADS * v + M_HEADS].unsqueeze(1))\
                    .then_inc(lstm_in, 16)
            pool.wait_ge(us_ready, 1)
            pool.dma_start(us_dram.rearrange("(k p) i c -> p k i c", p=P), us[:]).then_inc(us_stored, 16)
            pool.wait_ge(us_stored, 16)
            by_step = us_dram.rearrange("(g p) i c -> i p g c", p=GW)
            for i in range(STEP):
                k = STEP - 1 - i
                pool.dma_start(u_step[GW * k:GW * k + GW], by_step[i]).then_inc(us_loaded, 16)
            pool.wait_ge(ys_ready, 1)
            by_step = ys_dram.rearrange("(g p) j c -> j p g c", p=GW)
            for j in range(STEP):
                pool.dma_start(by_step[j], ys_step[GW * j:GW * j + GW]).then_inc(ys_stored, 16)
            pool.dma_start(us[:], us_dram.rearrange("(k p) i c -> p k i c", p=P)).then_inc(us_back, 16)
            pool.wait_ge(ys_stored, 16 * STEP)
            pool.dma_start(ys[:], ys_dram.rearrange("(k p) j c -> p k (j c)", p=P)).then_inc(ys_loaded, 16)

            for norms in ((sq_mix,), (sq_in, sq_ffn), (sq_in, sq_mix), (sq_in, sq_ffn), (sq_in,)):
                for sq in norms:
                    add_squares(sq)
            for i in range(2):
                if i:
                    add_squares(sq_ffn)
                pool.wait_ge(x_ready, 8 * (5 + 2 * i))
                pool.dma_start(late[:], a["late"]).then_inc(late_in, 16)
                pool.dma_start(sgw[:], a["sg_w_2"][i].rearrange("h p q -> p h q")).then_inc(late_in, 16)
                for h in range(8):
                    pool.dma_start(sgb[HEAD * (h % 2):HEAD * (h % 2) + HEAD, h // 2],
                                   a["sg_b_2"][i, h].partition_broadcast(HEAD)).then_inc(late_in, 16)
                n(sq_ready, 8)
                add_squares(sq_in)

        @block.tensor
        def _(pe):
            n = Count()
            at = {"slab": 0, "bank": 0}

            def take(b):
                pe.wait_ge(bank_free[b], n(bank_free[b]))
                return bank[b]

            def product(hi, lo, slabs, tiles, last=None):
                for _ in range(tiles):
                    out = take(at["bank"] % RING)
                    kt = 0
                    for many in slabs:
                        s = at["slab"] % RING
                        pe.wait_ge(lo_done, n(lo_done))
                        for k in range(many):
                            if last and kt == sum(slabs) - 1:
                                pe.wait_ge(*last)
                            for w, v in ((w_hi, hi), (w_lo, hi), (w_hi, lo)):
                                mm = nc.tensor.matmul(out[:], w[:, s, k], v[:, kt],
                                                      start=(kt == 0 and w is w_hi and v is hi),
                                                      stop=(kt == sum(slabs) - 1 and v is lo))
                            kt += 1
                        mm.then_inc(slab_done, 1)
                        at["slab"] += 1
                    at["bank"] += 1

            def products(hi, lo, slabs, tiles, last=None):
                times = tiles // RING
                per = [(lo_done, RING * len(slabs))] + [(bank_free[b], 1) for b in range(RING)]
                if times == 1:
                    product(hi, lo, slabs, RING, last)
                    return
                with n.loop(pe, times, per):
                    product(hi, lo, slabs, RING, last)
                at["slab"] += (times - 1) * RING * len(slabs)
                at["bank"] += (times - 1) * RING

            def open_group(hi, lo):
                outs = [take((at["bank"] + t) % RING) for t in range(GROUP)]
                slots = [(at["slab"] + t) % RING for t in range(GROUP)]
                at["slab"] += GROUP
                at["bank"] += GROUP

                def part(k, first, last):
                    pe.wait_ge(h_ready, n(h_ready))
                    for out, s in zip(outs, slots):
                        if first:
                            pe.wait_ge(lo_done, n(lo_done))
                        for w, v in ((w_hi, hi), (w_lo, hi), (w_hi, lo)):
                            mm = nc.tensor.matmul(out[:], w[:, s, k], v[:, k], start=(first and w is w_hi and v is hi),
                                                  stop=(last and v is lo))
                        if last:
                            mm.then_inc(slab_done, 1)

                return part

            def group(hi, lo, order=range(KD), between=None, before=None):
                part = open_group(hi, lo)
                for j, k in enumerate(order):
                    if before and j == before[0]:
                        before[1]()
                    part(k, j == 0, j == KD - 1)
                    if between and (j % 2 and j < KD - 1 or j == KD - 2):
                        between()

            def from_h(tiles, scaled=True):
                if scaled:
                    group(h_hi, h_lo)
                else:
                    group(h_hi, h_lo, before=(KD - 1, lambda: add_up(sq_in, KD)))
                    spread_inverse()
                product(h_hi, h_lo, [KD], -(GROUP - tiles) % RING)
                if tiles - GROUP >= RING:
                    products(h_hi, h_lo, [KD], (tiles - GROUP) // RING * RING)

            def add_up(squares, tiles):
                out = take(4)
                if tiles == KD:
                    pe.wait_ge(sum_ready, n(sum_ready))
                    n(sq_ready, KD - 1)
                    terms = [sq_sum[:], squares[:, KD - 1]]
                else:
                    terms = [squares[:, k] for k in range(tiles)]
                pe.wait_ge(sq_ready, n(sq_ready, 1 if tiles == KD else tiles))
                for t in range(TT):
                    for k, term in enumerate(terms):
                        mm = nc.tensor.matmul(out[:, t:t + 1], term[:, t * P:(t + 1) * P], ones[:, 0:1], start=(k == 0),
                                              stop=(k == len(terms) - 1))
                mm.then_inc(stat_ready, 1)

            def spread_inverse():
                out = take(5)
                pe.wait_ge(inv_ready, n(inv_ready))
                for t in range(TT):
                    mm = nc.tensor.matmul(out[:, t * P:(t + 1) * P], inv[:, t:t + 1].to_broadcast([P, P]), ident,
                                          start=True, stop=True)
                mm.then_inc(scale_ready, 1)

            def sums(squares, tiles):
                add_up(squares, tiles)
                spread_inverse()

            pe.wait_ge(lead_in, 16)
            pe.wait_ge(x_in, 16)
            for k in range(KD):
                if k == KD // 2:
                    pe.wait_ge(x_in_rest, 16)
                out = take(k % RING)
                for t in range(TT):
                    mm = nc.tensor.transpose(out[:, t * P:(t + 1) * P], x_tok[:, t, k * P:(k + 1) * P], ident)
                mm.then_inc(x_turned, 1)
            pe.wait_ge(gains_in, 16 * row_dmas[gains_in])
            nc.tensor.transpose(take(7)[:, 0:GAINS], rows[0:GAINS, 0], ident[0:GAINS, 0:GAINS]).then_inc(gains_turned, 1)

            def turn_rows():
                for landed in (rows_in, rows_in_fast):
                    pe.wait_ge(landed, 16 * row_dmas[landed])
                for b in range(ROW_BLOCKS):
                    out = take(4 + b % 4)
                    r = block_rows(b)
                    nc.tensor.transpose(out[:, 0:r], rows[0:r, b], ident[0:r, 0:r]).then_inc(par_turned, 1)

            def project():
                group(h_hi, h_lo, before=(4, turn_rows))
                product(h_hi, h_lo, [KD], 1)
                pe.wait_ge(s5_in_sem, 16 * 9)
                for v in range(2):
                    out = take(6 + v)
                    for b in range(4):
                        mm = nc.tensor.transpose(out[:, b * P:(b + 1) * P], s5_crow[:, v, b], ident)
                    mm.then_inc(prep["pe_to_vector"], 1)
                product(h_hi, h_lo, [KD], 4)
                pe.wait_ge(prep["vector_to_pe"], n(prep["vector_to_pe"]))
                for i in range(GROUPS // 4):
                    out = take(4 + i % 4)
                    for g in range(4):
                        mm = nc.tensor.transpose(out[:, g * P:(g + 1) * P],
                                                 s5_q[:, 4 * i + g].rearrange("p k w -> p (k w)"), ident)
                    mm.then_inc(prep["pe_to_scalar"], 1)
                pe.wait_ge(prep["vector_to_pe"], n(prep["vector_to_pe"]))
                out = take(4)
                for g in range(GROUPS):
                    mm = nc.tensor.matmul(out[:, g * GW:(g + 1) * GW], s5_q[:, g].rearrange("p k w -> p (k w)"),
                                          s5_cx[:, g], start=True, stop=True)
                mm.then_inc(prep["pe_to_scalar"], 1)
                product(h_hi, h_lo, [KD], 2)
                pe.wait_ge(prep["scalar_to_pe"], n(prep["scalar_to_pe"]))
                for j in range(STEP):
                    out = take(5 + j % 3)
                    off = P - GW * (STEP - 1 - j)
                    nc.tensor.matmul(out[:], shifted[:, off:off + P], s5_k.rearrange("p g w -> p (g w)"),
                                     start=True, stop=True).then_inc(prep["pe_to_scalar"], 1)
                product(h_hi, h_lo, [KD], 2)

            def s5_core():
                def flat(t, i):
                    return t[:, 8 * i:8 * i + 8].rearrange("p g c -> p (g c)")

                def enter(i):
                    out = take(4 + i)
                    for g in range(8):
                        mm = nc.tensor.matmul(out[:, g * CH:(g + 1) * CH], s5_in[:, 8 * i + g], u_step[:, 8 * i + g],
                                              start=True, stop=True)
                    mm.then_inc(s5["pe_to_scalar"], 1)

                def swap_inputs(i):
                    out = take(i)
                    pe.wait_ge(s5["scalar_to_pe"], n(s5["scalar_to_pe"]))
                    nc.tensor.matmul(out[:], swap, flat(s5_state, i), start=True, stop=True).then_inc(s5["pe_to_vector"], 1)

                def swap_sums(i):
                    out = take(4 + i)
                    nc.tensor.matmul(out[:], swap, flat(s5_z, i), start=True, stop=True).then_inc(s5["pe_to_vector"], 1)

                def leave(i):
                    out = take(i)
                    pe.wait_ge(s5["vector_to_pe"], n(s5["vector_to_pe"]))
                    for g in range(8):
                        c = g * CH
                        nc.tensor.matmul(out[:, c:c + CH], s5_conv[:, 8 * i + g].rearrange("p j w -> p (j w)"),
                                         u_step[:, 8 * i + g], start=True, stop=False)
                        mm = nc.tensor.matmul(out[:, c + 1:c + CH], s5_out[:, 8 * i + g].rearrange("p j w -> p (j w)"),
                                              s5_state[:, 8 * i + g, 0:CH - 1], start=False, stop=True)
                    mm.then_inc(s5["pe_to_scalar"], 1)

                pe.wait_ge(us_loaded, 16 * STEP)
                enter(0)
                enter(1)
                swap_inputs(0)
                enter(2)
                swap_inputs(1)
                enter(3)
                swap_inputs(2)
                swap_inputs(3)
                pe.wait_ge(s5["vector_to_pe"], n(s5["vector_to_pe"], 4))
                for i in range(4):
                    swap_sums(i)
                for i in range(4):
                    leave(i)

            def lstm_front():
                pe.wait_ge(lstm["vector_to_pe"], n(lstm["vector_to_pe"]))
                for k in range(4):
                    pe.wait_ge(lstm["scalar_to_pe"], n(lstm["scalar_to_pe"]))
                    for v, src in ((0, xc), (1, xc), (2, xm)):
                        out = take(4 + v)
                        nc.tensor.matmul(out[:], lstm_bd[:, v, k], src[:, k], start=True, stop=True)\
                            .then_inc(lstm["pe_to_scalar"], 1)
                    out = take(7)
                    for t in range(TT):
                        mm = nc.tensor.matmul(out[:, t * P:(t + 1) * P], xm[:, k, t * P:(t + 1) * P], lstm_bd[:, 3, k],
                                              start=True, stop=True)
                    mm.then_inc(lstm["pe_to_scalar"], 1)
                pe.wait_ge(lstm["scalar_to_pe"], n(lstm["scalar_to_pe"]))
                out = take(4)
                for j in range(12):
                    mm = nc.tensor.matmul(out[0:GATE_COLS, :], gate_w[:, j], (qm, km, vf)[j // 4][:, j % 4],
                                          start=(j == 0), stop=(j == 11))
                mm.then_inc(lstm["pe_to_scalar"], 1)

            def lstm_heads():
                pe.wait_ge(lstm["vector_to_pe"], n(lstm["vector_to_pe"]))
                out = take(6)
                for t in range(TT):
                    mm = nc.tensor.transpose(out[:, 4 * t:4 * t + 4], rowv[:, 7, t * P:(t + 1) * P], ident[0:4, 0:4])
                mm.then_inc(lstm["pe_to_vector"], 1)
                pe.wait_ge(lstm["scalar_to_pe"], n(lstm["scalar_to_pe"]))
                out = take(7)
                for t in range(TT):
                    mm = nc.tensor.transpose(out[:, 4 * t:4 * t + 4], rowv[:, 5, t * P:(t + 1) * P], ident[0:4, 0:4])
                mm.then_inc(lstm["pe_to_vector"], 1)

                def scores(h):
                    out = take(4)
                    nc.tensor.matmul(out[:], pick[:, h], rowv[:, 3], start=True, stop=True).then_inc(top_out, 1)
                    for t in range(TT):
                        out = take(6 + t % 2)
                        nc.tensor.matmul(out[:, 0:SEQ - t * P], km[:, h, t * P:(t + 1) * P], qm[:, h, t * P:SEQ],
                                         start=True, stop=True).then_inc(scored, 1)

                def sums_over(h):
                    num, den = take(3), take(5)
                    for t in range(TT):
                        pe.wait_ge(weighed, n(weighed))
                        mm = nc.tensor.matmul(num[:, t * P:SEQ], vt[:, h, t], sc_m[:, t, t * P:SEQ], start=(t == 0), stop=(t == 3))
                    mm.then_inc(lstm["pe_to_scalar"], 1)
                    for t in range(TT):
                        for s in range(t + 1):
                            mm = nc.tensor.matmul(den[:, t:t + 1], sc_m[:, s, t * P:(t + 1) * P], ones[:, 0:1],
                                                  start=(s == 0), stop=(s == t))
                    mm.then_inc(lstm["pe_to_vector"], 1)

                part = open_group(h_hi, h_lo)
                scores(0)
                part(4, True, False)
                part(5, False, False)
                sums_over(0)
                for h in range(M_HEADS):
                    if h + 1 < M_HEADS:
                        scores(h + 1)
                    out = take(4)
                    pe.wait_ge(lstm["scalar_to_pe"], n(lstm["scalar_to_pe"]))
                    for t in range(TT):
                        mm = nc.tensor.matmul(out[:, t:t + 1], num_sq[:, t * P:(t + 1) * P], ones[:, 0:1],
                                              start=True, stop=True)
                    mm.then_inc(lstm["pe_to_vector"], 1)
                    if h + 1 < M_HEADS:
                        sums_over(h + 1)
                    part((6, 7, 0, 1)[h], False, False)
                    out = take(5)
                    pe.wait_ge(head_scaled, n(head_scaled))
                    for t in range(TT):
                        mm = nc.tensor.matmul(out[:, t * P:(t + 1) * P], scale_col[:, t:t + 1].to_broadcast([P, P]), ident,
                                              start=True, stop=True)
                    mm.then_inc(lstm["pe_to_vector"], 1)
                part(2, False, False)
                part(3, False, True)

            def ab():
                sums(sq_ab, KD)
                project()
                s5_core()
                lstm_front()
                pe.wait_ge(h_ready, n(h_ready, 4))
                product(h_hi, h_lo, [4], 4)
                lstm_heads()
                product(h_hi, h_lo, [KD], 1)
                products(h_hi, h_lo, [KD], 4)
                sums(sq_mix, KD)

            def down():
                pe.wait_ge(hid_ready, n(hid_ready, KF - 1))
                products(hid_hi, hid_lo, DOWN, 8, (hid_ready, n(hid_ready)))

            def ffn(i):
                from_h(2 * KF, scaled=False)
                down()
                sums(sq_ffn, KD)

            def c():
                def weigh():
                    out = take(4)
                    pe.wait_ge(hgrn["scalar_to_pe"], n(hgrn["scalar_to_pe"]))
                    for t in range(TT):
                        mm = nc.tensor.transpose(out[:, t * P:(t + 1) * P], c_i[:, t * P:(t + 1) * P], ident)
                    mm.then_inc(hgrn["pe_to_scalar"], 1)
                    out = take(7)
                    pe.wait_ge(hgrn["vector_to_pe"], n(hgrn["vector_to_pe"]))
                    for t in range(TT):
                        mm = nc.tensor.transpose(out[:, t * P:(t + 1) * P], c_k[:, t * P:(t + 1) * P], ident)
                    mm.then_inc(hgrn["pe_to_scalar"], 1)
                    out = take(6)
                    for t in range(TT):
                        mm = nc.tensor.matmul(out[:, t * P:(t + 1) * P], c_k[:, t * P:(t + 1) * P], c_d[:, t * P:(t + 1) * P],
                                              start=True, stop=True)
                    mm.then_inc(hgrn["pe_to_vector"], 1)

                def update():
                    u = take(7), take(4)
                    pe.wait_ge(hgrn["scalar_to_pe"], n(hgrn["scalar_to_pe"]))
                    for j in range(7):
                        r = C_CHUNK * (j % 2)
                        mm = nc.tensor.matmul(u[j % 2][:, (j // 2) * P:(j // 2 + 1) * P], c_kt[r:r + C_CHUNK, j // 2],
                                              c_it[r:r + C_CHUNK, j // 2], start=True, stop=True)
                    mm.then_inc(hgrn["pe_to_vector"], 1)

                def read():
                    out = take(5)
                    pe.wait_ge(hgrn["vector_to_pe"], n(hgrn["vector_to_pe"], 2))
                    for t in range(TT):
                        nc.tensor.matmul(out[:, t * P:(t + 1) * P], c_it[:, t], c_s[:, t], start=True, stop=False)
                        for j in (2 * t, 2 * t + 1):
                            if j:
                                mm = nc.tensor.matmul(out[:, j * C_CHUNK:(j + 1) * C_CHUNK], c_state[:, j],
                                                      c_e[:, j * C_CHUNK:(j + 1) * C_CHUNK], start=False, stop=(j % 2 == 1))
                    mm.then_inc(hgrn["pe_to_scalar"], 1)

                def square():
                    out = take(6)
                    pe.wait_ge(hgrn["scalar_to_pe"], n(hgrn["scalar_to_pe"]))
                    nc.tensor.matmul(out[:], ones, c_o[:], start=True, stop=True).then_inc(hgrn["pe_to_scalar"], 1)

                sums(sq_in, KD)
                group(h_hi, h_lo)
                product(h_hi, h_lo, [KD], 1)
                per = [(hgrn["scalar_to_pe"], 3), (hgrn["vector_to_pe"], 3), (lo_done, 4)] + [
                    (bank_free[b], 2 if b in (4, 6, 7) else 1) for b in range(8)]
                with n.loop(pe, C_HEADS - 1, per):
                    for step in (weigh, update, read, square):
                        product(h_hi, h_lo, [KD], 1)
                        step()
                at["slab"] += RING * (C_HEADS - 2)
                at["bank"] += RING * (C_HEADS - 2)
                steps = iter((weigh, update, read, square))
                group(mix_hi, mix_lo, between=lambda: next(steps)())
                product(mix_hi, mix_lo, [KD], 1)
                products(mix_hi, mix_lo, [KD], 4)
                sums(sq_mix, KD)

            def gated(i):
                sums(sq_ffn if i else sq_in, KD)
                group(h_hi, h_lo)
                product(h_hi, h_lo, [KD], 4)
                out = take(4)
                pe.wait_ge(qk_squared, n(qk_squared, 5))
                pe.wait_ge(late_in, n(late_in, 16 * 10))
                for t in range(TT):
                    for j in range(5):
                        c = 2 * (5 * t + j)
                        mm = nc.tensor.matmul(out[:, c:c + 2], qk_sq[:, j, t * P:(t + 1) * P], halves[:, 0:P:HEAD],
                                              start=True, stop=True)
                mm.then_inc(qk_summed, 1)

                def partners(tiles):
                    for j, b in tiles:
                        nc.tensor.matmul(take(b)[:], turn, qa[:, j], start=True, stop=True).then_inc(qk_partner, 1)

                pe.wait_ge(qk_in, n(qk_in))
                partners(PARTNERS[:3])
                product(h_hi, h_lo, [KD], 1)
                out = take(4)
                pe.wait_ge(qk_inverted, n(qk_inverted))
                for t in range(TT):
                    for hh in range(2):
                        c = 2 * (5 * t + 4) + hh
                        mm = nc.tensor.matmul(out[HEAD * hh:HEAD * hh + HEAD, t * P:(t + 1) * P],
                                              head_dev[:, c:c + 1].to_broadcast([P, HEAD]), ident, start=True, stop=True)
                mm.then_inc(qk_spread, 1)
                partners(PARTNERS[3:])
                product(h_hi, h_lo, [KD], 1)
                out = take(4)
                pe.wait_ge(k_turned, n(k_turned))
                nc.tensor.matmul(out[:], swap, qa[:, 4], start=True, stop=True).then_inc(k_swapped, 1)
                out = take(5)
                pe.wait_ge(v_in, n(v_in))
                for t in range(TT):
                    mm = nc.tensor.transpose(out[:, t * P:(t + 1) * P], va[:, t * P:(t + 1) * P], ident)
                mm.then_inc(v_turned, 1)
                for v in range(2):
                    out = take(6 + v)
                    for h in range(4):
                        mm = nc.tensor.transpose(out[:, h * P:(h + 1) * P], sgw[:, 4 * v + h], ident)
                    mm.then_inc(sgw_turned, 1)
                product(h_hi, h_lo, [KD], 2)
                pe.wait_ge(vv_in, n(vv_in))
                for t in range(TT):
                    out = take(4 + t)
                    for f in range(4):
                        mm = nc.tensor.transpose(out[:, f * P:(f + 1) * P], vva[:, f, t * P:(t + 1) * P], ident)
                    mm.then_inc(vv_turned, 1)
                product(h_hi, h_lo, [KD], 3)

                def scores(u):
                    h, t = u // TT, u % TT
                    out = take(2 + u % 3)
                    nc.tensor.matmul(out[:], qa[:, h // 2, t * P:(t + 1) * P], k_pad[:, 2 * (h // 4) + h % 2],
                                     start=True, stop=True).then_inc(score_ready, 1)

                def mix(j):
                    out = take(5)
                    if j == 0:
                        pe.wait_ge(vv_normal, n(vv_normal))
                        pe.wait_ge(sgw_copied, n(sgw_copied))
                    for t in range(TT):
                        for hh in range(2):
                            mm = nc.tensor.matmul(out[HEAD * hh:HEAD * hh + HEAD, t * P:(t + 1) * P],
                                                  vv_tok[:, t, (2 * j + hh) * HEAD:(2 * j + hh + 1) * HEAD],
                                                  sgw_t[:, 2 * j + hh], start=True, stop=True)
                    mm.then_inc(gate_mixed, 1)

                def values(j, t, keys):
                    out = take(j % 2) if (t, keys[0]) == (0, 0) else bank[j % 2]
                    if keys[0] == 0:
                        pe.wait_ge(prob_copied, n(prob_copied, 1 if t else TT + 1))
                    q = slice(t * P, (t + 1) * P)
                    for s in keys:
                        for h in (2 * j, 2 * j + 1):
                            r = HEAD * (h % 2)
                            mm = nc.tensor.matmul(out[r:r + HEAD, q], v_tok[:, s, HEAD * (h // 4):HEAD * (h // 4) + HEAD],
                                                  prob_t[h % 4][:, s, q], start=(s == 0), stop=(s == TT - 1))
                    if (t, s) == (TT - 1, TT - 1):
                        mm.then_inc(head_done, 1)

                pe.wait_ge(q_turned, n(q_turned))
                pe.wait_ge(v_copied, n(v_copied))
                scores(0)
                scores(1)
                for u in range(UNITS):
                    if u + 2 < UNITS:
                        scores(u + 2)
                    out = take(6 + u % 2)
                    pe.wait_ge(prob_ready, n(prob_ready))
                    for s in range(TT):
                        mm = nc.tensor.transpose(out[:, s * P:(s + 1) * P], prob[:, u % 4, s * P:(s + 1) * P], ident)
                    mm.then_inc(prob_turned, 1)
                    j, piece = (u - TT - 1) // (2 * TT), (u - TT - 1) % (2 * TT)
                    if j == 3:
                        values(3, piece, range(TT))
                    elif j >= 0:
                        values(j, piece // 2, range(TT // 2 * (piece % 2), TT // 2 * (piece % 2 + 1)))
                    if u in MIX_AT:
                        mix(MIX_AT.index(u))
                values(3, TT - 1, range(TT))
                sums(ua_sq, 4)
                sums(oa_sq, 4)
                group(h_hi, h_lo, (4, 5, 6, 7, 0, 1, 2, 3))
                product(h_hi, h_lo, [KD], 1)
                products(h_hi, h_lo, [KD], 4)

            def conv_ffn(i):
                sums(sq_in, KD)
                from_h(2 * KF)
                down()

            for part in [ab, lambda: ffn(0), c, lambda: ffn(1), lambda: gated(0), lambda: conv_ffn(0),
                         lambda: gated(1), lambda: conv_ffn(1)]:
                part()
            pe.wait_ge(x_ready, KD * (1 + len(parts)))
            for t in range(TT):
                for v in range(2):
                    out = take(4 + (2 * t + v) % 4)
                    for k in range(4):
                        mm = nc.tensor.transpose(out[:, k * P:(k + 1) * P], x[:, 4 * v + k, t * P:(t + 1) * P], ident)
                    mm.then_inc(out_turned, 1)

        @block.scalar
        def _(act):
            n = Count()
            at = {"split": 0, "bank": 0}

            def split():
                if at["split"] < N_SLABS:
                    s = at["split"] % RING
                    act.wait_ge(raw_full[s], n(raw_full[s], 16))
                    nc.scalar.activation(w_hi[:, s], w_raw[:, s], ACT.Copy).then_inc(hi_done, 1)
                    at["split"] += 1

            def slab():
                act.wait_ge(slab_done, n(slab_done))
                split()

            def turns(times, slabs, body, extra=()):
                dry = at["split"] + times * slabs > N_SLABS
                k = times - dry
                if k > 1:
                    per = [(slab_done, slabs)] + [(raw_full[s], 16 * slabs // RING) for s in range(RING)] + list(extra)
                    with n.loop(act, k, per) as i:
                        body(i)
                    at["split"] += (k - 1) * slabs
                elif k:
                    body(0)
                if dry:
                    body(times - 1)

            def turned_bank():
                at["bank"] += 1
                return (at["bank"] - 1) % RING

            def squares(src, dst, wait=None):
                for k in range(src.shape[1]):
                    if wait is not None:
                        act.wait_ge(wait, n(wait))
                    nc.scalar.activation(dst[:, k], src[:, k], ACT.Square).then_inc(sq_ready, 1)

            def load_root():
                return nc.scalar.activation(warm[:], eps[:], ACT.Sqrt)

            def deviation(width):
                act.wait_ge(stat_ready, n(stat_ready))
                nc.scalar.activation(dev[:], bank[4][:, 0:TT], ACT.Sqrt, bias=eps[:, 0:1], scale=1.0 / width)\
                    .then_inc(std_ready, 1)

            def leave(y, sq, slabs):
                first = at["bank"]
                load_root()

                def body(i):
                    for t in range(RING):
                        for _ in range(slabs):
                            slab()
                        b = (first + t) % RING
                        k = bass.ds(i * RING + t, 1)
                        nc.scalar.activation(sq[:, k], bank[b][:].unsqueeze(1), ACT.Square).then_inc(sq_ready, 1)
                        nc.scalar.activation(y[:, k], bank[b][:].unsqueeze(1), ACT.Copy).then_inc(bank_free[b], 1)
                turns(2, RING * slabs, body)
                at["bank"] += KD
                deviation(D)

            def project():
                v = [s5_v[:, i] for i in range(16)]
                act.wait_ge(s5_in_sem, 16 * 9)
                nc.scalar.activation(v[0], s5_ldt, ACT.Exp).then_inc(prep["scalar_to_vector"], 1)
                act.wait_ge(prep["vector_to_scalar"], n(prep["vector_to_scalar"]))
                nc.scalar.activation(v[7], v[1], ACT.Exp)
                nc.scalar.activation(s5_r8[:], v[1], ACT.Exp, scale=float(STEP))
                nc.scalar.activation(v[8], v[4], ACT.Sin)
                nc.scalar.activation(v[9], v[5], ACT.Sin).then_inc(prep["scalar_to_vector"], 1)
                for t in range(4):
                    slab()
                    b = turned_bank()
                    nc.scalar.activation(xm[:, t], bank[b][:], ACT.Copy).then_inc(bank_free[b], 1)
                for t in range(4):
                    slab()
                for i in range(GROUPS // 4):
                    act.wait_ge(prep["pe_to_scalar"], n(prep["pe_to_scalar"]))
                    nc.scalar.activation(s5_in[:, 4 * i:4 * i + 4], bank[4 + i % 4][:].rearrange("p (g w) -> p g w", g=4),
                                         ACT.Copy).then_inc(bank_free[4 + i % 4], 1)
                act.wait_ge(prep["pe_to_scalar"], n(prep["pe_to_scalar"]))
                nc.scalar.activation(s5_k, bank[4][:].rearrange("p (g w) -> p g w", g=GROUPS), ACT.Copy)\
                    .then_inc(prep["scalar_to_pe"], 1)
                act.drain().then_inc(bank_free[4], 1)
                act.drain().then_inc(prep["scalar_to_vector"], 1)
                act.wait_ge(prep["vector_to_scalar"], n(prep["vector_to_scalar"]))
                for t in range(4):
                    b = turned_bank()
                    nc.scalar.activation(us[:, t], bank[b][:].rearrange("p (c i) -> p i c", i=STEP), ACT.Copy)\
                        .then_inc(bank_free[b], 1)
                act.drain().then_inc(us_ready, 1)

                def gate_in(t):
                    slab()
                    b = turned_bank()
                    nc.scalar.activation(zs[:, t], bank[b][:], ACT.Silu).then_inc(bank_free[b], 1)

                for t in (0, 1):
                    gate_in(t)
                for j in range(STEP):
                    act.wait_ge(prep["pe_to_scalar"], n(prep["pe_to_scalar"]))
                    nc.scalar.activation(s5_conv[:, :, j], bank[5 + j % 3][:].rearrange("p (g w) -> p g w", g=GROUPS),
                                         ACT.Copy).then_inc(bank_free[5 + j % 3], 1)
                for t in (2, 3):
                    gate_in(t)
                act.wait_ge(hgrn["vector_to_scalar"], n(hgrn["vector_to_scalar"]))
                nc.scalar.activation(small[:, 0:16], small[:, 0:16], ACT.Exp).then_inc(hgrn["scalar_to_vector"], 1)

            def convolved():
                for k in range(4):
                    act.wait_ge(lstm["vector_to_scalar"], n(lstm["vector_to_scalar"]))
                    nc.scalar.activation(xc[:, k], xc[:, k], ACT.Silu).then_inc(lstm["scalar_to_pe"], 1)

            def s5_core():
                for i in range(4):
                    act.wait_ge(s5["pe_to_scalar"], n(s5["pe_to_scalar"]))
                    nc.scalar.activation(s5_state[:, 8 * i:8 * i + 8], bank[4 + i][:].rearrange("p (g c) -> p g c", g=8),
                                         ACT.Copy).then_inc(s5["scalar_to_pe"], 1)
                for i in range(4):
                    act.wait_ge(s5["pe_to_scalar"], n(s5["pe_to_scalar"]))
                    nc.scalar.activation(ys_step[:, 8 * i:8 * i + 8], bank[i][:].rearrange("p (g c) -> p g c", g=8),
                                         ACT.Copy).then_inc(bank_free[i], 1)
                act.drain().then_inc(ys_ready, 1)

            def s5_gelu():
                act.wait_ge(s5["vector_to_scalar"], n(s5["vector_to_scalar"]))
                nc.scalar.activation(ys[:], ys[:], ACT.Gelu_apprx_tanh).then_inc(s5["scalar_to_vector"], 1)

            def s5_glu():
                for t in range(4):
                    slab()
                    nc.scalar.activation(gate[:, t], bank[turned_bank()][:], ACT.Sigmoid, bias=col("b_glu", t))\
                        .then_inc(s5["scalar_to_vector"], 1)

            def lstm_projections():
                for k in range(4):
                    for v, (dst, scale) in enumerate(((qm, 1.0), (km, float(P) ** -0.5), (vf, 1.0), (vt, 1.0))):
                        act.wait_ge(lstm["pe_to_scalar"], n(lstm["pe_to_scalar"]))
                        to = dst[:, k] if v < 3 else dst[:, k].rearrange("p t w -> p (t w)")
                        nc.scalar.activation(to, bank[4 + v][:], ACT.Copy, scale=scale).then_inc(bank_free[4 + v], 1)
                act.drain().then_inc(lstm["scalar_to_pe"], 1)

            def lstm_gates():
                act.wait_ge(lstm["pe_to_scalar"], n(lstm["pe_to_scalar"]))
                rows_i, rows_f = slice(0, M_HEADS), slice(GATE_ROW, GATE_COLS)
                r = [rowv[:, j] for j in range(8)]
                nc.scalar.activation(r[2], bank[4][rows_f, :], ACT.Abs, bias=lstm_bif[rows_f, 1:2]).then_inc(scalar_step, 1)
                nc.scalar.activation(r[1], bank[4][rows_f, :], ACT.Identity, bias=lstm_bif[rows_f, 1:2])
                nc.scalar.activation(r[0], bank[4][rows_i, :], ACT.Identity, bias=lstm_bif[rows_i, 0:1]).then_inc(bank_free[4], 1)
                act.wait_ge(scalar_step, n(scalar_step))
                nc.scalar.activation(r[3], r[2], ACT.Exp, scale=-1.0).then_inc(scalar_step, 1)
                act.wait_ge(scalar_step, n(scalar_step))
                nc.scalar.activation(r[4], r[3], ACT.Ln, bias=1.0).then_inc(lstm["scalar_to_vector"], 1)

            def lstm_heads():
                act.wait_ge(lstm["vector_to_scalar"], n(lstm["vector_to_scalar"]))
                nc.scalar.activation(rowv[:, 5], rowv[:, 4], ACT.Exp, scale=-1.0).then_inc(lstm["scalar_to_pe"], 1)

                def weights(h):
                    act.wait_ge(top_out, n(top_out))
                    nc.scalar.activation(neg_top[:], bank[4][:], ACT.Copy).then_inc(top_in, 1)
                    for t in range(TT):
                        act.wait_ge(expo_ready, n(expo_ready))
                        nc.scalar.activation(lstm_t[:, t, t * P:SEQ], lstm_t[:, t, t * P:SEQ], ACT.Exp).then_inc(weight_ready, 1)

                weights(0)
                for h in range(M_HEADS):
                    act.wait_ge(lstm["pe_to_scalar"], n(lstm["pe_to_scalar"]))
                    nc.scalar.activation(num_sq[:], bank[3][:], ACT.Square).then_inc(lstm["scalar_to_pe"], 1)
                    nc.scalar.activation(lstm_v[:, h % 2], bank[3][:], ACT.Copy, scale=col("mh_gain", h)).then_inc(bank_free[3], 1)
                    if h + 1 < M_HEADS:
                        weights(h + 1)
                    load_root().then_inc(scalar_step, 1)
                    act.wait_ge(scalar_step, n(scalar_step))
                    act.wait_ge(lstm["vector_to_scalar"], n(lstm["vector_to_scalar"]))
                    nc.scalar.activation(dev_col, var_col, ACT.Sqrt, bias=eps[:, 0:1]).then_inc(lstm["scalar_to_vector"], 1)

            def ab():
                deviation(D)
                high_of_scaled()
                project()
                act.wait_ge(par_ready, 1)
                act.wait_ge(lstm_in, 16 * 6)
                s5_core()
                convolved()
                lstm_projections()
                s5_gelu()
                lstm_gates()
                s5_glu()
                lstm_heads()
                leave(y_mix, sq_mix, 1)

            def high_of_scaled():
                for k in range(KD):
                    act.wait_ge(h_scaled, n(h_scaled))
                    nc.scalar.activation(h_hi[:, k], tmp[:, k % 4], ACT.Copy).then_inc(h_high, 1)

            def ffn(i):
                for k in range(KD):
                    act.wait_ge(x_ready, n(x_ready))
                    nc.scalar.activation(h_hi[:, k], x[:, k], ACT.Copy, scale=col("norm", 32 * i + 16 + k)).then_inc(h_high, 1)
                    nc.scalar.activation(sq_in[:, k], x[:, k], ACT.Square).then_inc(sq_ready, 1)
                deviation(D)

                def body(i):
                    for p in range(2):
                        slab()
                        act.wait_ge(dve_for_act, n(dve_for_act))
                        nc.scalar.activation(tmp[:, p], tmp[:, p], ACT.Silu).then_inc(act_for_dve, 1)
                        slab()
                turns(KF // 2, RING, body, [(dve_for_act, 2)])
                at["bank"] += 2 * KF
                leave(y_ffn, sq_ffn, 3)

            def c():
                squares(x, sq_in, x_ready)
                deviation(D)
                high_of_scaled()
                first = at["bank"]
                bank_of = [bank[(first + t) % RING] for t in range(RING)]
                free = [bank_free[(first + t) % RING] for t in range(RING)]

                def sigmoid(t):
                    slab()
                    nc.scalar.activation(c_sig[:, t], bank_of[t][:], ACT.Sigmoid).then_inc(hgrn["scalar_to_vector"], 1)

                def turn(gemm, mixer):
                    if gemm:
                        sigmoid(0)
                    if mixer:
                        act.wait_ge(hgrn["pe_to_scalar"], n(hgrn["pe_to_scalar"]))
                        nc.scalar.activation(c_it[:].rearrange("p t w -> p (t w)"), bank[4][:], ACT.Copy).then_inc(bank_free[4], 1)
                        act.wait_ge(hgrn["pe_to_scalar"], n(hgrn["pe_to_scalar"]))
                        nc.scalar.activation(c_kt[:].rearrange("p t w -> p (t w)"), bank[7][:], ACT.Copy).then_inc(bank_free[7], 1)
                        act.drain().then_inc(hgrn["scalar_to_pe"], 1)
                    if gemm:
                        sigmoid(1)
                        sigmoid(2)
                    if mixer:
                        act.wait_ge(hgrn["pe_to_scalar"], n(hgrn["pe_to_scalar"]))
                        nc.scalar.activation(c_o[:], bank[5][:], ACT.Square).then_inc(hgrn["scalar_to_pe"], 1)
                    if gemm:
                        act.wait_ge(hgrn["vector_to_scalar"], n(hgrn["vector_to_scalar"]))
                        nc.scalar.activation(c_f[:], c_f[:], ACT.Ln).then_inc(hgrn["scalar_to_vector"], 1)
                        act.wait_ge(hgrn["vector_to_scalar"], n(hgrn["vector_to_scalar"]))
                        nc.scalar.activation(c_e[:], c_b[:], ACT.Exp)
                        nc.scalar.activation(tmp[:, 0], c_d[:], ACT.Exp)
                        nc.scalar.activation(tmp[:, 1], c_d[:], ACT.Exp, scale=-1.0).then_inc(hgrn["scalar_to_vector"], 1)
                        slab()
                        nc.scalar.activation(c_i[:], bank_of[3][:], ACT.Copy).then_inc(free[3], 1)
                        act.drain().then_inc(hgrn["scalar_to_pe"], 1)
                    if mixer:
                        act.wait_ge(hgrn["pe_to_scalar"], n(hgrn["pe_to_scalar"]))
                        nc.scalar.activation(tmp[:, 2], bank[6][:], ACT.Ln, bias=eps[:, 0:1], scale=1.0 / P).then_inc(scalar_step, 1)
                        act.wait_ge(scalar_step, n(scalar_step))
                        nc.scalar.activation(tmp[:, 2], tmp[:, 2], ACT.Exp, scale=-0.5).then_inc(hgrn["scalar_to_vector"], 1)

                turn(True, False)
                per = [(slab_done, RING), (scalar_step, 1), (hgrn["vector_to_scalar"], 2), (hgrn["pe_to_scalar"], 4)] + [
                    (raw_full[s], 16) for s in range(RING)]
                with n.loop(act, C_HEADS - 1, per):
                    turn(True, True)
                at["split"] += RING * (C_HEADS - 2)
                turn(False, True)
                at["bank"] += RING * C_HEADS
                leave(y_mix, sq_mix, 1)

            def gated(i):
                if i == 0:
                    squares(x, sq_in, x_ready)
                deviation(D)
                high_of_scaled()
                for t in IN_ORDER:
                    if t == IN_ORDER[6]:
                        act.wait_ge(qk_summed, n(qk_summed))
                        nc.scalar.activation(head_dev, bank[4][:, 0:40], ACT.Sqrt, bias=eps[:, 0:1], scale=1.0 / HEAD)\
                            .then_inc(qk_rooted, 1)
                    slab()
                    b = turned_bank()
                    if t < 5:
                        nc.scalar.activation(qk_sq[:, t], bank[b][:], ACT.Square).then_inc(qk_squared, 1)
                        nc.scalar.activation(qa[:, t], bank[b][:], ACT.Copy, scale=col("q_norm" if t < 4 else "k_norm", i))\
                            .then_inc(bank_free[b], 1)
                        if t == 3:
                            act.drain().then_inc(qk_in, 1)
                    elif t == 5:
                        nc.scalar.activation(va[:], bank[b][:], ACT.Copy).then_inc(bank_free[b], 1)
                        act.drain().then_inc(v_in, 1)
                    else:
                        dst = ua[:, t - 6] if t < 10 else vva[:, t - 10]
                        nc.scalar.activation(dst, bank[b][:], ACT.Gelu_apprx_tanh).then_inc(bank_free[b], 1)
                    if t == 13:
                        act.drain().then_inc(vv_in, 1)
                        act.wait_ge(v_turned, n(v_turned))
                        nc.scalar.activation(v_tok[:].rearrange("p t w -> p (t w)"), bank[5][:], ACT.Copy).then_inc(bank_free[5], 1)
                        act.drain().then_inc(v_copied, 1)
                        for v in range(2):
                            act.wait_ge(sgw_turned, n(sgw_turned))
                            nc.scalar.activation(sgw_t[:, 4 * v:4 * v + 4].rearrange("p h w -> p (h w)"), bank[6 + v][:],
                                                 ACT.Copy).then_inc(bank_free[6 + v], 1)
                        act.drain().then_inc(sgw_copied, 1)
                    if t == 6:
                        for v in range(TT):
                            act.wait_ge(vv_turned, n(vv_turned))
                            nc.scalar.activation(prob_t[0][:, v], bank[4 + v][:], ACT.Square)
                            nc.scalar.activation(vv_tok[:, v], bank[4 + v][:], ACT.Copy).then_inc(bank_free[4 + v], 1)
                        act.drain().then_inc(vv_copied, 1)
                    if t == 8:
                        act.wait_ge(vv_summed, n(vv_summed))
                        nc.scalar.activation(gate_dev, gate_dev, ACT.Sqrt, bias=eps[:, 0:1], scale=1.0 / HEAD).then_inc(vv_rooted, 1)
                def exps(u):
                    c = 2 * (5 * (u % TT) + u // TT // 2) + u // TT % 2
                    act.wait_ge(max_ready, n(max_ready))
                    nc.scalar.activation(prob[:, u % 4], bank[2 + u % 3][:], ACT.Exp, bias=shift[:, u % 4:u % 4 + 1],
                                         scale=head_scale[:, c:c + 1], accum_out=total[:, u % 4:u % 4 + 1]).then_inc(exp_ready, 1)

                def head_out(j):
                    act.wait_ge(head_done, n(head_done))
                    nc.scalar.activation(oa_sq[:, j], bank[j % 2][:], ACT.Square).then_inc(sq_ready, 1)
                    nc.scalar.activation(oa[:, j], bank[j % 2][:], ACT.Copy).then_inc(bank_free[j % 2], 1)

                exps(0)
                for u in range(UNITS):
                    if u + 1 < UNITS:
                        exps(u + 1)
                    h, t = u // TT, u % TT
                    act.wait_ge(prob_turned, n(prob_turned))
                    nc.scalar.activation(prob_t[h % 4][:, :, t * P:(t + 1) * P], bank[6 + u % 2][:].rearrange("p (s w) -> p s w", s=TT),
                                         ACT.Copy).then_inc(bank_free[6 + u % 2], 1)
                    act.drain().then_inc(prob_copied, 1)
                    if u % (2 * TT) == TT + 1 and u > 2 * TT:
                        head_out(u // (2 * TT) - 1)
                    j = u - MIX_AT[-1] - 4
                    if 0 <= j < 4:
                        if j == 0:
                            act.wait_ge(gated_ready, n(gated_ready, 4))
                        nc.scalar.activation(ua_sq[:, j], ua[:, j], ACT.Square).then_inc(sq_ready, 1)
                deviation(4 * P)
                head_out(3)
                deviation(4 * P)
                stay(1, sq_in)

            def stay(slabs, sq):
                load_root()

                def body(i):
                    for t in range(RING):
                        for _ in range(slabs - 1):
                            slab()
                        act.wait_ge(slab_done, n(slab_done))
                        if sq is not None:
                            act.wait_ge(x_ready, n(x_ready))
                        split()
                        if sq is not None:
                            k = bass.ds(i * RING + t, 1)
                            nc.scalar.activation(sq[:, k], x[:, k], ACT.Square).then_inc(sq_ready, 1)
                turns(2, RING * slabs, body, [(x_ready, RING)] if sq is not None else [])
                at["bank"] += KD

            def conv_ffn(i):
                deviation(D)
                high_of_scaled()
                first = at["bank"]
                base = i * 8 * KF

                def body(j):
                    for p in range(2):
                        for v in range(2):
                            slab()
                            k = j * 2 + (p + v * KF + base)
                            nc.scalar.activation(tmp[:, 2 * p + v], bank[(first + 2 * p + v) % RING][:], ACT.Identity,
                                                 scale=col_at("up_conv", k + 2 * KF), bias=col_at("up_conv", k + 6 * KF))\
                                .then_inc(act_for_dve, 1)
                        act.wait_ge(dve_for_act, n(dve_for_act))
                        nc.scalar.activation(tmp[:, 2 * p], tmp[:, 2 * p], ACT.Silu).then_inc(act_for_dve, 1)
                turns(KF // 2, RING, body, [(dve_for_act, 2)])
                at["bank"] += 2 * KF
                stay(3, sq_ffn if i == 0 else None)

            act.wait_ge(eps_ready, 1)
            squares(x, sq_ab, x_ready)
            load_root()
            for _ in range(AHEAD):
                split()
            for part in [ab, lambda: ffn(0), c, lambda: ffn(1), lambda: gated(0), lambda: conv_ffn(0),
                         lambda: gated(1), lambda: conv_ffn(1)]:
                part()
            for t in range(TT):
                b = 5 + 2 * t % 4
                act.wait_ge(out_turned, n(out_turned, 2))
                nc.scalar.activation(out_tok[:, t, 512:1024], bank[b][:], ACT.Copy).then_inc(bank_free[b], 1)
                act.drain().then_inc(out_copied, 1)

        @block.vector
        def _(dve):
            n = Count()
            at = {"split": 0, "bank": 0}

            def split():
                if at["split"] < N_SLABS:
                    s = at["split"] % RING
                    dve.wait_ge(hi_done, n(hi_done))
                    nc.vector.tensor_tensor(w_lo[:, s], w_raw[:, s], w_hi[:, s].bitcast(F32), ALU.subtract).then_inc(lo_done, 1)
                    at["split"] += 1

            def turns(times, slabs, body, extra=()):
                dry = at["split"] + times * slabs > N_SLABS
                k = times - dry
                if k > 1:
                    with n.loop(dve, k, [(slab_done, slabs), (hi_done, slabs)] + list(extra)) as i:
                        body(i)
                    at["split"] += (k - 1) * slabs
                elif k:
                    body(0)
                if dry:
                    body(times - 1)

            def step(ins):
                ins.then_inc(vector_step, 1)
                n(vector_step)

            def settle(s=vector_step):
                dve.wait_ge(s, n.now(s))

            def own(ins, s):
                ins.then_inc(s, 1)
                n(s)

            def flag(s):
                dve.drain().then_inc(s, 1)

            def tt(out, x0, x1, op):
                step(nc.vector.tensor_tensor(out, x0, x1, op))

            def ts(out, x0, s1, s2, op0, op1):
                if op1 is None:
                    step(nc.vector.tensor_scalar(out, x0, s1, None, op0))
                else:
                    step(nc.vector.tensor_scalar(out, x0, s1, s2, op0, op1))

            def stt(out, x0, sc, x1, op0, op1):
                step(nc.vector.scalar_tensor_tensor(out, x0, sc, x1, op0, op1))

            def inverse():
                dve.wait_ge(std_ready, n(std_ready))
                nc.vector.reciprocal(inv[:], dev[:]).then_inc(inv_ready, 1)
                flag(bank_free[4])
                dve.wait_ge(scale_ready, n(scale_ready))

            def parts_of_h(srcs, k0):
                for j, src in enumerate(srcs):
                    ts(h_hi[:, k0 + j], src, 1.0, None, ALU.mult, None)
                settle()
                for j, src in enumerate(srcs):
                    own(nc.vector.tensor_tensor(h_lo[:, k0 + j], src, h_hi[:, k0 + j].bitcast(F32), ALU.subtract), h_ready)
                settle(h_ready)

            def normal_h(src, gain, k0=0):
                inverse()
                for k in range(0, src.shape[1], 2):
                    ts_ = [tmp[:, (k + j) % 4] for j in range(2)]
                    for j in range(2):
                        stt(ts_[j], src[:, k + j], col(gain[0], gain[1] + k + j), bank[5][:], ALU.mult, ALU.mult)
                    settle()
                    parts_of_h(ts_, k0 + k)
                flag(bank_free[5])

            def normal_x(gain):
                def low(k):
                    dve.wait_ge(h_high, n(h_high))
                    own(nc.vector.tensor_tensor(h_lo[:, k], tmp[:, k % 4], h_hi[:, k].bitcast(F32), ALU.subtract), h_ready)

                inverse()
                for k in range(KD):
                    if k >= 4:
                        settle(h_ready)
                    own(nc.vector.scalar_tensor_tensor(tmp[:, k % 4], x[:, k], col(gain[0], gain[1] + k), bank[5][:],
                                                       ALU.mult, ALU.mult), h_scaled)
                    if k:
                        if k == 1:
                            settle(h_scaled)
                        low(k - 1)
                flag(bank_free[5])
                settle(h_scaled)
                low(KD - 1)
                settle(h_ready)

            def add_normal(y, gain):
                inverse()
                for k in range(0, KD, 2):
                    for j in range(2):
                        stt(tmp[:, (k + j) % 4], y[:, k + j], col("norm", gain + k + j), bank[5][:], ALU.mult, ALU.mult)
                    settle()
                    for j in range(2):
                        own(nc.vector.tensor_tensor(x[:, k + j], x[:, k + j], tmp[:, (k + j) % 4], ALU.add), x_ready)
                    if k:
                        settle(x_ready)
                flag(bank_free[5])

            def add_normal_h(y, gain, next_gain):
                def low(k0):
                    for k in (k0, k0 + 1):
                        dve.wait_ge(h_high, n(h_high))
                        own(nc.vector.scalar_tensor_tensor(h_lo[:, k], x[:, k], col("norm", next_gain + k), h_hi[:, k].bitcast(F32),
                                                           ALU.mult, ALU.subtract), h_ready)

                inverse()
                for k in range(0, KD, 2):
                    for j in range(2):
                        stt(tmp[:, (k + j) % 4], y[:, k + j], col("norm", gain + k + j), bank[5][:], ALU.mult, ALU.mult)
                    settle()
                    for j in range(2):
                        own(nc.vector.tensor_tensor(x[:, k + j], x[:, k + j], tmp[:, (k + j) % 4], ALU.add), x_ready)
                    if k:
                        low(k - 2)
                        settle(x_ready)
                flag(bank_free[5])
                low(KD - 2)
                settle(h_ready)

            def late_inverse():
                inverse()
                step(nc.vector.tensor_copy(inv_all, bank[5][:]))
                flag(bank_free[5])
                settle()

            def only_split(slabs):
                for _ in range(slabs):
                    split()
                    n(slab_done)

            def leave(slabs):
                def body(i):
                    only_split(RING * slabs)
                turns(2, RING * slabs, body)
                at["bank"] += KD

            def s5_prepare():
                v = [s5_v[:, i] for i in range(16)]
                are = par[:, ROWS["a_re"]:ROWS["a_re"] + GROUPS]
                aim = par[:, ROWS["a_im"]:ROWS["a_im"] + GROUPS]
                dve.wait_ge(prep["scalar_to_vector"], n(prep["scalar_to_vector"]))
                settle()
                tt(v[1], v[0], are, ALU.mult)
                tt(v[2], v[0], aim, ALU.mult)
                settle()
                ts(v[3], v[2], 1.0 / TWO_PI, ROUND, ALU.mult, ALU.add)
                settle()
                ts(v[3], v[3], -ROUND, None, ALU.add, None)
                settle()
                stt(v[4], v[3], -PI_HIGH, v[2], ALU.mult, ALU.add)
                settle()
                stt(v[4], v[3], -PI_MID, v[4], ALU.mult, ALU.add)
                settle()
                stt(v[4], v[3], -PI_LOW, v[4], ALU.mult, ALU.add)
                settle()
                ts(v[4], v[4], PI_IN, -PI_IN, ALU.min, ALU.max)
                settle()
                ts(v[5], v[4], TWO_PI / 4, None, ALU.add, None)
                settle()
                ts(v[6], v[5], PI_IN, -TWO_PI, ALU.is_gt, ALU.mult)
                settle()
                tt(v[5], v[5], v[6], ALU.add)
                settle()
                nc.vector.tensor_scalar(v[5], v[5], PI_IN, -PI_IN, ALU.min, ALU.max).then_inc(prep["vector_to_scalar"], 1)
                dve.wait_ge(early_in, 16)
                dve.wait_ge(prep["scalar_to_vector"], n(prep["scalar_to_vector"]))
                tt(v[10], v[7], v[9], ALU.mult)
                tt(v[11], v[7], v[8], ALU.mult)
                tt(v[12], are, are, ALU.mult)
                tt(v[13], aim, aim, ALU.mult)
                settle()
                tt(v[12], v[12], v[13], ALU.add)
                ts(v[14], v[10], -1.0, None, ALU.add, None)
                settle()
                step(nc.vector.reciprocal(v[12], v[12]))
                tt(v[15], v[14], are, ALU.mult)
                tt(v[6], v[11], aim, ALU.mult)
                tt(v[3], v[11], are, ALU.mult)
                tt(v[2], v[14], aim, ALU.mult)
                settle()
                tt(v[15], v[15], v[6], ALU.add)
                tt(v[3], v[3], v[2], ALU.subtract)
                settle()
                tt(v[15], v[15], v[12], ALU.mult)
                tt(v[3], v[3], v[12], ALU.mult)
                settle()
                ts(v[6], v[3], sign, None, ALU.mult, None)
                settle()

                only_split(1)

                def over(t):
                    return t.unsqueeze(2).to_broadcast([P, GROUPS, GW])

                t0 = tmp[:, 0].rearrange("p (g w) -> p g w", g=GROUPS)
                t1 = tmp[:, 1].rearrange("p (g w) -> p g w", g=GROUPS)
                tt(s5_bb[:, 0], over(v[15]), s5_b[:, 0], ALU.mult)
                tt(t0, over(v[6]), s5_b[:, 1], ALU.mult)
                tt(s5_bb[:, 1], over(v[15]), s5_b[:, 1], ALU.mult)
                tt(t1, over(v[6]), s5_b[:, 0], ALU.mult)
                settle()
                tt(s5_bb[:, 0], s5_bb[:, 0], t0, ALU.add)
                tt(s5_bb[:, 1], s5_bb[:, 1], t1, ALU.subtract)
                re, im = s5_pow[:, 0], s5_pow[:, 1]
                step(nc.vector.memset(re[:, 0], 1.0))
                step(nc.vector.memset(im[:, 0], 0.0))
                step(nc.vector.tensor_copy(re[:, 1], v[10]))
                step(nc.vector.tensor_copy(im[:, 1], v[11]))
                settle()
                for m_ in (1, 2, 4):
                    def last(t):
                        return t[:, m_:m_ + 1].to_broadcast([P, m_, GROUPS])

                    t2 = tmp[:, 2].rearrange("p (k g) -> p k g", g=GROUPS)[:, 0:m_]
                    t3 = tmp[:, 3].rearrange("p (k g) -> p k g", g=GROUPS)[:, 0:m_]
                    a_, b_ = slice(1, m_ + 1), slice(m_ + 1, 2 * m_ + 1)
                    tt(re[:, b_], re[:, a_], last(re), ALU.mult)
                    tt(t2, im[:, a_], last(im), ALU.mult)
                    tt(im[:, b_], re[:, a_], last(im), ALU.mult)
                    tt(t3, im[:, a_], last(re), ALU.mult)
                    settle()
                    tt(re[:, b_], re[:, b_], t2, ALU.subtract)
                    tt(im[:, b_], im[:, b_], t3, ALU.add)
                    settle()
                ims = tmp[:, 2, 0:STEP * GROUPS].rearrange("p (k g) -> p k g", g=GROUPS)
                ts(ims, im[:, 0:STEP], sign, None, ALU.mult, None)
                settle()

                def powers(t):
                    return t.rearrange("p k g -> p g k").unsqueeze(3).to_broadcast([P, part, STEP, GW])

                def weights(t):
                    return t.unsqueeze(2).to_broadcast([P, part, STEP, GW])

                part = GROUPS // 4
                quarters = [slice(part * i, part * i + part) for i in range(4)]
                only_split(1)
                for i, g in enumerate(quarters):
                    tt(s5_q[:, g], weights(s5_bb[:, 0, g]), powers(re[:, 0:STEP, g]), ALU.mult)
                    tt(s5_big[:], weights(s5_bb[:, 1, g]), powers(ims[:, :, g]), ALU.mult)
                    settle()
                    tt(s5_q[:, g], s5_q[:, g], s5_big[:], ALU.add)
                    if i % 2:
                        only_split(1)
                    settle()
                flag(prep["vector_to_pe"])
                for j in range(2):
                    dve.wait_ge(prep["pe_to_vector"], n(prep["pe_to_vector"]))
                    step(nc.vector.tensor_copy(s5_c[:, j], bank[6 + j][:].rearrange("p (g w) -> p g w", g=GROUPS)))
                    flag(bank_free[6 + j])
                settle()
                step(nc.vector.tensor_scalar(s5_cx[:], s5_c[:, 0], sign, -1.0, ALU.mult, ALU.mult))
                settle()
                flag(prep["vector_to_pe"])
                for i, g in enumerate(quarters):
                    tt(s5_out[:, g], weights(s5_cx[:, g]), powers(re[:, 1:STEP + 1, g]), ALU.mult)
                    tt(s5_big[:], weights(s5_c[:, 1, g]), powers(im[:, 1:STEP + 1, g]), ALU.mult)
                    settle()
                    tt(s5_out[:, g], s5_out[:, g], s5_big[:], ALU.subtract)
                    only_split(1)
                    settle()
                flag(prep["vector_to_scalar"])
                dve.wait_ge(prep["scalar_to_vector"], n(prep["scalar_to_vector"]))
                ec, es, t2, t3 = v[9], v[8], v[12], v[13]

                def square():
                    tt(t2, ec, ec, ALU.mult)
                    tt(t3, es, es, ALU.mult)
                    tt(es, ec, es, ALU.mult)
                    settle()
                    tt(ec, t2, t3, ALU.subtract)
                    ts(es, es, 2.0, None, ALU.mult, None)
                    settle()

                for _ in range(3):
                    square()
                step(nc.vector.memset(s5_cos[:, :, 0:1], 1.0))
                step(nc.vector.memset(s5_sin[:, :, 0:1], 0.0))
                settle()
                m_ = 1
                while m_ < CH:
                    def by(t):
                        return t.unsqueeze(2).to_broadcast([P, GROUPS, m_])

                    c0, s0, c1, s1 = (t[:, :, k] for t, k in ((s5_cos, slice(0, m_)), (s5_sin, slice(0, m_)),
                                                             (s5_cos, slice(m_, 2 * m_)), (s5_sin, slice(m_, 2 * m_))))
                    t0 = s5_t[:, :, 0:m_]
                    tt(c1, c0, by(ec), ALU.mult)
                    tt(t0, s0, by(es), ALU.mult)
                    tt(s1, c0, by(es), ALU.mult)
                    settle()
                    tt(c1, c1, t0, ALU.subtract)
                    settle()
                    tt(t0, s0, by(ec), ALU.mult)
                    settle()
                    tt(s1, s1, t0, ALU.add)
                    settle()
                    m_ *= 2
                    if m_ in (8, 32):
                        only_split(1)
                    if m_ < CH:
                        square()
                ts(s5_sin[:], s5_sin[:], sign, -1.0, ALU.mult, ALU.mult)
                settle()

            def convolve():
                for tiles in ((0, 1), (2, 3)):
                    for k in tiles:
                        ts(xc[:, k], xm[:, k], col("conv_w", 12 + k), col("conv_b", k), ALU.mult, ALU.add)
                    settle()
                    for j in (1, 2, 3):
                        for k in tiles:
                            stt(xc[:, k, j:SEQ], xm[:, k, 0:SEQ - j], col("conv_w", 4 * (3 - j) + k), xc[:, k, j:SEQ],
                                ALU.mult, ALU.add)
                        settle()
                    for k in tiles:
                        flag(lstm["vector_to_scalar"])

            def s5_core():
                def flat(t, i):
                    return t[:, 8 * i:8 * i + 8].rearrange("p g c -> p (g c)")

                def turn_and_sum(i):
                    dve.wait_ge(s5["pe_to_vector"], n(s5["pe_to_vector"]))
                    tt(flat(s5_w, i), bank[i][:], flat(s5_sin, i), ALU.mult)
                    tt(flat(s5_z, i), flat(s5_state, i), flat(s5_cos, i), ALU.mult)
                    settle()
                    flag(bank_free[i])
                    flag(bank_free[4 + i])
                    tt(flat(s5_w, i), flat(s5_w, i), flat(s5_z, i), ALU.add)
                    settle()
                    for g in range(8 * i, 8 * i + 8):
                        step(nc.vector.tensor_tensor_scan(s5_z[:, g], s5_r8[:, g:g + 1].to_broadcast([P, CH]), s5_w[:, g], 0.0,
                                                          ALU.mult, ALU.add))
                    flag(s5["vector_to_pe"])
                    settle()

                def turn_back(i):
                    dve.wait_ge(s5["pe_to_vector"], n(s5["pe_to_vector"]))
                    tt(flat(s5_w, i), bank[4 + i][:], flat(s5_sin, i), ALU.mult)
                    tt(flat(s5_state, i), flat(s5_z, i), flat(s5_cos, i), ALU.mult)
                    settle()
                    flag(bank_free[4 + i])
                    nc.vector.tensor_tensor(flat(s5_state, i), flat(s5_state, i), flat(s5_w, i), ALU.subtract)\
                        .then_inc(s5["vector_to_pe"], 1)

                for i in range(4):
                    turn_and_sum(i)
                for i in range(4):
                    turn_back(i)

            def lay_out():
                dve.wait_ge(lstm_in, 16 * 6)
                step(nc.vector.memset(gate_w[:], 0.0))
                settle()
                for v in range(2):
                    step(nc.vector.tensor_copy(gate_w[:, :, GATE_ROW * v:GATE_ROW * v + M_HEADS],
                                               lstm_wif[:, :, M_HEADS * v:M_HEADS * v + M_HEADS]))
                for v in range(3):
                    tt(lstm_bd[:, v].rearrange("p t (n e) -> p t n e", e=4),
                       lstm_w4[:, v].unsqueeze(2).to_broadcast([P, 4, 32, 4]),
                       quad.unsqueeze(1).unsqueeze(3).to_broadcast([P, 4, 32, 4]), ALU.mult)
                step(nc.vector.tensor_reduce(value_mean, lstm_w4[:, 2], AX.X, ALU.add))
                settle()
                ts(value_mean, value_mean, -1.0 / P, None, ALU.mult, None)
                settle()
                for k in range(4):
                    ts(lstm_bd[:, 3, k], lstm_bd[:, 2, k], value_mean[:, k:k + 1], None, ALU.add, None)
                flag(lstm["vector_to_pe"])

            def s5_gelu():
                dve.wait_ge(us_back, 16)
                dve.wait_ge(ys_loaded, 16)
                for k in range(4):
                    step(nc.vector.scalar_tensor_tensor(ys[:, k], us[:, k].rearrange("p i c -> p (i c)"), col("s5_d", k),
                                                        ys[:, k], ALU.mult, ALU.add))
                settle()
                flag(s5["vector_to_scalar"])
                dve.wait_ge(s5["scalar_to_vector"], n(s5["scalar_to_vector"]))
                parts_of_h([ys[:, k] for k in range(4)], 0)

            def s5_glu():
                for t in range(4):
                    split()
                    dve.wait_ge(slab_done, n(slab_done))
                    dve.wait_ge(s5["scalar_to_vector"], n(s5["scalar_to_vector"]))
                    tt(gated_ys[:, t].rearrange("p (c i) -> p i c", i=STEP), ys[:, t].rearrange("p (i c) -> p i c", i=STEP),
                       gate[:, t].rearrange("p (i c) -> p i c", i=STEP), ALU.mult)
                    flag(bank_free[at["bank"] % RING])
                    at["bank"] += 1
                settle()

            def lstm_gates():
                r = [rowv[:, j] for j in range(8)]
                dve.wait_ge(lstm["scalar_to_vector"], n(lstm["scalar_to_vector"]))
                stt(r[5], r[1], 0.0, r[4], ALU.min, ALU.subtract)
                settle()
                step(nc.vector.tensor_tensor_scan(r[6], ones[0:M_HEADS, 0:1].to_broadcast([M_HEADS, SEQ]), r[5], 0.0,
                                                  ALU.mult, ALU.add))
                settle()
                tt(r[7], r[0], r[6], ALU.subtract)
                settle()
                step(nc.vector.tensor_tensor_scan(r[2], r[7], r[7], 0.0, ALU.max, ALU.max))
                settle()
                ts(r[3], r[2], -1.0, None, ALU.mult, None)
                tt(r[4], r[6], r[2], ALU.add)
                settle()
                flag(lstm["vector_to_pe"])
                flag(lstm["vector_to_scalar"])

            def lstm_heads():
                for b, columns in ((6, g_col), (7, low_col)):
                    dve.wait_ge(lstm["pe_to_vector"], n(lstm["pe_to_vector"]))
                    step(nc.vector.tensor_copy(columns, bank[b][:, 0:16].rearrange("p (s h) -> p s h", s=TT)))
                    flag(bank_free[b])
                settle()

                def exponents(h):
                    dve.wait_ge(top_in, n(top_in))
                    flag(bank_free[4])
                    for t in range(TT):
                        own(nc.vector.tensor_scalar(lstm_t[:, t, t * P:SEQ], neg_top[:, t * P:SEQ], g_col[:, t, h:h + 1], 0.0,
                                                    ALU.add, ALU.min), expo_ready)

                def weigh(h):
                    for t in range(TT):
                        dve.wait_ge(scored, n(scored))
                        dve.wait_ge(weight_ready, n(weight_ready))
                        tt(sc_m[:, t, t * P:SEQ], bank[6 + t % 2][:, 0:SEQ - t * P], lstm_t[:, t, t * P:SEQ], ALU.mult)
                        settle()
                        flag(bank_free[6 + t % 2])
                        own(nc.vector.tensor_tensor(sc_m[:, t, t * P:(t + 1) * P], sc_m[:, t, t * P:(t + 1) * P], causal, ALU.mult),
                            weighed)
                    settle(weighed)

                def denominators(h):
                    den = bank[5][:, 0:TT]
                    dve.wait_ge(lstm["pe_to_vector"], n(lstm["pe_to_vector"]))
                    stt(den_col, den, -1.0, low_col[:, :, h], ALU.mult, ALU.max)
                    settle()
                    tt(den_col, den, den_col, ALU.max)
                    flag(bank_free[5])
                    settle()
                    step(nc.vector.reciprocal(den_col, den_col))
                    settle()

                def scale(h):
                    dve.wait_ge(lstm["pe_to_vector"], n(lstm["pe_to_vector"]))
                    stt(var_col, bank[4][:, 0:TT], 1.0 / P, den_col, ALU.mult, ALU.mult)
                    flag(bank_free[4])
                    settle()
                    tt(var_col, var_col, den_col, ALU.mult)
                    flag(lstm["vector_to_scalar"])
                    dve.wait_ge(lstm["scalar_to_vector"], n(lstm["scalar_to_vector"]))
                    step(nc.vector.reciprocal(scale_col, dev_col))
                    settle()
                    own(nc.vector.tensor_tensor(scale_col, scale_col, den_col, ALU.mult), head_scaled)
                    settle(head_scaled)

                exponents(0)
                parts_of_h([gated_ys[:, t] for t in range(4)], 4)
                weigh(0)
                denominators(0)
                for h in range(M_HEADS):
                    if h + 1 < M_HEADS:
                        exponents(h + 1)
                        weigh(h + 1)
                    scale(h)
                    if h + 1 < M_HEADS:
                        denominators(h + 1)
                    dve.wait_ge(lstm["pe_to_vector"], n(lstm["pe_to_vector"]))
                    tt(lstm_v[:, 2], lstm_v[:, h % 2], bank[5][:], ALU.mult)
                    flag(bank_free[5])
                    settle()
                    stt(lstm_v[:, 3], xc[:, h], col("skip", h), lstm_v[:, 2], ALU.mult, ALU.add)
                    settle()
                    tt(lstm_v[:, 3], lstm_v[:, 3], zs[:, h], ALU.mult)
                    settle()
                    parts_of_h([lstm_v[:, 3]], h)

            def lower_bounds():
                e, w = small[:, 0:16], small[:, 16:32]
                r0, r1 = (par[:, ROWS["lb_raw"] + 8 * j:ROWS["lb_raw"] + 8 * j + 8] for j in range(2))
                tt(w[:, 0:8], r0, r1, ALU.max)
                settle()
                tt(e[:, 0:8], r0, w[:, 0:8], ALU.subtract)
                tt(e[:, 8:16], r1, w[:, 0:8], ALU.subtract)
                settle()
                flag(hgrn["vector_to_scalar"])
                dve.wait_ge(hgrn["scalar_to_vector"], n(hgrn["scalar_to_vector"]))
                tt(w[:, 0:8], e[:, 0:8], e[:, 8:16], ALU.add)
                settle()
                step(nc.vector.reciprocal(w[:, 8:16], w[:, 0:8]))
                settle()
                tt(e[:, 0:8], e[:, 0:8], w[:, 8:16], ALU.mult)
                tt(e[:, 8:16], e[:, 8:16], w[:, 8:16], ALU.mult)
                settle()
                tt(w[:, 0:8], e[:, 0:8], e[:, 8:16], ALU.add)
                settle()
                tt(lb[:, 0], w[:, 0:8], e[:, 0:8], ALU.subtract)
                settle()
                ts(lb[:, 1], lb[:, 0], -1.0, 1.0, ALU.mult, ALU.add)
                ts(lb[:, 2], lb[:, 0], 1.0, None, ALU.subtract, None)
                settle()

            def turned_rows():
                for b in range(ROW_BLOCKS):
                    dve.wait_ge(par_turned, n(par_turned))
                    first, r = GAINS if b == 0 else 0, block_rows(b)
                    step(nc.vector.tensor_copy(par[:, b * P + first:b * P + r], bank[4 + b % 4][:, first:r]))
                    settle()
                    flag(bank_free[4 + b % 4])
                flag(par_ready)

            def ab():
                normal_x(("norm", 0))
                turned_rows()
                s5_prepare()
                only_split(2)
                lower_bounds()
                at["bank"] += 12
                s5_core()
                lay_out()
                convolve()
                s5_gelu()
                lstm_gates()
                s5_glu()
                lstm_heads()
                leave(1)
                add_normal_h(y_mix, 8, 16)

            def ffn(i):
                late_inverse()
                first = at["bank"]

                def body(j):
                    for p in range(2):
                        g, u = (first + 2 * p) % RING, (first + 2 * p + 1) % RING
                        only_split(1)
                        dve.wait_ge(slab_done, n.now(slab_done))
                        tt(tmp[:, p], bank[g][:], inv_all, ALU.mult)
                        flag(bank_free[g])
                        flag(dve_for_act)
                        only_split(1)
                        dve.wait_ge(slab_done, n.now(slab_done))
                        tt(tmp[:, 2 + p], bank[u][:], inv_all, ALU.mult)
                        flag(bank_free[u])
                        settle()
                        dve.wait_ge(act_for_dve, n(act_for_dve))
                        tt(tmp[:, 2 + p], tmp[:, 2 + p], tmp[:, p], ALU.mult)
                        k = bass.ds(j * 2 + p, 1)
                        settle()
                        ts(hid_hi[:, k], tmp[:, 2 + p:3 + p], 1.0, None, ALU.mult, None)
                        settle()
                        own(nc.vector.tensor_tensor(hid_lo[:, k], tmp[:, 2 + p:3 + p], hid_hi[:, k].bitcast(F32), ALU.subtract),
                            hid_ready)
                        settle(hid_ready)
                turns(KF // 2, RING, body, [(act_for_dve, 2), (vector_step, 8), (hid_ready, 2)])
                at["bank"] += 2 * KF
                leave(3)
                add_normal(y_ffn, 32 * i + 24)

            def c():
                normal_x(("norm", 32))
                chunk = 8
                decay = small[:, 32:40]
                first = at["bank"]
                bank_of = [bank[(first + t) % RING] for t in range(RING)]
                free = [bank_free[(first + t) % RING] for t in range(RING)]
                b3, d3, e3 = (t[:].rearrange("p (c t) -> p c t", c=chunk) for t in (c_b, c_d, c_e))

                def turn(gemm, mixer):
                    if gemm is not None:
                        k = bass.ds(gemm, 1)
                        low, kept, less = lb[:, 0, k], lb[:, 1, k], lb[:, 2, k]
                        only_split(1)
                        dve.wait_ge(hgrn["scalar_to_vector"], n(hgrn["scalar_to_vector"]))
                        tt(c_q[:], bank_of[0][:], c_sig[:, 0], ALU.mult)
                        flag(free[0])
                        only_split(1)
                    if mixer is not None:
                        dve.wait_ge(hgrn["pe_to_vector"], n(hgrn["pe_to_vector"]))
                        ts(c_s[:], bank[6][:].rearrange("p (t w) -> p t w", t=TT), HUGE, -HUGE, ALU.min, ALU.max)
                        flag(bank_free[6])
                        settle()
                        tt(c_s[:], c_s[:], causal_c.unsqueeze(1).to_broadcast([P, TT, P]), ALU.mult)
                        flag(hgrn["vector_to_pe"])
                    if mixer is not None:
                        dve.wait_ge(hgrn["pe_to_vector"], n(hgrn["pe_to_vector"]))
                        step(nc.vector.tensor_copy(c_state[:, 1], bank[7][:, 0:P]))
                        for j in range(1, 7):
                            settle()
                            stt(c_state[:, j + 1], c_state[:, j], decay[:, j:j + 1],
                                bank[4 if j % 2 else 7][:, (j // 2) * P:(j // 2 + 1) * P], ALU.mult, ALU.add)
                        flag(bank_free[7])
                        flag(bank_free[4])
                        flag(hgrn["vector_to_pe"])
                    if gemm is not None:
                        dve.wait_ge(hgrn["scalar_to_vector"], n(hgrn["scalar_to_vector"]))
                        ts(c_k[:].unsqueeze(1), c_sig[:, 1:2], less, kept, ALU.mult, ALU.add)
                        nc.vector.tensor_scalar(c_f[:].unsqueeze(1), c_sig[:, 1:2], kept, low, ALU.mult, ALU.add)\
                            .then_inc(hgrn["vector_to_scalar"], 1)
                        flag(free[1])
                        only_split(1)
                        dve.wait_ge(hgrn["scalar_to_vector"], n(hgrn["scalar_to_vector"]))
                        tt(gc[:, k], bank_of[2][:].unsqueeze(1), c_sig[:, 2:3], ALU.mult)
                        flag(free[2])
                        dve.wait_ge(hgrn["scalar_to_vector"], n(hgrn["scalar_to_vector"]))
                        step(nc.vector.tensor_tensor_scan(c_b[:], restart, c_f[:], 0.0, ALU.mult, ALU.add))
                        settle()
                        nc.vector.tensor_tensor(d3, b3, b3[:, :, C_CHUNK - 1:C_CHUNK].to_broadcast([P, chunk, C_CHUNK]), ALU.subtract)\
                            .then_inc(hgrn["vector_to_scalar"], 1)
                        dve.wait_ge(hgrn["scalar_to_vector"], n(hgrn["scalar_to_vector"]))
                        step(nc.vector.tensor_copy(decay, e3[:, :, C_CHUNK - 1]))
                        settle()
                        tt(c_e[:], c_q[:], c_e[:], ALU.mult)
                        tt(c_d[:], c_q[:], tmp[:, 0], ALU.mult)
                        tt(c_k[:], c_k[:], tmp[:, 1], ALU.mult)
                        flag(hgrn["vector_to_pe"])
                        only_split(1)
                    if mixer is not None:
                        k = bass.ds(mixer, 1)
                        dve.wait_ge(hgrn["scalar_to_vector"], n(hgrn["scalar_to_vector"]))
                        tt(tmp[:, 2], bank[5][:], tmp[:, 2], ALU.mult)
                        flag(bank_free[6])
                        flag(bank_free[5])
                        settle()
                        stt(tmp[:, 3:4], tmp[:, 2:3], col_at("c_gain", mixer), gc[:, k], ALU.mult, ALU.mult)
                        settle()
                        ts(mix_hi[:, k], tmp[:, 3:4], 1.0, None, ALU.mult, None)
                        settle()
                        own(nc.vector.tensor_tensor(mix_lo[:, k], tmp[:, 3:4], mix_hi[:, k].bitcast(F32), ALU.subtract), h_ready)
                        settle(h_ready)

                turn(0, None)
                per = [(slab_done, RING), (hi_done, RING), (hgrn["scalar_to_vector"], 6), (hgrn["pe_to_vector"], 2),
                       (vector_step, 20), (h_ready, 1)]
                with n.loop(dve, C_HEADS - 1, per) as i:
                    turn(i + 1, i)
                at["split"] += RING * (C_HEADS - 2)
                turn(None, C_HEADS - 1)
                at["bank"] += RING * C_HEADS
                leave(1)
                add_normal_h(y_mix, 40, 48)

            def gated(i):
                normal_x(("attn_norm", 8 * i))
                for v, half in enumerate((slice(HEAD, P), slice(0, HEAD), slice(HEAD, P), slice(0, HEAD))):
                    step(nc.vector.memset(k_pad[half, v], 0.0))
                only_split(6)
                dve.wait_ge(qk_rooted, n(qk_rooted))
                own(nc.vector.reciprocal(head_dev, head_dev), qk_inverted)
                flag(bank_free[4])
                settle(qk_inverted)
                ts(head_scale, head_dev, HEAD ** -0.5, None, ALU.mult, None)
                only_split(1)
                dve.wait_ge(late_in, 16 * 10 * (i + 1))
                for place_, (j, b) in enumerate(PARTNERS):
                    a_ = tmp[:, place_ % 4]
                    dve.wait_ge(qk_partner, n(qk_partner))
                    tt(a_, bank[b][:], sin, ALU.mult)
                    tt(qa[:, j], qa[:, j], cos, ALU.mult)
                    settle()
                    flag(bank_free[b])
                    tt(qa[:, j], qa[:, j], a_, ALU.add)
                    if j == 1:
                        settle()
                        only_split(1)
                        dve.wait_ge(qk_spread, n(qk_spread))
                        own(nc.vector.tensor_tensor(qa[:, 4], qa[:, 4], bank[4][:], ALU.mult), k_turned)
                        flag(bank_free[4])
                        settle(k_turned)
                        step(nc.vector.tensor_copy(k_pad[0:HEAD, 0], qa[0:HEAD, 4]))
                        step(nc.vector.tensor_copy(k_pad[HEAD:P, 3], qa[HEAD:P, 4]))
                    if j == 2:
                        only_split(1)
                only_split(1)
                dve.wait_ge(k_swapped, n(k_swapped))
                step(nc.vector.tensor_copy(k_pad[0:HEAD, 2], bank[4][0:HEAD]))
                step(nc.vector.tensor_copy(k_pad[HEAD:P, 1], bank[4][HEAD:P]))
                flag(bank_free[4])
                flag(q_turned)
                only_split(1)
                dve.wait_ge(vv_copied, n(vv_copied))
                for t in range(TT):
                    step(nc.vector.tensor_reduce(gate_dev[:, 8 * t:8 * t + 8], prob_t[0][:, t].rearrange("p (h d) -> p h d", h=8),
                                                 AX.X, ALU.add))
                flag(vv_summed)
                only_split(2)
                dve.wait_ge(vv_rooted, n(vv_rooted))
                settle()
                step(nc.vector.reciprocal(gate_dev, gate_dev))
                settle()
                for t in range(TT):
                    tt(vv_tok[:, t].rearrange("p (h d) -> p h d", h=8), vv_tok[:, t].rearrange("p (h d) -> p h d", h=8),
                       gate_dev[:, 8 * t:8 * t + 8].unsqueeze(2).to_broadcast([P, 8, HEAD]), ALU.mult)
                flag(vv_normal)
                only_split(1)

                def maxima(u):
                    c = u % 4
                    dve.wait_ge(score_ready, n(score_ready))
                    step(nc.vector.tensor_reduce(top_score[:, c:c + 1], bank[2 + u % 3][:], AX.X, ALU.max))
                    settle()
                    k = 2 * (5 * (u % TT) + u // TT // 2) + u // TT % 2
                    own(nc.vector.tensor_scalar(shift[:, c:c + 1], top_score[:, c:c + 1], -1.0, head_scale[:, k:k + 1],
                                                ALU.mult, ALU.mult), max_ready)

                maxima(0)
                maxima(1)
                for u in range(UNITS):
                    c = u % 4
                    dve.wait_ge(exp_ready, n(exp_ready))
                    step(nc.vector.reciprocal(share[:, c:c + 1], total[:, c:c + 1]))
                    flag(bank_free[2 + u % 3])
                    settle()
                    own(nc.vector.tensor_scalar(prob[:, c], prob[:, c], share[:, c:c + 1], None, ALU.mult), prob_ready)
                    if u + 2 < UNITS:
                        maxima(u + 2)
                    if u - 1 in MIX_AT:
                        j = MIX_AT.index(u - 1)
                        dve.wait_ge(gate_mixed, n(gate_mixed))
                        stt(mixed[:].rearrange("p (c w) -> p c w", c=TT), bank[5][:].rearrange("p (c w) -> p c w", c=TT),
                            col("sg_norm", 4 * i + j), sgb[:, j].unsqueeze(1).to_broadcast([P, TT, P]), ALU.mult, ALU.add)
                        settle()
                        flag(bank_free[5])
                        own(nc.vector.tensor_tensor(ua[:, j], ua[:, j], mixed[:], ALU.mult), gated_ready)
                settle(prob_ready)
                at["bank"] += len(IN_ORDER)
                normal_h(ua, ("sg_gain", 4 * i), 4)
                normal_h(oa, ("attn_gain", 4 * i), 0)
                add_result(1)

            def add_result(slabs):
                first = at["bank"]

                def body(i):
                    for t in range(RING):
                        only_split(slabs - 1)
                        b = (first + t) % RING
                        dve.wait_ge(slab_done, n(slab_done))
                        k = bass.ds(i * RING + t, 1)
                        own(nc.vector.tensor_tensor(x[:, k], x[:, k], bank[b][:].unsqueeze(1), ALU.add), x_ready)
                        flag(bank_free[b])
                        split()
                turns(2, RING * slabs, body, [(x_ready, RING)])
                at["bank"] += KD

            def conv_ffn(i):
                normal_x(("ffn_norm", 8 * i))
                first = at["bank"]
                base = i * 8 * KF

                def body(j):
                    for p in range(2):
                        only_split(2)
                        for v in range(2):
                            b = (first + 2 * p + v) % RING
                            k = j * 2 + (p + v * KF + base)
                            c_ = tmp[:, 2 * p + v]
                            dve.wait_ge(act_for_dve, n(act_for_dve))
                            stt(c_[:, 1:SEQ], bank[b][:, 0:SEQ - 1], col_at("up_conv", k), c_[:, 1:SEQ], ALU.mult, ALU.add)
                            settle()
                            ins = nc.vector.scalar_tensor_tensor(c_[:, 0:SEQ - 1], bank[b][:, 1:SEQ],
                                                                 col_at("up_conv", k + 4 * KF), c_[:, 0:SEQ - 1], ALU.mult, ALU.add)
                            if v == 0:
                                ins.then_inc(dve_for_act, 1)
                            else:
                                step(ins)
                        flag(bank_free[(first + 2 * p) % RING])
                        flag(bank_free[(first + 2 * p + 1) % RING])
                        settle()
                        dve.wait_ge(act_for_dve, n(act_for_dve))
                        kk = bass.ds(j * 2 + p, 1)
                        tt(tmp[:, 2 * p + 1], tmp[:, 2 * p], tmp[:, 2 * p + 1], ALU.mult)
                        settle()
                        ts(hid_hi[:, kk], tmp[:, 2 * p + 1:2 * p + 2], 1.0, None, ALU.mult, None)
                        settle()
                        own(nc.vector.tensor_tensor(hid_lo[:, kk], tmp[:, 2 * p + 1:2 * p + 2], hid_hi[:, kk].bitcast(F32),
                                                    ALU.subtract), hid_ready)
                        settle(hid_ready)
                turns(KF // 2, RING, body, [(act_for_dve, 6), (vector_step, 10), (hid_ready, 2)])
                at["bank"] += 2 * KF
                add_result(3)

            nc.vector.memset(eps[:], EPS).then_inc(eps_ready, 1)
            for b in range(8):
                flag(bank_free[b])
            for k in range(KD):
                dve.wait_ge(x_turned, n(x_turned))
                step(nc.vector.tensor_copy(x[:, k], bank[k % RING][:]))
                settle()
                flag(bank_free[k % RING])
                own(dve.drain(), x_ready)
            at["bank"] += KD
            dve.wait_ge(gains_turned, 1)
            step(nc.vector.tensor_copy(par[:, 0:GAINS], bank[7][:, 0:GAINS]))
            settle()
            flag(bank_free[7])
            for _ in range(AHEAD):
                split()
            for part in [ab, lambda: ffn(0), c, lambda: ffn(1), lambda: gated(0), lambda: conv_ffn(0),
                         lambda: gated(1), lambda: conv_ffn(1)]:
                part()
            for t in range(TT):
                b = 4 + 2 * t % 4
                dve.wait_ge(out_turned, n(out_turned, 2) - 1)
                own(nc.vector.tensor_copy(out_tok[:, t, 0:512], bank[b][:]), out_ready)
                flag(bank_free[b])


_NAMES = ["x", "norm_g", "ab_w_in", "ab_conv_w", "ab_conv_b", "ab_wq", "ab_wk", "ab_wv", "ab_w_if", "ab_b_if", "ab_mh_gain",
          "ab_skip", "ab_a_re", "ab_a_im", "ab_log_dt", "ab_b_re", "ab_b_im", "ab_c_re", "ab_c_im", "ab_d", "ab_w_glu",
          "ab_b_glu", "ab_w_out", "c_w_in", "c_lb_raw", "c_g_gain", "c_w_out", "ffn_w1", "ffn_w3", "ffn_w2",
          "attn_norm_g_2", "w_in_2", "q_norm_g_2", "k_norm_g_2", "sg_norm_g_2", "sg_w_2", "sg_b_2", "attn_out_g_2",
          "sg_out_g_2", "w_o_2", "ffn_norm_g_2", "w_up_2", "conv_w_2", "conv_b_2", "w_down_2"]


def kernel(**inputs):
    import concourse.bacc as bacc
    from concourse.bass_utils import run_bass_kernel_spmd

    nc = bacc.Bacc("TRN2", target_bir_lowering=False, num_devices=1)
    arrays = {f"in_{k}": np.ascontiguousarray(inputs[k]) for k in _NAMES}
    arrays.update({f"in_{k}": v for k, v in constants().items()})
    aps = {k[3:]: nc.dram_tensor(k, v.shape, F32, kind="ExternalInput").ap() for k, v in arrays.items()}
    aps["out"] = nc.dram_tensor("out_x", (1, SEQ, D), F32, kind="ExternalOutput").ap()
    program(nc, aps)
    r = run_bass_kernel_spmd(nc, [arrays], core_ids=[0])
    return r.results[0]["out_x"]
```
